# Optimizing a Trainium2 kernel written in Bass

```python
import jax
import jax.numpy as jnp
from jax import lax
import numpy as np
import jax, jax.numpy as jnp

D_MODEL = 1024
BATCH = 1
SEQ = 256
DEPTH = 2

D_MIX = 2 * D_MODEL
SSD_WIDTH = D_MIX // 2
SSD_HEAD_DIM = 64
SSD_HEADS = SSD_WIDTH // SSD_HEAD_DIM
SSD_GROUPS = 2
SSD_STATE = 64
SSD_CONV = 4
SSD_CHUNK = 128
D_XBC = SSD_WIDTH + 2 * SSD_GROUPS * SSD_STATE
D_SSD_IN = SSD_WIDTH + D_XBC + SSD_HEADS
MLSTM_WIDTH = D_MIX // 4
MLSTM_HEAD_DIM = 128
MLSTM_HEADS = MLSTM_WIDTH // MLSTM_HEAD_DIM
MLSTM_CONV = 4
MLSTM_CHUNK = 128
D_MLSTM_IN = 2 * MLSTM_WIDTH + 2 * MLSTM_HEADS
RWKV_WIDTH = D_MIX // 4
RWKV_HEAD_DIM = 64
RWKV_HEADS = RWKV_WIDTH // RWKV_HEAD_DIM
RWKV_DECAY_RANK = 64
RWKV_AAA_RANK = 64
RWKV_GATE_RANK = 128
D_RWKV_IN = 3 * RWKV_WIDTH + RWKV_DECAY_RANK + RWKV_AAA_RANK + RWKV_GATE_RANK
D_IN = D_SSD_IN + D_MLSTM_IN + D_RWKV_IN
D_FF = 2816
FFN_HALF = 0.5
EPS = 1e-6
RWKV_GN_EPS = 64e-5


def rms_norm(x, g):
    xf = x.astype(jnp.float32)
    xf = xf * lax.rsqrt(jnp.mean(xf * xf, axis=-1, keepdims=True) + EPS)
    return (xf * g).astype(x.dtype)

def group_rms_norm(y, g, n_groups):
    b, t, w = y.shape
    yf = y.astype(jnp.float32).reshape(b, t, n_groups, w // n_groups)
    yf = yf * lax.rsqrt(jnp.mean(yf * yf, axis=-1, keepdims=True) + EPS)
    return yf.reshape(b, t, w) * g

def swiglu(x, w_gate_up, w_down):
    gate, up = jnp.split(x @ w_gate_up, 2, axis=-1)
    return (jax.nn.silu(gate) * up) @ w_down

def causal_depthwise_conv(x, w, b):
    k = w.shape[0]
    y = lax.conv_general_dilated(x, w[:, None, :].astype(x.dtype), window_strides=(1,),
                                 padding=[(k - 1, 0)], dimension_numbers=('NWC', 'WIO', 'NWC'),
                                 feature_group_count=x.shape[-1])
    return y + b

def causal_mask(n):
    return jnp.tril(jnp.ones((n, n), dtype=bool))

def ssd_mixer(u, conv_w, conv_b, dt_bias, a_log, d_skip, norm_g):
    bsz, t, _ = u.shape
    nc, L, G, J, P, N = t // SSD_CHUNK, SSD_CHUNK, SSD_GROUPS, SSD_HEADS // SSD_GROUPS, SSD_HEAD_DIM, SSD_STATE
    z, xbc, dt_raw = jnp.split(u, [SSD_WIDTH, SSD_WIDTH + D_XBC], axis=-1)
    xbc = jax.nn.silu(causal_depthwise_conv(xbc, conv_w, conv_b).astype(jnp.float32))
    xs, b_in, c_in = jnp.split(xbc, [SSD_WIDTH, SSD_WIDTH + G * N], axis=-1)
    dt = jax.nn.softplus((dt_raw + dt_bias).astype(jnp.float32)).reshape(bsz, nc, L, G, J)
    a = dt * (-jnp.exp(a_log.astype(jnp.float32))).reshape(G, J)
    a_cum = jnp.cumsum(a, axis=2)
    X = xs.reshape(bsz, nc, L, G, J, P)
    Bc = b_in.reshape(bsz, nc, L, G, N)
    Cc = c_in.reshape(bsz, nc, L, G, N)
    x_dt = X * dt[..., None]
    seg = a_cum[:, :, :, None] - a_cum[:, :, None, :]
    decay_ls = jnp.exp(jnp.where(causal_mask(L)[:, :, None, None], seg, -jnp.inf))
    cb = jnp.einsum('bclgn,bcsgn->bclsg', Cc, Bc)
    y_diag = jnp.einsum('bclsgj,bcsgjp->bclgjp', cb[..., None] * decay_ls, x_dt)
    decay_to_end = jnp.exp(a_cum[:, :, -1:] - a_cum)
    states = jnp.einsum('bcsgn,bcsgjp->bcgjpn', Bc, x_dt * decay_to_end[..., None])
    chunk_decay = jnp.exp(a_cum[:, :, -1])

    def step(s, inp):
        st, dec = inp
        return s * dec[..., None, None] + st, s

    _, s_prev = lax.scan(step, jnp.zeros_like(states[:, 0]),
                         (jnp.moveaxis(states, 1, 0), jnp.moveaxis(chunk_decay, 1, 0)))
    s_prev = jnp.moveaxis(s_prev, 0, 1)
    y_off = jnp.einsum('bclgn,bcgjpn->bclgjp', Cc, s_prev) * jnp.exp(a_cum)[..., None]
    y = y_diag + y_off + X * d_skip.astype(jnp.float32).reshape(G, J, 1)
    y = y.reshape(bsz, t, SSD_WIDTH) * jax.nn.silu(z.astype(jnp.float32))
    return group_rms_norm(y, norm_g, G).astype(u.dtype)

def mlstm_mixer(u, conv_w, conv_b, wq, wk, wv, gate_bias, norm_g):
    bsz, t, _ = u.shape
    H, Dh, L = MLSTM_HEADS, MLSTM_HEAD_DIM, MLSTM_CHUNK
    nc = t // L
    xm, o_pre, if_pre = jnp.split(u, [MLSTM_WIDTH, 2 * MLSTM_WIDTH], axis=-1)
    xc = jax.nn.silu(causal_depthwise_conv(xm, conv_w, conv_b).astype(jnp.float32))
    xc_h = xc.reshape(bsz, t, H, Dh)
    xm_h = xm.astype(jnp.float32).reshape(bsz, t, H, Dh)
    q = jnp.einsum('bthd,hde->bthe', xc_h, wq)
    k = jnp.einsum('bthd,hde->bthe', xc_h, wk) * (Dh ** -0.5)
    v = jnp.einsum('bthd,hde->bthe', xm_h, wv)
    gates = (if_pre + gate_bias).astype(jnp.float32)
    log_i = gates[..., :H].reshape(bsz, nc, L, H)
    log_f = jax.nn.log_sigmoid(gates[..., H:]).reshape(bsz, nc, L, H)
    o = jax.nn.sigmoid(o_pre.astype(jnp.float32)).reshape(bsz, t, H, Dh)
    qc = q.reshape(bsz, nc, L, H, Dh)
    kc = k.reshape(bsz, nc, L, H, Dh)
    vc = v.reshape(bsz, nc, L, H, Dh)
    bcum = jnp.cumsum(log_f, axis=2)
    d_log = bcum[:, :, :, None] - bcum[:, :, None, :] + log_i[:, :, None, :]
    d_log = jnp.where(causal_mask(L)[:, :, None], d_log, -jnp.inf)
    m_intra = jnp.max(d_log, axis=3)
    end_log = bcum[:, :, -1:] - bcum + log_i
    m_loc = jnp.max(end_log, axis=2)
    w_end = jnp.exp(end_log - m_loc[:, :, None])
    c_loc = jnp.einsum('bcshd,bcshe->bchde', vc * w_end[..., None], kc)
    n_loc = jnp.einsum('bcsh,bcshe->bche', w_end, kc)
    b_end = bcum[:, :, -1]

    def step(carry, inp):
        c_st, n_st, m_st = carry
        cl, nl, ml, be = inp
        m_new = jnp.maximum(be + m_st, ml)
        s_old = jnp.exp(be + m_st - m_new)
        s_new = jnp.exp(ml - m_new)
        c_new = c_st * s_old[..., None, None] + cl * s_new[..., None, None]
        n_new = n_st * s_old[..., None] + nl * s_new[..., None]
        return (c_new, n_new, m_new), (c_st, n_st, m_st)

    init = (jnp.zeros((bsz, H, Dh, Dh), jnp.float32), jnp.zeros((bsz, H, Dh), jnp.float32),
            jnp.zeros((bsz, H), jnp.float32))
    _, (c_prev, n_prev, m_prev) = lax.scan(
        step, init, (jnp.moveaxis(c_loc, 1, 0), jnp.moveaxis(n_loc, 1, 0),
                     jnp.moveaxis(m_loc, 1, 0), jnp.moveaxis(b_end, 1, 0)))
    c_prev = jnp.moveaxis(c_prev, 0, 1)
    n_prev = jnp.moveaxis(n_prev, 0, 1)
    m_prev = jnp.moveaxis(m_prev, 0, 1)
    inter_log = bcum + m_prev[:, :, None]
    m_t = jnp.maximum(inter_log, m_intra)
    w_intra = jnp.exp(d_log - m_t[:, :, :, None])
    w_inter = jnp.exp(inter_log - m_t)
    qk = jnp.einsum('bclhe,bcshe->bclsh', qc, kc) * w_intra
    num = (jnp.einsum('bclsh,bcshd->bclhd', qk, vc)
           + jnp.einsum('bclhe,bchde->bclhd', qc, c_prev) * w_inter[..., None])
    den = jnp.sum(qk, axis=3) + jnp.einsum('bclhe,bche->bclh', qc, n_prev) * w_inter
    h = num / jnp.maximum(jnp.abs(den), jnp.exp(-m_t))[..., None]
    h = h.reshape(bsz, t, H, Dh) * o
    return group_rms_norm(h.reshape(bsz, t, MLSTM_WIDTH), norm_g, H).astype(u.dtype)

def rwkv7_mixer(u, shift_mu, w0, w_up, a0, a_up, g_up, k_k, k_a, r_k, ln_w, ln_b):
    bsz, t, _ = u.shape
    H, N, W = RWKV_HEADS, RWKV_HEAD_DIM, RWKV_WIDTH
    uf = u.astype(jnp.float32)
    u_prev = jnp.pad(uf, ((0, 0), (1, 0), (0, 0)))[:, :-1]
    us = uf + (u_prev - uf) * shift_mu
    r, k, v, wl, al, gl = jnp.split(
        us, [W, 2 * W, 3 * W, 3 * W + RWKV_DECAY_RANK, 3 * W + RWKV_DECAY_RANK + RWKV_AAA_RANK], axis=-1)
    w_log = -jax.nn.softplus(-(w0 + jnp.tanh(wl) @ w_up)) - 0.5
    decay = jnp.exp(-jnp.exp(w_log))
    a = jax.nn.sigmoid(a0 + al @ a_up)
    g = jax.nn.sigmoid(gl) @ g_up
    kk = (k * k_k).reshape(bsz, t, H, N)
    kk = kk / jnp.maximum(jnp.sqrt(jnp.sum(kk * kk, axis=-1, keepdims=True)), 1e-6)
    k = k * (1.0 + (a - 1.0) * k_a)
    rh, kh, vh = (z.reshape(bsz, t, H, N) for z in (r, k, v))
    dh, ah = decay.reshape(bsz, t, H, N), a.reshape(bsz, t, H, N)

    def tm(z):
        return jnp.moveaxis(z, 1, 0)

    def step(s, inp):
        r_t, w_t, k_t, v_t, kk_t, a_t = inp
        sa = jnp.einsum('bhvk,bhk->bhv', s, -kk_t)
        s = (s * w_t[:, :, None, :] + sa[..., None] * (kk_t * a_t)[:, :, None, :]
             + v_t[..., None] * k_t[:, :, None, :])
        return s, jnp.einsum('bhvk,bhk->bhv', s, r_t)

    _, y = lax.scan(step, jnp.zeros((bsz, H, N, N), jnp.float32),
                    (tm(rh), tm(dh), tm(kh), tm(vh), tm(kk), tm(ah)))
    y = jnp.moveaxis(y, 0, 1)
    mu = jnp.mean(y, axis=-1, keepdims=True)
    var = jnp.mean(jnp.square(y - mu), axis=-1, keepdims=True)
    y = (y - mu) * lax.rsqrt(var + RWKV_GN_EPS) * ln_w.reshape(H, N) + ln_b.reshape(H, N)
    y = y + jnp.sum(rh * kh * r_k, axis=-1, keepdims=True) * vh
    return (y.reshape(bsz, t, W) * g).astype(u.dtype)

def first_inputs(seed: int = 0) -> dict:
    key = jax.random.key(seed)
    keys = iter(jax.random.split(key, 48))
    L, D = DEPTH, D_MODEL

    def nrm(shape, scale):
        return scale * jax.random.normal(next(keys), shape, jnp.float32)

    def unif(shape, lo, hi):
        return jax.random.uniform(next(keys), shape, jnp.float32, lo, hi)

    dt_init = jnp.exp(unif((L, SSD_HEADS), float(np.log(1e-3)), float(np.log(1e-1))))
    return {
        'x': nrm((BATCH, SEQ, D), 1.0),
        'ffn1_norm': 1.0 + nrm((L, D), 0.02),
        'ffn1_w_gate_up': nrm((L, D, 2 * D_FF), D ** -0.5),
        'ffn1_w_down': nrm((L, D_FF, D), D_FF ** -0.5),
        'mix_norm': 1.0 + nrm((L, D), 0.02),
        'w_in': nrm((L, D, D_IN), D ** -0.5),
        'ssd_conv_w': nrm((L, SSD_CONV, D_XBC), SSD_CONV ** -0.5),
        'ssd_conv_b': nrm((L, D_XBC), 0.02),
        'ssd_dt_bias': dt_init + jnp.log(-jnp.expm1(-dt_init)),
        'ssd_a_log': jnp.log(unif((L, SSD_HEADS), 1.0, 16.0)),
        'ssd_d': 1.0 + nrm((L, SSD_HEADS), 0.02),
        'ssd_norm': 1.0 + nrm((L, SSD_WIDTH), 0.02),
        'mlstm_conv_w': nrm((L, MLSTM_CONV, MLSTM_WIDTH), MLSTM_CONV ** -0.5),
        'mlstm_conv_b': nrm((L, MLSTM_WIDTH), 0.02),
        'mlstm_wq': nrm((L, MLSTM_HEADS, MLSTM_HEAD_DIM, MLSTM_HEAD_DIM), MLSTM_HEAD_DIM ** -0.5),
        'mlstm_wk': nrm((L, MLSTM_HEADS, MLSTM_HEAD_DIM, MLSTM_HEAD_DIM), MLSTM_HEAD_DIM ** -0.5),
        'mlstm_wv': nrm((L, MLSTM_HEADS, MLSTM_HEAD_DIM, MLSTM_HEAD_DIM), MLSTM_HEAD_DIM ** -0.5),
        'mlstm_gate_bias': jnp.concatenate(
            [nrm((L, MLSTM_HEADS), 0.1),
             jnp.linspace(3.0, 6.0, MLSTM_HEADS, dtype=jnp.float32) + nrm((L, MLSTM_HEADS), 0.1)], axis=-1),
        'mlstm_norm': 1.0 + nrm((L, MLSTM_WIDTH), 0.02),
        'rwkv_shift_mu': unif((L, D_RWKV_IN), 0.0, 1.0),
        'rwkv_w0': jnp.linspace(-6.0, -1.0, RWKV_WIDTH, dtype=jnp.float32) + nrm((L, RWKV_WIDTH), 0.1),
        'rwkv_w_up': nrm((L, RWKV_DECAY_RANK, RWKV_WIDTH), 0.5 * RWKV_DECAY_RANK ** -0.5),
        'rwkv_a0': nrm((L, RWKV_WIDTH), 0.1),
        'rwkv_a_up': nrm((L, RWKV_AAA_RANK, RWKV_WIDTH), 0.5 * RWKV_AAA_RANK ** -0.5),
        'rwkv_g_up': nrm((L, RWKV_GATE_RANK, RWKV_WIDTH), RWKV_GATE_RANK ** -0.5),
        'rwkv_k_k': 0.85 + nrm((L, RWKV_WIDTH), 0.02),
        'rwkv_k_a': 1.0 + nrm((L, RWKV_WIDTH), 0.02),
        'rwkv_r_k': nrm((L, RWKV_HEADS, RWKV_HEAD_DIM), 0.1),
        'rwkv_ln_w': 1.0 + nrm((L, RWKV_WIDTH), 0.02),
        'rwkv_ln_b': nrm((L, RWKV_WIDTH), 0.02),
        'w_out': nrm((L, D_MIX, D), D_MIX ** -0.5),
        'ffn2_norm': 1.0 + nrm((L, D), 0.02),
        'ffn2_w_gate_up': nrm((L, D, 2 * D_FF), D ** -0.5),
        'ffn2_w_down': nrm((L, D_FF, D), D_FF ** -0.5),
        'final_norm': 1.0 + nrm((D,), 0.02),
    }

def first_block(x, ffn1_norm, ffn1_w_gate_up, ffn1_w_down, mix_norm, w_in,
              ssd_conv_w, ssd_conv_b, ssd_dt_bias, ssd_a_log, ssd_d, ssd_norm,
              mlstm_conv_w, mlstm_conv_b, mlstm_wq, mlstm_wk, mlstm_wv, mlstm_gate_bias, mlstm_norm,
              rwkv_shift_mu, rwkv_w0, rwkv_w_up, rwkv_a0, rwkv_a_up, rwkv_g_up, rwkv_k_k, rwkv_k_a,
              rwkv_r_k, rwkv_ln_w, rwkv_ln_b, w_out, ffn2_norm, ffn2_w_gate_up, ffn2_w_down, final_norm):
    for l in range(DEPTH):
        x = x + FFN_HALF * swiglu(rms_norm(x, ffn1_norm[l]), ffn1_w_gate_up[l], ffn1_w_down[l])
        u = rms_norm(x, mix_norm[l]) @ w_in[l]
        u_ssd, u_ml, u_rw = jnp.split(u, [D_SSD_IN, D_SSD_IN + D_MLSTM_IN], axis=-1)
        y_ssd = ssd_mixer(u_ssd, ssd_conv_w[l], ssd_conv_b[l], ssd_dt_bias[l], ssd_a_log[l],
                          ssd_d[l], ssd_norm[l])
        y_ml = mlstm_mixer(u_ml, mlstm_conv_w[l], mlstm_conv_b[l], mlstm_wq[l], mlstm_wk[l],
                           mlstm_wv[l], mlstm_gate_bias[l], mlstm_norm[l])
        y_rw = rwkv7_mixer(u_rw, rwkv_shift_mu[l], rwkv_w0[l], rwkv_w_up[l], rwkv_a0[l], rwkv_a_up[l],
                           rwkv_g_up[l], rwkv_k_k[l], rwkv_k_a[l], rwkv_r_k[l], rwkv_ln_w[l], rwkv_ln_b[l])
        y = jnp.concatenate([y_ssd, y_ml, y_rw], axis=-1)
        x = x + y @ w_out[l]
        x = x + FFN_HALF * swiglu(rms_norm(x, ffn2_norm[l]), ffn2_w_gate_up[l], ffn2_w_down[l])
    return rms_norm(x, final_norm)


_first_inputs = first_inputs


def first_inputs(seed=0):
    import zlib

    import numpy as np

    out = dict(_first_inputs(seed))
    spreads = {}
    factors = {'ffn1_norm': 3.249,
     'ssd_conv_b': 2.884,
     'ssd_d': 14.041,
     'ssd_norm': 12.098,
     'mlstm_norm': 17.012,
     'rwkv_w_up': 5.266,
     'rwkv_a0': 4.457,
     'rwkv_k_k': 61.103,
     'rwkv_k_a': 25.352,
     'rwkv_ln_w': 37.297,
     'rwkv_ln_b': 33.159,
     'ffn2_norm': 5.824,
     'final_norm': 8.644}
    for name, (base, spread) in spreads.items():
        noise = np.random.default_rng([zlib.crc32(name.encode()), seed]).standard_normal(out[name].shape)
        drawn = base * np.exp(spread * noise) if base else spread * noise
        out[name] = jnp.asarray(drawn.astype(out[name].dtype))
    for name, factor in factors.items():
        out[name] = (out[name] * factor).astype(out[name].dtype)
    return out


_narrow_inputs = first_inputs


def first_inputs(seed=0):
    out = dict(_narrow_inputs(seed))
    wider = {'ssd_a_log': 3.67,
     'ssd_d': 3.21,
     'ssd_norm': 3.23,
     'mlstm_norm': 3.22,
     'rwkv_k_k': 5.14,
     'rwkv_ln_w': 3.18,
     'final_norm': 3.31}
    for name, times in wider.items():
        mean = out[name].mean()
        out[name] = (mean + times * (out[name] - mean)).astype(out[name].dtype)
    return out


CTX_LEN = 256
GRID_W = 64
N_MIXERS = 2
FFN_DIM = 2816
N_FOURIER_GROUPS = 4
FOURIER_GROUP_DIM = D_MODEL // N_FOURIER_GROUPS
RET_HEADS = 4
RET_QK_DIM = D_MODEL // RET_HEADS
RET_V_DIM = 2 * D_MODEL // RET_HEADS
RET_QK_TOTAL = RET_HEADS * RET_QK_DIM
RET_V_TOTAL = RET_HEADS * RET_V_DIM
RET_IN_DIM = 2 * RET_QK_TOTAL + 2 * RET_V_TOTAL
RET_CHUNK = 128
ROPE_BASE = 10000.0
N_MOD = 9
NORM_EPS = 1e-6
N_FOURIER_LAYERS = (DEPTH + N_MIXERS - 1) // N_MIXERS
N_RET_LAYERS = DEPTH // N_MIXERS


def rmsnorm(x, g):
    xf = x.astype(jnp.float32)
    y = xf * lax.rsqrt(jnp.mean(xf * xf, axis=-1, keepdims=True) + NORM_EPS)
    return (y * g.astype(jnp.float32)).astype(x.dtype)

def modulate(h, shift, scale):
    return h * (1 + scale) + shift

def swiglu_2(h, w_gate, w_up, w_down):
    return (jax.nn.silu(h @ w_gate) * (h @ w_up)) @ w_down

def fourier_mix(h):
    b, n, d = h.shape
    hg = h.reshape(b, n, N_FOURIER_GROUPS, FOURIER_GROUP_DIM).astype(jnp.float32)
    f = jnp.fft.fft2(hg, axes=(1, 3), norm="ortho").real
    return f.reshape(b, n, d).astype(h.dtype)

def fourier_layer(h_lat, h_ctx, w, bias):
    y_lat = fourier_mix(h_lat) @ w + bias
    y_ctx = None if h_ctx is None else fourier_mix(h_ctx) @ w + bias
    return y_lat, y_ctx

def axial_rope(n_tokens):
    rows = n_tokens // GRID_W
    row = jnp.repeat(jnp.arange(rows, dtype=jnp.float32), GRID_W)
    col = jnp.tile(jnp.arange(GRID_W, dtype=jnp.float32), rows)
    n_freq = RET_QK_DIM // 4
    inv_freq = ROPE_BASE ** (-jnp.arange(n_freq, dtype=jnp.float32) / n_freq)
    ang = jnp.concatenate([row[:, None] * inv_freq, col[:, None] * inv_freq], axis=-1)
    return jnp.cos(ang), jnp.sin(ang)

def apply_rope(t, cos, sin):
    t1, t2 = jnp.split(t, 2, axis=-1)
    cos = cos.astype(t.dtype)
    sin = sin.astype(t.dtype)
    return jnp.concatenate([t1 * cos - t2 * sin, t2 * cos + t1 * sin], axis=-1)

def ret_project(h, w_in):
    b, n, _ = h.shape
    p = h @ w_in
    q, k, v, g = jnp.split(p, [RET_QK_TOTAL, 2 * RET_QK_TOTAL, 2 * RET_QK_TOTAL + RET_V_TOTAL], axis=-1)
    q = q.reshape(b, n, RET_HEADS, RET_QK_DIM).transpose(0, 2, 1, 3)
    k = k.reshape(b, n, RET_HEADS, RET_QK_DIM).transpose(0, 2, 1, 3) * (RET_QK_DIM ** -0.5)
    v = v.reshape(b, n, RET_HEADS, RET_V_DIM).transpose(0, 2, 1, 3)
    return q, k, v, g

def retention_scan(q, k, v, lg, s0):
    b, h, n, dk = q.shape
    dv = v.shape[-1]
    nc = n // RET_CHUNK
    dt = q.dtype
    pos = jnp.arange(RET_CHUNK, dtype=jnp.float32)
    diff = pos[:, None] - pos[None, :]
    intra = jnp.where(diff >= 0, jnp.exp(lg[:, None, None] * jnp.maximum(diff, 0.0)), 0.0).astype(dt)
    q_dec = jnp.exp(lg[:, None] * (pos + 1.0))[:, :, None].astype(dt)
    k_dec = jnp.exp(lg[:, None] * (RET_CHUNK - 1.0 - pos))[:, :, None].astype(dt)
    chunk_dec = jnp.exp(lg * RET_CHUNK)[:, None, None].astype(dt)

    def to_chunks(t):
        return jnp.moveaxis(t.reshape(b, h, nc, RET_CHUNK, t.shape[-1]), 2, 0)

    def step(s, qkv):
        qc, kc, vc = qkv
        scores = jnp.einsum('bhid,bhjd->bhij', qc, kc) * intra
        y = (jnp.einsum('bhij,bhje->bhie', scores, vc)
             + jnp.einsum('bhid,bhde->bhie', qc * q_dec, s))
        s = chunk_dec * s + jnp.einsum('bhjd,bhje->bhde', kc * k_dec, vc)
        return s, y

    s_final, y = lax.scan(step, s0, (to_chunks(q), to_chunks(k), to_chunks(v)))
    y = jnp.moveaxis(y, 0, 2).reshape(b, h, n, dv)
    return y, s_final

def bidirectional_retention(q, k, v, lg_fwd, lg_bwd, s_fwd, s_bwd):
    y_f, s_f = retention_scan(q, k, v, lg_fwd, s_fwd)
    y_b_rev, s_b = retention_scan(jnp.flip(q, 2), jnp.flip(k, 2), jnp.flip(v, 2), lg_bwd, s_bwd)
    return y_f + jnp.flip(y_b_rev, 2), s_f, s_b

def ret_output(y, g, w_out):
    b, h, n, dv = y.shape
    yf = y.astype(jnp.float32)
    mu = jnp.mean(yf, axis=-1, keepdims=True)
    var = jnp.mean(jnp.square(yf - mu), axis=-1, keepdims=True)
    yn = ((yf - mu) * lax.rsqrt(var + NORM_EPS)).astype(g.dtype)
    yn = yn.transpose(0, 2, 1, 3).reshape(b, n, h * dv)
    return (jax.nn.silu(g) * yn) @ w_out

def retention_layer(h_lat, h_ctx, w_in, w_out, decay, cos, sin, need_ctx_out):
    lg = -jnp.abs(decay.astype(jnp.float32))
    qc, kc, vc, gc = ret_project(h_ctx, w_in)
    zeros = jnp.zeros((h_ctx.shape[0], RET_HEADS, RET_QK_DIM, RET_V_DIM), vc.dtype)
    yc, s_f, s_b = bidirectional_retention(qc, kc, vc, lg[0], lg[1], zeros, zeros)
    ql, kl, vl, gl = ret_project(h_lat, w_in)
    ql = apply_rope(ql, cos, sin)
    kl = apply_rope(kl, cos, sin)
    yl, _, _ = bidirectional_retention(ql, kl, vl, lg[0], lg[1], s_f, s_b)
    y_lat = ret_output(yl, gl, w_out)
    y_ctx = ret_output(yc, gc, w_out) if need_ctx_out else None
    return y_lat, y_ctx

def second_inputs(seed: int = 0) -> dict:
    key = jax.random.key(seed)
    ks = jax.random.split(key, 16)
    f32 = jnp.float32
    base_rate = -np.log(1.0 - 2.0 ** (-5.0 - np.arange(RET_HEADS, dtype=np.float32)))
    base_rate = jnp.asarray(base_rate, dtype=f32)
    return {
        "x": jax.random.normal(ks[0], (BATCH, SEQ, D_MODEL), f32),
        "c": jax.random.normal(ks[1], (BATCH, D_MODEL), f32),
        "ctx": jax.random.normal(ks[2], (BATCH, CTX_LEN, D_MODEL), f32),
        "c_ctx": jax.random.normal(ks[3], (D_MODEL,), f32),
        "ada_w": jax.random.normal(ks[4], (DEPTH, D_MODEL, N_MOD * D_MODEL), f32) * (0.5 * D_MODEL ** -0.5),
        "ada_b": jax.random.normal(ks[5], (DEPTH, N_MOD * D_MODEL), f32) * 0.01,
        "norm_g": 1.0 + 0.02 * jax.random.normal(ks[6], (DEPTH, 3, D_MODEL), f32),
        "final_g": 1.0 + 0.02 * jax.random.normal(ks[7], (D_MODEL,), f32),
        "ffn_w_gate": jax.random.normal(ks[8], (DEPTH, 2, D_MODEL, FFN_DIM), f32) * D_MODEL ** -0.5,
        "ffn_w_up": jax.random.normal(ks[9], (DEPTH, 2, D_MODEL, FFN_DIM), f32) * D_MODEL ** -0.5,
        "ffn_w_down": jax.random.normal(ks[10], (DEPTH, 2, FFN_DIM, D_MODEL), f32) * FFN_DIM ** -0.5,
        "four_w": jax.random.normal(ks[11], (N_FOURIER_LAYERS, D_MODEL, D_MODEL), f32) * D_MODEL ** -0.5,
        "four_b": jax.random.normal(ks[12], (N_FOURIER_LAYERS, D_MODEL), f32) * 0.01,
        "ret_w_in": jax.random.normal(ks[13], (N_RET_LAYERS, D_MODEL, RET_IN_DIM), f32) * D_MODEL ** -0.5,
        "ret_w_out": jax.random.normal(ks[14], (N_RET_LAYERS, RET_V_TOTAL, D_MODEL), f32) * RET_V_TOTAL ** -0.5,
        "ret_decay": base_rate * (1.0 + 0.05 * jax.random.normal(ks[15], (N_RET_LAYERS, 2, RET_HEADS), f32)),
    }

def second_block(x, c, ctx, c_ctx, ada_w, ada_b, norm_g, final_g, ffn_w_gate, ffn_w_up, ffn_w_down,
              four_w, four_b, ret_w_in, ret_w_out, ret_decay):
    cos, sin = axial_rope(x.shape[1])
    silu_c = jax.nn.silu(c)
    silu_cc = jax.nn.silu(c_ctx)
    for l in range(DEPTH):
        last = l == DEPTH - 1
        mixer = l % N_MIXERS
        slot = l // N_MIXERS
        ctx_read = (not last) or (mixer == 1)
        m_lat = jnp.split((silu_c @ ada_w[l] + ada_b[l])[:, None, :], N_MOD, axis=-1)
        m_ctx = jnp.split(silu_cc @ ada_w[l] + ada_b[l], N_MOD, axis=-1)

        def half_ffn(t, m, j):
            h = modulate(rmsnorm(t, norm_g[l, j]), m[3 * j], m[3 * j + 1])
            return t + 0.5 * m[3 * j + 2] * swiglu_2(h, ffn_w_gate[l, j // 2], ffn_w_up[l, j // 2],
                                                  ffn_w_down[l, j // 2])

        x = half_ffn(x, m_lat, 0)
        if ctx_read:
            ctx = half_ffn(ctx, m_ctx, 0)

        h_lat = modulate(rmsnorm(x, norm_g[l, 1]), m_lat[3], m_lat[4])
        h_ctx = modulate(rmsnorm(ctx, norm_g[l, 1]), m_ctx[3], m_ctx[4]) if ctx_read else None
        if mixer == 0:
            y_lat, y_ctx = fourier_layer(h_lat, h_ctx, four_w[slot], four_b[slot])
        else:
            y_lat, y_ctx = retention_layer(h_lat, h_ctx, ret_w_in[slot], ret_w_out[slot], ret_decay[slot],
                                           cos, sin, not last)
        x = x + m_lat[5] * y_lat
        if not last:
            ctx = ctx + m_ctx[5] * y_ctx

        x = half_ffn(x, m_lat, 2)
        if not last:
            ctx = half_ffn(ctx, m_ctx, 2)
    return rmsnorm(x, final_g)


def setup_inputs(seed=0):
    out = dict(first_inputs(seed))
    for name, value in second_inputs(seed + 1).items():
        if name != "x":
            out[name + "_2"] = value
    return out


def reference(
    x, ffn1_norm, ffn1_w_gate_up, ffn1_w_down, mix_norm, w_in, ssd_conv_w, ssd_conv_b,
    ssd_dt_bias, ssd_a_log, ssd_d, ssd_norm, mlstm_conv_w, mlstm_conv_b, mlstm_wq, mlstm_wk,
    mlstm_wv, mlstm_gate_bias, mlstm_norm, rwkv_shift_mu, rwkv_w0, rwkv_w_up, rwkv_a0,
    rwkv_a_up, rwkv_g_up, rwkv_k_k, rwkv_k_a, rwkv_r_k, rwkv_ln_w, rwkv_ln_b, w_out, ffn2_norm,
    ffn2_w_gate_up, ffn2_w_down, final_norm, c_2, ctx_2, c_ctx_2, ada_w_2, ada_b_2, norm_g_2,
    final_g_2, ffn_w_gate_2, ffn_w_up_2, ffn_w_down_2, four_w_2, four_b_2, ret_w_in_2,
    ret_w_out_2, ret_decay_2,
):
    x = first_block(
        x, ffn1_norm, ffn1_w_gate_up, ffn1_w_down, mix_norm, w_in, ssd_conv_w, ssd_conv_b,
        ssd_dt_bias, ssd_a_log, ssd_d, ssd_norm, mlstm_conv_w, mlstm_conv_b, mlstm_wq, mlstm_wk,
        mlstm_wv, mlstm_gate_bias, mlstm_norm, rwkv_shift_mu, rwkv_w0, rwkv_w_up, rwkv_a0,
        rwkv_a_up, rwkv_g_up, rwkv_k_k, rwkv_k_a, rwkv_r_k, rwkv_ln_w, rwkv_ln_b, w_out,
        ffn2_norm, ffn2_w_gate_up, ffn2_w_down, final_norm,
    )
    return second_block(
        x, c_2, ctx_2, c_ctx_2, ada_w_2, ada_b_2, norm_g_2, final_g_2, ffn_w_gate_2, ffn_w_up_2,
        ffn_w_down_2, four_w_2, four_b_2, ret_w_in_2, ret_w_out_2, ret_decay_2,
    )


_drawn_inputs = setup_inputs


def setup_inputs(seed=0):
    import zlib

    import numpy as np

    out = dict(_drawn_inputs(seed))
    spreads = {}
    factors = {'ctx_2': 7.327,
     'c_ctx_2': 6.366,
     'ada_b_2': 8.0,
     'norm_g_2': 8.0,
     'final_g_2': 7.871,
     'four_b_2': 64.0,
     'ret_decay_2': 7.111}
    for name, (base, spread) in spreads.items():
        noise = np.random.default_rng([zlib.crc32(name.encode()), seed]).standard_normal(out[name].shape)
        drawn = base * np.exp(spread * noise) if base else spread * noise
        out[name] = jnp.asarray(drawn.astype(out[name].dtype))
    for name, factor in factors.items():
        out[name] = (out[name] * factor).astype(out[name].dtype)
    return out
```

```python
from contextlib import ExitStack

import numpy as np

import concourse.bass as bass
from concourse import mybir

F32 = mybir.dt.float32
ALU = mybir.AluOpType
ACT = mybir.ActivationFunctionType
AX = mybir.AxisListType.X
P = 128
NSLOT = 4
SLOT = 4096
ARENA = 27600
DECAY = float(np.exp(-0.5))

COLS1 = [("n1", 8), ("nm", 8), ("n2", 8), ("cw", 56), ("cb", 14), ("sn", 8), ("mn", 4), ("mu", 14),
         ("w0", 4), ("a0", 4), ("kk", 4), ("ka", 4), ("rk", 4), ("lw", 4), ("lb", 4)]
NCOL1 = sum(n for _, n in COLS1)
NCOLS = 2 * NCOL1 + 2 * 24 + 2 * 72 + 16
MASKS = ["ident", "tri", "ones", "negT", "neg", "bones", "l2", "l2t", "l4", "l8", "l16", "l32", "l64", "i2"]


class Queue:

    def __init__(self, name, sem, chained):
        self.name, self.sem, self.chained = name, sem, chained
        self.items, self.n, self.seen, self.pending = [], 0, {}, []

    def wait(self, *tokens):
        for t in tokens:
            if t is None:
                continue
            if isinstance(t, list):
                self.wait(*t)
                continue
            sem, n, key = t
            if n > self.seen.get(key, 0):
                self.seen[key] = n
                self.items.append((sem, n))

    def __call__(self, fn, *after, mark=True):
        if self.pending:
            self.wait(*self.pending)
            self.pending = []
        self.wait(*after)
        if self.chained and self.n:
            self.wait((self.sem, self.n, self.name))
        if mark:
            self.n += 1
        self.items.append((fn, mark))
        return (self.sem, self.n, self.name) if mark else None

    def last(self):
        return (self.sem, self.n, self.name) if self.n else None

    def emit(self, eng):
        for a, b in self.items:
            if callable(a):
                ins = a(eng)
                if b is True:
                    ins.then_inc(self.sem, 1)
                elif b:
                    ins.then_inc(b, 16)
            else:
                eng.wait_ge(a, b)


class Bank:
    def __init__(self, t, i):
        self.t, self.i, self.free, self.busy = t, i, None, False

    def done(self, token):
        self.free, self.busy = token, False


class Banks:
    def __init__(self, tensors):
        self.banks = [Bank(t, i) for i, t in enumerate(tensors)]
        self.at = 0

    def get(self):
        b = self.banks[self.at % len(self.banks)]
        self.at += 1
        assert not b.busy
        b.busy = True
        return b


class Ring:

    def __init__(self, tensor, sems, sp):
        self.t, self.sems, self.sp = tensor, sems, sp
        self.at, self.count, self.owner = 0, [0] * NSLOT, [None] * NSLOT

    def load(self, src, width):
        i = self.at % NSLOT
        self.at += 1
        assert self.owner[i] != "busy"
        dst = self.t[:, i, 0:width]
        if len(src.shape) == 3:
            dst = dst.rearrange("p (c n) -> p c n", n=src.shape[2])
        self.sp.wait(self.owner[i])
        sem = self.sems[i]
        self.sp.items.append((lambda e: e.dma_start(dst, src, max_dma_last_dim=16384), sem))
        self.owner[i] = "busy"
        self.count[i] += 16
        return self.t[:, i, 0:width], (sem, self.count[i], f"ring{i}"), i

    def free(self, i, token):
        self.owner[i] = token


def build(nc, A, out):
    with ExitStack() as ctx:
        sbt = lambda name, shape: ctx.enter_context(nc.sbuf_tensor(name, shape, F32))
        sem = lambda name: ctx.enter_context(nc.semaphore(name))

        ring_t = sbt("ring", [P, NSLOT, SLOT])
        xt = sbt("xt", [P, 2, 1024])
        msk = sbt("msk", [P, len(MASKS), 128])
        mask4 = sbt("mask4", [P, 4, 128])
        scanm = sbt("scanm", [P, 256])
        cols = sbt("cols", [P, NCOLS])
        rows = sbt("rows", [P, 120])
        smallw = sbt("smallw", [P, 2560])
        mods = sbt("mods", [P, 2, 72, 2])
        sil = sbt("sil", [P, 8, 2])
        st = sbt("st", [P, 512])
        arena = sbt("arena", [P, ARENA])
        psums = [ctx.enter_context(nc.psum_tensor(f"ps{i}", [P, 512], F32)) for i in range(8)]

        pe = Queue("pe", sem("s_pe"), False)
        ac = Queue("ac", sem("s_ac"), True)
        dv = Queue("dv", sem("s_dv"), True)
        po = Queue("po", sem("s_po"), True)
        sp = Queue("sp", sem("s_sp"), False)
        ring = Ring(ring_t, [sem(f"s_ring{i}") for i in range(NSLOT)], sp)
        banks = Banks(psums)

        ident, tri, ones, negT, neg, bones, l2, l2t = (msk[:, i, :] for i in range(8))
        lvl = [msk[:, 8 + i, :] for i in range(5)]
        i2 = msk[:, 13, 0:64]
        onesrow = msk[0:1, 2, :]

        def mm(o, l, r, *after, start=True, stop=True, mark=False):
            return pe(lambda e: e.matmul(o, l, r, start=start, stop=stop, skip_group_check=True), *after, mark=mark)

        def tr(o, i, *after, mark=False):
            return pe(lambda e: e.transpose(o, i, ident), *after, mark=mark)

        def act(o, i, f, *after, **kw):
            return ac(lambda e: e.activation(o, i, f, **kw), *after)

        def tt(q, o, a, b, op, *after):
            return q(lambda e: e.tensor_tensor(o, a, b, op), *after)

        def ts(q, o, a, s1, s2, op0, op1, *after):
            if s2 is None:
                return q(lambda e: e.tensor_scalar(o, a, s1, None, op0), *after)
            return q(lambda e: e.tensor_scalar(o, a, s1, s2, op0, op1), *after)

        def stt(o, a, s, b, op0, op1, *after):
            return dv(lambda e: e.scalar_tensor_tensor(out=o, in0=a, scalar=s, in1=b, op0=op0, op1=op1), *after)

        def cp(q, o, a, *after):
            if q is ac:
                return act(o, a, ACT.Copy, *after)
            return q(lambda e: e.tensor_copy(o, a), *after)

        def red(o, a, op, *after):
            return dv(lambda e: e.tensor_reduce(o, a, AX, op), *after)

        def rcp(o, a, *after):
            return dv(lambda e: e.reciprocal(o, a), *after)

        def zero(o):
            return dv(lambda e: e.memset(o, 0.0))

        small = {}

        def load(name, dst, src, *after):
            s, n, _ = small.get(name) or (sem("s_" + name), 0, None)
            ac.wait(*ac.pending, *after)
            ac.pending = []
            ac.wait(ac.last())
            ac.items.append((lambda e: e.dma_start(dst, src), s))
            small[name] = (s, n + 16, "load_" + name)

        def barrier(*more):
            toks = [q.last() for q in (pe, ac, dv, po)] + list(more)
            for q in (pe, ac, dv, po):
                q.pending += [t for t in toks if t and t[2] != q.name]

        top = [0]

        def area(n):
            a = arena[:, top[0]:top[0] + n]
            top[0] += n
            assert top[0] <= ARENA, top[0]
            return a

        def area3(n, m):
            return area(n * m).rearrange("p (a b) -> p a b", b=m)

        def area4(n, m, k):
            return area(n * m * k).rearrange("p (a b c) -> p a b c", b=m, c=k)

        def col(l, name, i=0, n=1):
            at = l * NCOL1
            for nm, w in COLS1:
                if nm == name:
                    break
                at += w
            return cols[:, at + i:at + i + n]

        C2 = 2 * NCOL1
        ng2 = cols[:, C2:C2 + 48].rearrange("p (l j c) -> p l j c", l=2, j=3)
        ab2 = cols[:, C2 + 48:C2 + 192].rearrange("p (l c) -> p l c", l=2)
        cc2 = cols[:, C2 + 192:C2 + 208].rearrange("p (c v) -> p c v", v=2)

        load("const", msk[:, :, :], A["c_msk"])
        load("const", cols[:, :], A["c_cols"])
        load("const", rows[:, :], A["c_rows"].broadcast_to([P, 120]))
        load("x", xt[:, :, :], A["x"].rearrange("o (t p) d -> p (o t) d", p=P))
        load("const", mask4[:, :, :], A["c_mask4"])
        load("const", scanm[:, :], A["c_scan"])
        cst = dv(lambda e: e.memset(st[:, 500:501], -0.5))
        barrier(small["const"], small["x"])

        act(sil[:, :, :], cc2, ACT.Silu)
        units = [(l, t) for l in range(2) for t in range(18)]

        def fill(n):
            for _ in range(min(n, len(units))):
                l, t = units.pop(0)
                w, ready, slot = ring.load(A["ada_w_2"][l, t], 4096)
                w = w.rearrange("p (k n) -> p k n", k=8)
                b = banks.get()
                for i in range(4):
                    for k in range(8):
                        tk = mm(b.t[:, 2 * i:2 * i + 2], w[:, k, i * 128:(i + 1) * 128], sil[:, k, :], ready, b.free,
                                ac_sil, start=k == 0, stop=k == 7, mark=(i == 3 and k == 7))
                ring.free(slot, tk)
                bias = ab2[:, l, 4 * t:4 * t + 4].unsqueeze(2).broadcast_to([P, 4, 2])
                b.done(tt(dv, mods[:, l, 4 * t:4 * t + 4, :],
                          b.t[:, 0:8].rearrange("p (a b) -> p a b", b=2), bias, ALU.add, tk))
        ac_sil = ac.last()

        def power(o, v, n):
            return po(lambda e: e.tensor_tensor(o, v, st[:, 500:501].broadcast_to([P, n]), ALU.pow))

        def rstd(tiles, o, n, width, eps, junk, *after):
            for i, a in enumerate(tiles):
                t = ac(lambda e, a=a, i=i: e.activation(junk[:, 0:width], a, ACT.Square,
                                                       accum_out=o[:, i:i + 1]), *after)
            ts(po, o[:, 0:n], o[:, 0:n], 1.0 / width, eps, ALU.mult, ALU.add, t)
            return power(o[:, 0:n], o[:, 0:n], n)

        def norm_t(tiles, hT, scale, bias, xs, junk):
            n = len(tiles)
            r = rstd(tiles, st[:, 0:n], n, 1024, 1e-6, junk)
            done = [ts(dv, xs[:, i, :], tiles[i], st[:, i:i + 1], None, ALU.mult, None, r) for i in range(n)]
            jobs = [(c, s) for c in range(8) for s in range(n // 2)]
            for j in range(0, len(jobs), 2):
                b = banks.get()
                for m, (c, s) in enumerate(jobs[j:j + 2]):
                    for t in range(2):
                        o = (2 * m + t) * 128
                        tk = tr(b.t[:, o:o + 128], xs[:, 2 * s + t, c * 128:(c + 1) * 128], done[2 * s + t], b.free,
                                mark=(m == 1 and t == 1))
                use_act = (j // 2) % 2
                for m, (c, s) in enumerate(jobs[j:j + 2]):
                    o = hT[:, c, s * 256:(s + 1) * 256]
                    i = b.t[:, m * 256:(m + 1) * 256]
                    sc, bi = scale(c, s), bias(c, s) if bias else None
                    if use_act:
                        if bi is None:
                            e = act(o, i, ACT.Copy, tk, scale=sc)
                        else:
                            e = act(o, i, ACT.Identity, tk, scale=sc, bias=bi)
                    elif bi is None:
                        e = ts(dv, o, i, sc, None, ALU.mult, None, tk)
                    else:
                        e = ts(dv, o, i, sc, bi, ALU.mult, ALU.add, tk)
                b.done(e)
            return [ac.last(), dv.last()]

        def ffn(hT, ready, gu, down, hf, sg, nt, finish):
            N = nt * 128
            hold = [None] * 3
            hfd = []
            for g in range(11):
                w, rd, slot = ring.load(gu[g], 4096)
                w = w.rearrange("p (k h n) -> p k h n", k=8, h=2)
                for f in range(2):
                    j = 2 * g + f
                    if nt == 2:
                        b1 = b2 = banks.get()
                        po1, po2 = b1.t[:, 0:256], b1.t[:, 256:512]
                    else:
                        b1, b2 = banks.get(), banks.get()
                        po1, po2 = b1.t[:, :], b2.t[:, :]
                    for h, (b, o) in enumerate(((b1, po1), (b2, po2))):
                        for k in range(8):
                            tk = mm(o, w[:, k, h, f * 128:(f + 1) * 128], hT[:, k, 0:N], rd, ready, b.free,
                                    start=k == 0, stop=k == 7, mark=(h == 1 and k == 7))
                    s = sg[:, j % 3, 0:N]
                    a = act(s, po1, ACT.Silu, tk, hold[j % 3])
                    d = tt(dv, hf[:, j, 0:N], s, po2, ALU.mult, a, tk)
                    hold[j % 3] = d
                    hfd.append(d)
                    b1.done(d)
                    if b2 is not b1:
                        b1.done(a)
                        b2.done(d)
                ring.free(slot, tk)
            acc = [[banks.get() for _ in range(2)] for _ in range(nt)]
            for q in range(6):
                nj = min(4, 22 - 4 * q)
                w, rd, slot = ring.load(down[q * 512:q * 512 + nj * 128, :].rearrange("(c p) n -> p c n", p=P),
                                        nj * 1024)
                w = w.rearrange("p (c n) -> p c n", n=1024)
                for jj in range(nj):
                    j = 4 * q + jj
                    for t in range(nt):
                        for h in range(2):
                            b = acc[t][h]
                            tk = mm(b.t[:, :], hf[:, j, t * 128:(t + 1) * 128], w[:, jj, h * 512:(h + 1) * 512],
                                    rd, hfd[j], b.free, start=j == 0, stop=j == 21,
                                    mark=(j == 21 or (jj == nj - 1 and t == nt - 1 and h == 1)))
                            if j == 21:
                                b.tok = tk
                ring.free(slot, tk)
            for t in range(nt):
                for h in range(2):
                    b = acc[t][h]
                    b.done(finish(t, h, b.t[:, :], b.tok))

        xa = [xt[:, t, :] for t in range(2)]

        def ffn1(l, which):
            top[0] = 0
            barrier()
            hT, hf, xs = area3(8, 256), area3(22, 256), area3(2, 1024)
            sg, junk = area3(3, 256), area(1024)
            nm = "n1" if which == 1 else "n2"
            ready = norm_t(xa, hT, lambda c, s: col(l, nm, c), None, xs, junk)
            ffn(hT, ready, A[f"ffn{which}_w_gate_up"][l], A[f"ffn{which}_w_down"][l], hf, sg, 2,
                lambda t, h, p, tk: stt(xt[:, t, h * 512:(h + 1) * 512], p, 0.5, xt[:, t, h * 512:(h + 1) * 512],
                                        ALU.mult, ALU.add, tk))

        def load_small(l, *after):
            sw = smallw[:, 0:1536].rearrange("p (w h e) -> p w h e", w=3, h=4)
            for i, nm in enumerate(("mlstm_wq", "mlstm_wk", "mlstm_wv")):
                load(f"sm{l}", sw[:, i], A[nm][l].rearrange("h d e -> d h e"), *after)
            load(f"sm{l}", smallw[0:64, 1536:2048], A["rwkv_w_up"][l])
            load(f"sm{l}", smallw[64:128, 1536:2048], A["rwkv_a_up"][l])
            load(f"sm{l}", smallw[:, 2048:2560], A["rwkv_g_up"][l])

        load_small(0)

        def evac(q, o, i, *after, scale=None):
            if q is ac:
                return act(o, i, ACT.Copy, *after, scale=1.0 if scale is None else scale)
            if scale is not None:
                return ts(q, o, i, scale, None, ALU.mult, None, *after)
            return cp(q, o, i, *after)

        def v256(b):
            return b.t[:, :].rearrange("p (a b) -> p a b", b=256)

        def v128(b):
            return b.t[:, :].rearrange("p (a b) -> p a b", b=128)

        def v64(b):
            return b.t[:, :].rearrange("p (a b) -> p a b", b=64)

        def bc(a, n):
            return a.unsqueeze(1).broadcast_to([a.shape[0], n, a.shape[1]])

        def bl(a, n):
            return a.unsqueeze(2).broadcast_to([a.shape[0], a.shape[1], n])

        def mixers(l):
            top[0] = 0
            barrier(small[f"sm{l}"])
            hT, yT = area3(8, 256), area3(16, 256)
            base = top[0]
            xs, junk = area3(2, 1024), area(1024)
            ready = norm_t(xa, hT, lambda c, s: col(l, "nm", c), None, xs, junk)
            sw = smallw[:, 0:1536].rearrange("p (w h e) -> p w h e", w=3, h=4)

            def project_t(uT, pad, first):
                for q in range(0, 7, 2):
                    n = min(2, 7 - q)
                    w, rd, slot = ring.load(A["w_in_t"][l, first + q:first + q + n].rearrange("a p n -> p a n"), n * 2048)
                    w = w.rearrange("p (a k n) -> p a k n", a=n, k=8)
                    for i in range(n):
                        b = banks.get()
                        for m in range(2):
                            for k in range(8):
                                tk = mm(b.t[:, m * 256:(m + 1) * 256], w[:, i, k, m * 128:(m + 1) * 128], hT[:, k, :],
                                        rd, ready, b.free, start=k == 0, stop=k == 7, mark=(m == 1 and k == 7))
                        c = 2 * (q + i)
                        b.done(cp(ac if i else dv, uT[:, c:c + 2, pad:pad + 256], v256(b), tk))
                    ring.free(slot, tk)

            top[0] = base
            barrier()
            KR = area4(8, 2, 128)
            be, ch = area3(4, 256), area3(4, 256)
            KBV = area3(16, 128)
            bet, cht, vt = area3(2, 512), area3(2, 512), area3(2, 512)
            gl = area(256)
            Wc = area3(4, 4)
            keep = top[0]
            uT = area3(14, 257)
            us = area3(14, 256)
            ab = area3(4, 256)
            cwb = area3(4, 256)
            tm = [area3(4, 256) for _ in range(2)]
            zero(uT[:, :, 0:1])
            project_t(uT, 1, 0)
            uev = [ac.last(), dv.last()]
            tt(dv, us[:, :, :], uT[:, :, 0:256], uT[:, :, 1:257], ALU.subtract, uev)
            for i in range(14):
                stt(us[:, i, :], us[:, i, :], col(l, "mu", i), uT[:, i, 1:257], ALU.mult, ALU.add)
            r_, k_, v_ = us[:, 0:4, :], us[:, 4:8, :], us[:, 8:12, :]
            usd = dv.last()
            sgw = uT[:, 0:4, 1:257]
            act(us[0:64, 12, :], us[0:64, 12, :], ACT.Tanh, usd)
            th = act(gl, us[:, 13, :], ACT.Sigmoid)
            bw = [banks.get(), banks.get()]
            ba = [banks.get(), banks.get()]
            for c in range(4):
                o = slice((c % 2) * 256, (c % 2) * 256 + 256)
                cs = slice(1536 + c * 128, 1664 + c * 128)
                mm(bw[c // 2].t[:, o], smallw[0:64, cs], us[0:64, 12, :], th, bw[c // 2].free)
            for c in range(4):
                o = slice((c % 2) * 256, (c % 2) * 256 + 256)
                cs = slice(1536 + c * 128, 1664 + c * 128)
                tk = mm(ba[c // 2].t[:, o], smallw[64:128, cs], us[64:128, 12, :], ba[c // 2].free, mark=True)
            for c in range(4):
                o = slice((c % 2) * 256, (c % 2) * 256 + 256)
                e = act(sgw[:, c, :], bw[c // 2].t[:, o], ACT.Sigmoid, tk, bias=col(l, "w0", c))
                bw[c // 2].done(e)
            for c in range(4):
                o = slice((c % 2) * 256, (c % 2) * 256 + 256)
                e = act(ab[:, c, :], ba[c // 2].t[:, o], ACT.Sigmoid, tk, bias=col(l, "a0", c))
                ba[c // 2].done(e)
            sgd = e
            kk = tm[0]
            for c in range(4):
                ts(dv, kk[:, c, :], k_[:, c, :], col(l, "kk", c), None, ALU.mult, None)
            sq = act(tm[1], kk, ACT.Square, dv.last())
            bs = [banks.get(), banks.get()]
            for c in range(4):
                o = slice((c % 2) * 256, (c % 2) * 256 + 256)
                tk = mm(bs[c // 2].t[:, o], bones, tm[1][:, c, :], sq, bs[c // 2].free, mark=True)
            for i in range(2):
                e = act(tm[1][:, 2 * i:2 * i + 2, :], bs[i].t[:, :].rearrange("p (a b) -> p a b", b=256), ACT.Sqrt, tk)
                bs[i].done(e)
            ts(dv, tm[1], tm[1], 1e-6, None, ALU.max, None, e)
            rcp(tm[1], tm[1])
            tt(dv, kk, kk, tm[1], ALU.mult)
            for c in range(4):
                ts(dv, tm[1][:, c, :], ab[:, c, :], 1.0, col(l, "ka", c), ALU.subtract, ALU.mult, sgd)
            stt(k_, tm[1], 1.0, k_, ALU.add, ALU.mult)
            for c in range(4):
                stt(tm[1][:, c, :], r_[:, c, :], col(l, "rk", c), k_[:, c, :], ALU.mult, ALU.mult)
            bs = [banks.get(), banks.get()]
            t1 = dv.last()
            for c in range(4):
                o = slice((c % 2) * 256, (c % 2) * 256 + 256)
                tk = mm(bs[c // 2].t[:, o], bones, tm[1][:, c, :], t1, bs[c // 2].free, mark=True)
            for i in range(2):
                e = tt(dv, yT[:, 12 + 2 * i:14 + 2 * i, :], bs[i].t[:, :].rearrange("p (a b) -> p a b", b=256),
                       v_[:, 2 * i:2 * i + 2, :], ALU.mult, tk)
                bs[i].done(e)
            tt(dv, ab, kk, ab, ALU.mult)
            for c in range(4):
                dv(lambda e, o=cwb[:, c, :], i=sgw[:, c, :]: e.tensor_tensor_scan(o, scanm[:, :], i, 0.0,
                                                       ALU.mult, ALU.add))
            cw4 = cwb.rearrange("p c (a b) -> p (c a) b", b=64)
            cwd = dv.last()
            ww = tm[1]
            t8 = lambda a: a.rearrange("p c (t n) -> p (c t) n", n=128)
            w1 = act(ww, cwb, ACT.Exp, cwd, scale=-DECAY)
            d1 = tt(dv, KR[:, :, 1, :], t8(ww), t8(r_), ALU.mult, w1)
            d2 = tt(dv, sgw, cwb, sgw, ALU.subtract)
            w2 = act(ww, sgw, ACT.Exp, d1, d2, scale=-DECAY)
            d3 = tt(dv, KR[:, :, 0, :], t8(ww), t8(kk), ALU.mult, w2)
            w3 = act(ww, cwb, ACT.Exp, d3, scale=DECAY)
            tt(dv, be, ab, ww, ALU.mult, w3)
            tt(dv, ch, k_, ww, ALU.mult)
            w4 = act(Wc.rearrange("p c a -> p (c a)").unsqueeze(2), cw4[:, :, 63:64], ACT.Exp, scale=-DECAY)
            d4 = tt(dv, sgw2 := tm[0].rearrange("p c (a b) -> p (c a) b", b=64), cw4,
                    cw4[:, :, 63:64].broadcast_to([P, 16, 64]), ALU.subtract)
            w5 = act(tm[0], tm[0], ACT.Exp, d4, scale=DECAY)
            d5 = tt(dv, ab, ab, tm[0], ALU.mult, w5)
            d6 = tt(dv, k_, k_, tm[0], ALU.mult)
            for q, (src, dst) in enumerate(((lambda c, T: KR[:, 2 * c + T, 0, :], None),
                                            (lambda c, T: ab[:, c, T * 128:T * 128 + 128], bet),
                                            (lambda c, T: k_[:, c, T * 128:T * 128 + 128], cht),
                                            (lambda c, T: v_[:, c, T * 128:T * 128 + 128], vt))):
                for T in range(2):
                    b = banks.get()
                    for c in range(4):
                        tk = tr(b.t[:, c * 128:(c + 1) * 128], src(c, T), d6, b.free, mark=(c == 3))
                    o = KBV[:, T * 8:T * 8 + 8, 0:64] if dst is None else dst[:, T, :]
                    b.done(cp((ac, dv)[T], o, v64(b) if dst is None else b.t[:, :], tk))

            top[0] = keep
            barrier()
            GH = area4(16, 2, 128)
            over = top[0]
            Tm, TT, X, CT = (area3(8, 128) for _ in range(4))
            nT = area3(16, 128)
            nTT = area3(4, 256)
            MT = area4(2, 4, 64)
            yf = yT[:, 0:12, :].rearrange("p a b -> p (a b)")
            AB = yf[:, 0:2048].rearrange("p (u w n) -> p u w n", u=8, w=2)
            NN = yf[:, 2048:2816].rearrange("p (c h n) -> p c h n", c=3, h=4)
            for T in range(2):
                for h in range(8):
                    c, j = h // 2, h % 2
                    js = slice(64 * j, 64 * j + 64)
                    b = banks.get()
                    kr = KR[js, 2 * c + T, :, :].rearrange("p a b -> p (a b)")
                    mm(b.t[:, 0:256], be[js, c, T * 128:T * 128 + 128], kr, b.free)
                    tk = mm(b.t[:, 256:512], ch[js, c, T * 128:T * 128 + 128], kr, mark=True)
                    g4 = b.t[:, :].rearrange("p (a b n) -> p a b n", a=2, b=2)
                    m4 = mask4[:, :, :].rearrange("p (a b) n -> p a b n", b=2)
                    tt(dv, AB[:, 4 * j + c, :, :], g4[:, :, 0, :], m4[:, :, 0, :], ALU.mult, tk)
                    b.done(tt(dv, GH[:, T * 8 + h, :, :], g4[:, :, 1, :], m4[:, :, 1, :], ALU.mult))
                abd = dv.last()
                for j in range(2):
                    js = slice(64 * j, 64 * j + 64)
                    b = banks.get()
                    for c in range(4):
                        tk = mm(b.t[:, c * 128:(c + 1) * 128], KR[js, 2 * c + T, 0, :],
                                be[js, c, T * 128:T * 128 + 128], b.free, mark=(c == 3))
                    gs = slice(4 * j, 4 * j + 4)
                    b.done(tt(dv, Tm[:, gs, :], v128(b), bc(l2, 4), ALU.mult, tk))
                    tt(dv, Tm[:, gs, :], bc(ident, 4), Tm[:, gs, :], ALU.subtract)
                    tt(po, TT[:, gs, :], AB[:, gs, 0, :], bc(l2t, 4), ALU.mult, abd)
                    tt(po, TT[:, gs, :], bc(ident, 4), TT[:, gs, :], ALU.subtract)
                tdone = [[dv.last(), po.last()]] * 2
                xd = [None, None]
                for L in range(5):
                    for j in range(2):
                        gs = slice(4 * j, 4 * j + 4)
                        ct = tt(po, CT[:, gs, :], AB[:, gs, 0, :], bc(lvl[L], 4), ALU.mult, tdone[j])
                        b = banks.get()
                        for c in range(4):
                            u = 4 * j + c
                            tk = mm(b.t[:, c * 128:(c + 1) * 128], CT[:, u, :], Tm[:, u, :], ct, tdone[j], b.free,
                                    mark=(c == 3))
                        xd[j] = cp(ac, X[:, gs, :], v128(b), tk)
                        b.done(xd[j])
                    for j in range(2):
                        gs = slice(4 * j, 4 * j + 4)
                        b2, b3 = banks.get(), banks.get()
                        for c in range(4):
                            u = 4 * j + c
                            tk = mm(b3.t[:, c * 128:(c + 1) * 128], X[:, u, :], TT[:, u, :], xd[j], b3.free,
                                    mark=(c == 3))
                        if L < 4:
                            for c in range(4):
                                u = 4 * j + c
                                tk = mm(b2.t[:, c * 128:(c + 1) * 128], TT[:, u, :], X[:, u, :], b2.free,
                                        mark=(c == 3))
                            b2.done(tt(dv, Tm[:, gs, :], Tm[:, gs, :], v128(b2), ALU.subtract, tk))
                        else:
                            b2.done(b2.free)
                        tdone[j] = tt(dv, TT[:, gs, :], TT[:, gs, :], v128(b3), ALU.subtract, tk)
                        b3.done(tdone[j])
                    fill(1)
                b = banks.get()
                for h in range(8):
                    c, j = h // 2, h % 2
                    tk = mm(b.t[:, h * 64:(h + 1) * 64], AB[:, 4 * j + c, 1, :], vt[:, T, h * 64:(h + 1) * 64],
                            b.free, mark=(h == 7))
                bv = cp(dv, KBV[:, T * 8:T * 8 + 8, 64:128], v64(b), tk)
                b.done(bv)
                for q in range(2):
                    b = banks.get()
                    for m in range(4):
                        h = 4 * q + m
                        c, j = h // 2, h % 2
                        tk = mm(b.t[:, m * 128:(m + 1) * 128], TT[:, 4 * j + c, :], KBV[:, T * 8 + h, :], bv, tdone,
                                b.free, mark=(m == 3))
                    nt_ = evac(ac, nT[:, T * 8 + 4 * q:T * 8 + 4 * q + 4, :], v128(b), tk, scale=-1.0)
                    b.done(nt_)
                b = banks.get()
                for h in range(8):
                    c, j = h // 2, h % 2
                    tk = mm(b.t[64 * j:64 * j + 64, c * 128:(c + 1) * 128], KBV[:, T * 8 + h, 0:64],
                            TT[:, 4 * j + c, :], b.free, mark=(h == 7))
                b.done(evac(ac, nTT[:, :, T * 128:T * 128 + 128], v128(b), tk, scale=-1.0))
                for i in range(2):
                    cc = 2 * T + i
                    if cc == 3:
                        continue
                    rs = slice(64 * i, 64 * i + 64)
                    b = banks.get()
                    for h in range(8):
                        c, j = h // 2, h % 2
                        hs = slice(h * 64, (h + 1) * 64)
                        os = slice(64 * j, 64 * j + 64)
                        mm(b.t[os, c * 128:c * 128 + 64], nT[rs, T * 8 + h, 0:64], bet[rs, T, hs], nt_, b.free)
                        mm(b.t[os, c * 128 + 64:c * 128 + 128], cht[rs, T, hs], vt[rs, T, hs], start=True, stop=False)
                        tk = mm(b.t[os, c * 128 + 64:c * 128 + 128], bet[rs, T, hs], nT[rs, T * 8 + h, 64:128],
                                start=False, stop=True, mark=(h == 7))
                    if cc:
                        for c in range(4):
                            stt(MT[:, cc - 1, c, :], i2, Wc[:, c, cc:cc + 1], b.t[:, c * 128:c * 128 + 64],
                                ALU.mult, ALU.add, tk)
                    b.done(cp(dv, NN[:, cc, :, :], v128(b)[:, :, 64:128], tk))

            top[0] = over
            barrier()
            S = area4(4, 4, 64)
            SA = area3(16, 64)
            Yb = area3(16, 64)
            Yc = area3(16, 64)
            zero(S[:, 0, :, :])
            sd = cp(dv, S[:, 1, :, :], NN[:, 0, :, :])
            for cc in (1, 2):
                bj = [banks.get(), banks.get()]
                for j in range(2):
                    js = slice(64 * j, 64 * j + 64)
                    for c in range(4):
                        tk = mm(bj[j].t[js, c * 64:(c + 1) * 64], MT[js, cc - 1, c, :], S[js, cc, c, :], sd,
                                bj[j].free, mark=(c == 3))
                for j in range(2):
                    js = slice(64 * j, 64 * j + 64)
                    sd = tt(dv, S[js, cc + 1, :, :], v64(bj[j])[js, 0:4, :], NN[js, cc, :, :], ALU.add, tk)
                    bj[j].done(sd)
            fill(2)
            bj = [banks.get(), banks.get()]
            for j in range(2):
                js = slice(64 * j, 64 * j + 64)
                for cc in range(4):
                    for c in range(4):
                        T, i = cc // 2, cc % 2
                        tk = mm(bj[j].t[64 * i:64 * i + 64, (T * 4 + c) * 64:(T * 4 + c + 1) * 64],
                                nTT[js, c, cc * 64:cc * 64 + 64], S[js, cc, c, :], sd, bj[j].free,
                                mark=(cc == 3 and c == 3))
            SAj = SA.rearrange("p (a j) n -> p a j n", j=2)
            nTj = nT.rearrange("p (a j) n -> p a j n", j=2)
            Ybj = Yb.rearrange("p (a j) n -> p a j n", j=2)
            for j in range(2):
                sad = tt(dv, SAj[:, :, j, :], v64(bj[j]), nTj[:, :, j, 64:128], ALU.add, tk)
                bj[j].done(sad)
            for j in range(2):
                js = slice(64 * j, 64 * j + 64)
                b = banks.get()
                for T in range(2):
                    for c in range(4):
                        u = T * 8 + 2 * c + j
                        rg = slice((T * 4 + c) * 64, (T * 4 + c + 1) * 64)
                        mm(b.t[:, rg], GH[:, u, 0, :], SA[:, u, :], sad, b.free, start=True, stop=False)
                        mm(b.t[:, rg], GH[:, u, 1, :], vt[:, T, (2 * c + j) * 64:(2 * c + j + 1) * 64],
                           start=False, stop=False)
                        for i in range(2):
                            tk = mm(b.t[64 * i:64 * i + 64, rg], KR[js, 2 * c + T, 1, 64 * i:64 * i + 64],
                                    S[js, 2 * T + i, c, :], start=False, stop=True,
                                    mark=(T == 1 and c == 3 and i == 1))
                b.done(cp(dv, Ybj[:, :, j, :], v64(b), tk))
            fill(3)
            mu = st[:, 16:32]
            va = st[:, 32:48]
            red(mu, Yb, ALU.add)
            ts(dv, mu, mu, 1.0 / 64, None, ALU.mult, None)
            yc = tt(dv, Yc, Yb, bl(mu, 64), ALU.subtract)
            s2 = act(Yb, Yc, ACT.Square, yc)
            r2 = red(va, Yb, ALU.add, s2)
            ts(po, va, va, 1.0 / 64, 64e-5, ALU.mult, ALU.add, r2)
            pw = power(va, va, 16)
            yn = tt(dv, Yc, Yc, bl(va, 64), ALU.mult, pw)
            Ycf = Yc.rearrange("p (t h) n -> p t (h n)", t=2)
            for q in range(2):
                b, bg = banks.get(), banks.get()
                for m in range(2):
                    c = 2 * q + m
                    for T in range(2):
                        tr(b.t[:, (2 * m + T) * 128:(2 * m + T + 1) * 128], Ycf[:, T, c * 128:(c + 1) * 128], yn, b.free)
                for m in range(2):
                    c = 2 * q + m
                    tk = mm(bg.t[:, m * 256:(m + 1) * 256], smallw[:, 2048 + c * 128:2176 + c * 128], gl, bg.free,
                            mark=True)
                tmp = Yb.rearrange("p a b -> p (a b)")[:, 0:512].rearrange("p (a b) -> p a b", b=256)
                for m in range(2):
                    c = 2 * q + m
                    ts(dv, tmp[:, m, :], b.t[:, m * 256:(m + 1) * 256], col(l, "lw", c), col(l, "lb", c),
                       ALU.mult, ALU.add, tk)
                ys = yT[:, 12 + 2 * q:14 + 2 * q, :]
                b.done(tt(dv, ys, tmp, ys, ALU.add))
                bg.done(tt(dv, ys, ys, v256(bg), ALU.mult))

            top[0] = base
            barrier()
            uT = area3(14, 259)
            zt = area3(2, 1024)
            ot = area3(2, 512)
            dg = area3(2, 24)
            xc = area3(14, 256)
            here = top[0]
            zero(uT[:, :, 0:3])
            project_t(uT, 3, 7)
            cvd = [ac.last(), dv.last()]
            for q in range(4):
                n = 512 if q < 3 else 24
                src = A["w_in_n"][l, q] if q < 3 else A["w_in_s"][l]
                w, rd, slot = ring.load(src, 8 * n)
                w = w.rearrange("p (k n) -> p k n", k=8)
                for T in range(2):
                    b = banks.get()
                    for k in range(8):
                        tk = mm(b.t[:, 0:n], hT[:, k, T * 128:(T + 1) * 128], w[:, k, :], rd, b.free,
                                start=k == 0, stop=k == 7, mark=(k == 7))
                    if q < 2:
                        e = act(zt[:, T, q * 512:(q + 1) * 512], b.t[:, :], ACT.Silu, tk)
                    elif q == 2:
                        e = act(ot[:, T, :], b.t[:, :], ACT.Sigmoid, tk)
                    else:
                        e = cp(ac, dg[:, T, :], b.t[:, 0:24], tk)
                    b.done(e)
                ring.free(slot, tk)
            for c in range(14):
                ts(dv, xc[:, c, :], uT[:, c, 0:256], col(l, "cw", 4 * c), None, ALU.mult, None, cvd)
                for k in range(1, 4):
                    stt(xc[:, c, :], uT[:, c, k:k + 256], col(l, "cw", 4 * c + k), xc[:, c, :], ALU.mult, ALU.add)
            cd = dv.last()
            for c in range(14):
                xcd = act(xc[:, c, :], xc[:, c, :], ACT.Silu, cd, bias=col(l, "cb", c))

            def softplus(o, x, n, *after):
                t = st[:, 440:440 + n]
                a = act(t, x, ACT.Abs, dv.last(), *after)
                a = act(t, t, ACT.Exp, scale=-1.0)
                a = act(t, t, ACT.Ln, a, bias=1.0)
                return stt(o, x, 0.0, t, ALU.max, ALU.add, a)

            R0 = 56 * l
            Xt = area3(2, 1024)
            xd_ = area3(2, 1024)
            xw = area(1024)
            Bt = area(128)
            Ss = area(512)
            cb = area4(2, 2, 128)
            Ms = [area3(4, 128) for _ in range(3)]
            yy = area3(2, 1024)
            dt = st[:, 64:96].rearrange("p (t h) -> p t h", t=2)
            ad = st[:, 96:128].rearrange("p (t h) -> p t h", t=2)
            acu = st[:, 128:160].rearrange("p (t h) -> p t h", t=2)
            nac = st[:, 160:192].rearrange("p (t h) -> p t h", t=2)
            en = st[:, 192:208]
            wd = st[:, 208:224]
            xa1 = st[:, 224:240]
            nA = st[:, 240:256]
            gm = st[:, 256:264]
            w = act(nA, rows[:, R0 + 16:R0 + 32], ACT.Exp, cd)
            ts(dv, nA, nA, -1.0, None, ALU.mult, None, w)
            tt(dv, dt, dg[:, :, 0:16], bc(rows[:, R0:R0 + 16], 2), ALU.add, ac.last())
            softplus(st[:, 64:96], st[:, 64:96], 32)
            a_ = tt(dv, ad, dt, bc(nA, 2), ALU.mult)
            b = banks.get()
            for T in range(2):
                mm(b.t[:, T * 16:T * 16 + 16], tri, ad[:, T, :], a_, b.free)
            tk = mm(b.t[:, 32:48], ones, ad[:, 0, :], mark=True)
            cp(dv, st[:, 128:160], b.t[:, 0:32], tk)
            ts(dv, st[:, 160:192], b.t[:, 0:32], -1.0, None, ALU.mult, None)
            e = tt(dv, en, b.t[:, 32:48], acu[:, 0, :], ALU.subtract)
            b.done(e)
            w = act(wd, en, ACT.Exp, e)
            w = act(xa1, acu[:, 1, :], ACT.Exp)
            for T in range(2):
                for q in range(2):
                    b = banks.get()
                    for c in range(4):
                        tk = tr(b.t[:, c * 128:(c + 1) * 128], xc[:, 4 * q + c, T * 128:(T + 1) * 128], xcd, b.free,
                                mark=(c == 3))
                    b.done(cp(ac, Xt[:, T, q * 512:(q + 1) * 512], b.t[:, :], tk))
            b = banks.get()
            tk = tr(b.t[:, 0:128], xc[:, 8, 0:128], b.free, mark=True)
            b.done(cp(ac, Bt, b.t[:, 0:128], tk))
            xd = ac.last()
            h64 = lambda a: a.rearrange("p (h n) -> p h n", n=64)
            for T in range(2):
                tt(dv, h64(xd_[:, T, :]), h64(Xt[:, T, :]), bl(dt[:, T, :], 64), ALU.mult, xd)
            xwd = tt(dv, h64(xw), h64(xd_[:, 0, :]), bl(wd, 64), ALU.mult)
            bg = [banks.get(), banks.get()]
            for g in range(2):
                for T in range(2):
                    s = slice(T * 128, (T + 1) * 128)
                    tk = mm(bg[g].t[:, s], xc[64 * g:64 * g + 64, 8, s], xc[64 * g:64 * g + 64, 9, s], xcd,
                            bg[g].free, mark=(T == 1))
            for g in range(2):
                bg[g].done(cp(ac, cb[:, g, :, :], bg[g].t[:, 0:256].rearrange("p (a b) -> p a b", b=128), tk))
            b = banks.get()
            for g in range(2):
                tk = mm(b.t[64 * g:64 * g + 64, :], Bt[:, 64 * g:64 * g + 64], xw[:, g * 512:(g + 1) * 512], xwd, xd,
                        b.free, mark=(g == 1))
            ssd = cp(ac, Ss, b.t[:, :], tk)
            b.done(ssd)
            n = 0
            hold = [None] * 3
            for T in range(2):
                for g in range(2):
                    by = banks.get()
                    for q in range(2):
                        b = banks.get()
                        for m in range(4):
                            h = 8 * g + 4 * q + m
                            tk = mm(b.t[:, m * 128:(m + 1) * 128], ad[:, T, h:h + 1].broadcast_to([P, 128]), tri,
                                    b.free, mark=(m == 3))
                        M = Ms[n % 3]
                        for m in range(4):
                            h = 8 * g + 4 * q + m
                            e = stt(M[:, m, :], b.t[:, m * 128:(m + 1) * 128], nac[:, T, h:h + 1], negT, ALU.add,
                                    ALU.add, tk, hold[n % 3])
                        b.done(e)
                        x = act(M, M, ACT.Exp, e)
                        e = tt(dv, M, M, bc(cb[:, g, T, :], 4), ALU.mult, x)
                        for m in range(4):
                            h = 8 * g + 4 * q + m
                            hold[n % 3] = tk = mm(by.t[:, (4 * q + m) * 64:(4 * q + m + 1) * 64], M[:, m, :],
                                                  xd_[:, T, h * 64:(h + 1) * 64], e, by.free, mark=(m == 3))
                        n += 1
                    ys = yy[:, T, g * 512:(g + 1) * 512]
                    by.done(cp(dv, ys, by.t[:, :], tk))
                    if T == 1:
                        b = banks.get()
                        tk = mm(b.t[:, :], xc[64 * g:64 * g + 64, 9, 128:256], Ss[64 * g:64 * g + 64, :], ssd, b.free,
                                mark=True)
                        tmp = xw[:, g * 512:(g + 1) * 512]
                        e = tt(dv, h64(tmp), v64(b), bl(xa1[:, 8 * g:8 * g + 8], 64), ALU.mult, tk)
                        b.done(e)
                        tt(dv, ys, ys, tmp, ALU.add)
            for T in range(2):
                tt(dv, h64(Xt[:, T, :]), h64(Xt[:, T, :]), bl(rows[:, R0 + 32:R0 + 48], 64), ALU.mult)
                tt(dv, yy[:, T, :], yy[:, T, :], Xt[:, T, :], ALU.add)
                e = tt(dv, yy[:, T, :], yy[:, T, :], zt[:, T, :], ALU.mult)
            tiles = [yy[:, T, g * 512:(g + 1) * 512] for T in range(2) for g in range(2)]
            r = rstd(tiles, gm, 4, 512, 1e-6, Xt[:, 0, :], e)
            for i, a in enumerate(tiles):
                e = ts(dv, a, a, gm[:, i:i + 1], None, ALU.mult, None, r)

            def back(src, first, count, name, *after):
                for c in range(0, count, 2):
                    b = banks.get()
                    for m in range(2):
                        for T in range(2):
                            tk = tr(b.t[:, (2 * m + T) * 128:(2 * m + T + 1) * 128],
                                    src[:, T, (c + m) * 128:(c + m + 1) * 128], b.free, *after, mark=(m == 1 and T == 1))
                    for m in range(2):
                        e = ts(dv, yT[:, first + c + m, :], b.t[:, m * 256:(m + 1) * 256], col(l, name, c + m), None,
                               ALU.mult, None, tk)
                    b.done(e)

            back(yy, 0, 8, "sn", e)

            top[0] = here
            barrier()
            qT, kT = area3(4, 256), area3(4, 256)
            kt, vt, vw = area3(4, 128), area4(2, 4, 128), area3(4, 128)
            Dm = [area3(4, 128) for _ in range(2)]
            PT = [area3(4, 128) for _ in range(2)]
            Cs = area3(4, 128)
            nv = area(4)
            hh = area3(2, 512)
            s4 = lambda i: st[:, 64 + 8 * i:72 + 8 * i].rearrange("p (t h) -> p t h", t=2)
            li, lf, bcu, mi, il, mt, wi, em, den = (s4(i) for i in range(9))
            nl = st[:, 136:144].rearrange("p (t h) -> p t h", t=2)
            g8 = st[:, 144:160].rearrange("p (t h) -> p t h", t=2)
            bend, mpv, wend, t4 = (st[:, 160 + 4 * i:164 + 4 * i] for i in range(4))
            nmt = st[:, 176:184].rearrange("p (t h) -> p t h", t=2)
            gm = st[:, 184:192]
            xm = uT[:, 10:14, 3:259]
            xcc = xc[:, 10:14, :]
            sc = 128 ** -0.5
            for i, (o, scale) in enumerate(((qT, None), (kT, sc))):
                for q in range(2):
                    b = banks.get()
                    for m in range(2):
                        tk = mm(b.t[:, m * 256:(m + 1) * 256], sw[:, i, 2 * q + m, :], xcc[:, 2 * q + m, :], b.free,
                                mark=(m == 1))
                    b.done(evac(ac, o[:, 2 * q:2 * q + 2, :], v256(b), tk, scale=scale))
            b = banks.get()
            for h in range(4):
                tk = mm(b.t[:, h * 128:(h + 1) * 128], xcc[:, h, 0:128], sw[:, 1, h, :], b.free, mark=(h == 3))
            b.done(evac(ac, kt, v128(b), tk, scale=sc))
            for T in range(2):
                b = banks.get()
                for h in range(4):
                    tk = mm(b.t[:, h * 128:(h + 1) * 128], xm[:, h, T * 128:(T + 1) * 128], sw[:, 2, h, :], b.free,
                            mark=(h == 3))
                b.done(cp(ac, vt[:, T, :, :], v128(b), tk))
            projd = ac.last()
            if l == 0:
                load_small(1, tk)
            tt(dv, g8, dg[:, :, 16:24], bc(rows[:, R0 + 48:R0 + 56], 2), ALU.add)
            cp(dv, li, g8[:, :, 0:4])
            ts(dv, lf, g8[:, :, 4:8], -1.0, None, ALU.mult, None)
            lff = st[:, 72:80]
            softplus(lff, lff, 8)
            cp(dv, nl, lf)
            ld = ts(dv, lff, lff, -1.0, None, ALU.mult, None)
            b = banks.get()
            for T in range(2):
                mm(b.t[:, 4 * T:4 * T + 4], tri, lf[:, T, :], ld, b.free)
            tk = mm(b.t[:, 8:12], ones, lf[:, 0, :], mark=True)
            cp(dv, st[:, 80:88], b.t[:, 0:8], tk)
            e = cp(dv, bend, b.t[:, 8:12])
            b.done(e)
            be_ = []
            for T in range(2):
                b = banks.get()
                for h in range(4):
                    hs = slice(h * 128, (h + 1) * 128)
                    mm(b.t[:, hs], nl[:, T, h:h + 1].broadcast_to([P, 128]), tri, b.free, stop=False)
                    tk = mm(b.t[:, hs], li[:, T, h:h + 1].broadcast_to([P, 128]), ident, start=False, mark=(h == 3))
                if T == 0:
                    red(t4, v128(b), ALU.max, tk)
                    tt(dv, t4, t4, bend, ALU.add)
                    tt(dv, mpv, bend, t4, ALU.max)
                    tt(dv, wend, li[:, 0, :], bcu[:, 0, :], ALU.subtract)
                    tt(dv, wend, wend, bend, ALU.add)
                    e = tt(dv, wend, wend, mpv, ALU.subtract)
                    we = act(wend, wend, ACT.Exp, e)
                for h in range(4):
                    e = stt(Dm[T][:, h, :], b.t[:, h * 128:(h + 1) * 128], bcu[:, T, h:h + 1], neg, ALU.add, ALU.add, tk)
                b.done(e)
                red(mi[:, T, :], Dm[T], ALU.max)
            cp(dv, il[:, 0, :], bcu[:, 0, :])
            tt(dv, il[:, 1, :], bcu[:, 1, :], mpv, ALU.add)
            tt(dv, st[:, 104:112], st[:, 96:104], st[:, 88:96], ALU.max)
            tt(dv, st[:, 112:120], st[:, 96:104], st[:, 104:112], ALU.subtract)
            e = ts(dv, st[:, 176:184], st[:, 104:112], -1.0, None, ALU.mult, None)
            act(st[:, 112:120], st[:, 112:120], ACT.Exp, e)
            act(st[:, 120:128], st[:, 176:184], ACT.Exp)
            for T in range(2):
                for h in range(4):
                    wx = act(Dm[T][:, h, :], Dm[T][:, h, :], ACT.Exp, bias=nmt[:, T, h:h + 1])
            vwd = tt(dv, vw, vt[:, 0, :, :], bl(wend, 128), ALU.mult, we, projd)
            b = banks.get()
            for h in range(4):
                tk = mm(b.t[:, h * 128:(h + 1) * 128], kt[:, h, :], vw[:, h, :], vwd, projd, b.free, mark=(h == 3))
            csd = cp(ac, Cs, v128(b), tk)
            b.done(csd)
            b = banks.get()
            for h in range(4):
                tk = mm(b.t[:, h:h + 1], kt[:, h, :], wend[:, h:h + 1], b.free, mark=(h == 3))
            csd = cp(ac, nv, b.t[:, 0:4], tk)
            b.done(csd)
            for T in range(2):
                b = banks.get()
                for h in range(4):
                    s = slice(T * 128, (T + 1) * 128)
                    tk = mm(b.t[:, h * 128:(h + 1) * 128], qT[:, h, s], kT[:, h, s], projd, b.free, mark=(h == 3))
                e = tt(dv, Dm[T], v128(b), Dm[T], ALU.mult, tk, wx)
                b.done(e)
                red(den[:, T, :], Dm[T], ALU.add)
                b = banks.get()
                for h in range(4):
                    tk = tr(b.t[:, h * 128:(h + 1) * 128], Dm[T][:, h, :], e, b.free, mark=(h == 3))
                pt = cp(ac, PT[T], v128(b), tk)
                b.done(pt)
                b = banks.get()
                for h in range(4):
                    tk = mm(b.t[:, h * 128:(h + 1) * 128], PT[T][:, h, :], vt[:, T, h, :], pt, b.free, mark=(h == 3))
                h4 = hh[:, T, :].rearrange("p (h n) -> p h n", h=4)
                b.done(cp(dv, h4, v128(b), tk))
                if T == 1:
                    b, b2 = banks.get(), banks.get()
                    for h in range(4):
                        mm(b.t[:, h * 128:(h + 1) * 128], qT[:, h, 128:256], Cs[:, h, :], csd, b.free)
                    for h in range(4):
                        tk = mm(b2.t[:, h:h + 1], qT[:, h, 128:256], nv[:, h:h + 1], b2.free, mark=(h == 3))
                    e = tt(dv, vw, v128(b), bl(wi[:, 1, :], 128), ALU.mult, tk)
                    b.done(e)
                    tt(dv, h4, h4, vw, ALU.add)
                    e = tt(dv, t4, b2.t[:, 0:4], wi[:, 1, :], ALU.mult)
                    b2.done(e)
                    tt(dv, den[:, 1, :], den[:, 1, :], t4, ALU.add)
            dn = st[:, 128:136]
            e = act(dn, dn, ACT.Abs, dv.last())
            tt(dv, dn, dn, st[:, 120:128], ALU.max, e)
            rcp(dn, dn)
            for T in range(2):
                h4 = hh[:, T, :].rearrange("p (h n) -> p h n", h=4)
                tt(dv, h4, h4, bl(den[:, T, :], 128), ALU.mult)
                e = tt(dv, hh[:, T, :], hh[:, T, :], ot[:, T, :], ALU.mult)
            tiles = [hh[:, T, h * 128:(h + 1) * 128] for T in range(2) for h in range(4)]
            r = rstd(tiles, gm, 8, 128, 1e-6, Dm[0][:, 0, :], e)
            for i, a in enumerate(tiles):
                e = ts(dv, a, a, gm[:, i:i + 1], None, ALU.mult, None, r)
            back(hh, 8, 4, "mn", e)
            yd = [dv.last(), ac.last()]
            acc = [[banks.get() for _ in range(2)] for _ in range(2)]
            for q in range(4):
                w, rd, slot = ring.load(A["w_out"][l, q * 512:(q + 1) * 512, :].rearrange("(c p) n -> p c n", p=P), 4096)
                w = w.rearrange("p (c n) -> p c n", n=1024)
                for jj in range(4):
                    j = 4 * q + jj
                    for T in range(2):
                        for h in range(2):
                            b = acc[T][h]
                            tk = b.tok = mm(b.t[:, :], yT[:, j, T * 128:(T + 1) * 128], w[:, jj, h * 512:(h + 1) * 512],
                                            rd, yd, b.free, start=j == 0, stop=j == 15, mark=(j == 15 or jj == 3))
                ring.free(slot, tk)
            for T in range(2):
                for h in range(2):
                    b = acc[T][h]
                    o = xt[:, T, h * 512:(h + 1) * 512]
                    b.done(tt(dv, o, b.t[:, :], o, ALU.add, b.tok))

        def second():
            lg = rows[:, 112:120]
            ctx_off = 2048

            def gate(l, j, gb, dg, n, half):
                for v in range(n):
                    for c in range(8):
                        e = ts(dv, dg[:, c, :], ident, mods[:, l, 8 * (3 * j + 2) + c, v:v + 1], half, ALU.mult, ALU.mult)
                    for q in range(2):
                        b = banks.get()
                        for m in range(4):
                            tk = mm(b.t[:, m * 128:(m + 1) * 128], ones, dg[:, 4 * q + m, :], e, b.free, mark=(m == 3))
                        t = cp(ac, gb[:, v, q * 512:(q + 1) * 512], b.t[:, :], tk)
                        b.done(t)
                        dv.wait(tk)
                return t

            def modulated(l, j, tiles, hT, xs, junk):
                sct = st[:, 256:272].rearrange("p (c v) -> p c v", v=2)
                s = 8 * (3 * j + 1)
                stt(sct, mods[:, l, s:s + 8, :], 1.0, bl(ng2[:, l, j, :], 2), ALU.add, ALU.mult)
                ac.wait(dv.last())
                return norm_t(tiles, hT, lambda c, v: sct[:, c, v:v + 1],
                              lambda c, v: mods[:, l, 8 * 3 * j + c, v:v + 1], xs, junk)

            def add_gated(tiles, gb, tmp, gd):
                hold = [None] * 2
                cnt = [0]

                def finish(t, h, p, tk):
                    i = cnt[0] % 2
                    cnt[0] += 1
                    s = slice(h * 512, (h + 1) * 512)
                    m = tt(dv, tmp[:, i, :], p, gb[:, t // 2, s], ALU.mult, tk, gd, hold[i])
                    hold[i] = tt(po, tiles[t][:, s], tiles[t][:, s], tmp[:, i, :], ALU.add, m)
                    return m
                return finish

            top[0] = 0
            barrier()
            fill(99)
            ct = area3(2, 1024)
            fn = area(1024)
            junk = area(1024)
            ba = [q.last() for q in (pe, dv, po)]
            load("ctx", ct, A["ctx_2"].rearrange("o (t p) d -> p (o t) d", p=P), *ba)
            load("fn", fn, A["final_norm"].unsqueeze(0).broadcast_to([P, 1024]))
            r = rstd(xa, st[:, 0:2], 2, 1024, 1e-6, junk)
            for t in range(2):
                stt(xa[t], xa[t], st[:, t:t + 1], fn, ALU.mult, ALU.mult, r, small["fn"])
            barrier(small["ctx"])
            both = xa + [ct[:, t, :] for t in range(2)]

            def half_ffn(l, j, nt):
                top[0] = ctx_off
                barrier()
                hT, hf, xs = area3(8, nt * 128), area3(22, nt * 128), area3(nt, 1024)
                sg, junk, gb = area3(3, nt * 128), area(1024), area3(2, 1024)
                tiles = both[:nt]
                ready = modulated(l, j, tiles, hT, xs, junk)
                barrier()
                gd = gate(l, j, gb, xs[:, 0:1, :].rearrange("p a (c n) -> p (a c) n", c=8), nt // 2, 0.5)
                ffn(hT, ready, A["ffn_gu_2"][l, j // 2], A["ffn_w_down_2"][l, j // 2], hf, sg, nt,
                    add_gated(tiles, gb, xs[:, 0:1, :].rearrange("p a (c n) -> p (a c) n", c=2), gd))

            def fourier(l):
                top[0] = ctx_off
                barrier()
                hT, gb, row = area3(8, 512), area3(2, 1024), area(1024)
                d1, d2 = area3(2, 512), area3(2, 512)
                Z = area4(4, 4, 512)
                fT = area3(8, 512)
                load("four", d1, A["c_dft1"])
                load("four", d2, A["c_dft2"])
                load("four", row[0:1, :], A["four_b_2"])
                Zf = Z.rearrange("p a b c -> p (a b c)")
                xs = Zf[:, 0:4096].rearrange("p (a b) -> p a b", b=1024)
                ready = modulated(l, 1, both, hT, xs, Zf[:, 4096:5120])
                barrier(small["four"])
                gd = gate(l, 1, gb, Zf[:, 0:1024].rearrange("p (c n) -> p c n", c=8), 2, 1.0)
                barrier()
                for t in range(4):
                    for g in range(4):
                        b = banks.get()
                        for m in range(2):
                            tk = mm(b.t[:, :], hT[:, 2 * g + m, t * 128:(t + 1) * 128], d1[:, m, :], b.free,
                                    start=m == 0, stop=m == 1, mark=(m == 1))
                        b.done(cp((ac, dv)[g % 2], Z[:, t, g, :], b.t[:, :], tk))
                zd = [ac.last(), dv.last()]
                for c in range(8):
                    b = banks.get()
                    for s in range(2):
                        i = 0
                        for m in range(2):
                            for h in range(2):
                                o = h * 256 + (c % 2) * 128
                                tk = mm(b.t[:, s * 256:(s + 1) * 256], Z[:, 2 * s + m, c // 2, o:o + 128],
                                        d2[:, m, h * 256:(h + 1) * 256], zd, b.free, start=i == 0, stop=i == 3,
                                        mark=(i == 3 and s == 1))
                                i += 1
                    b.done(cp((ac, dv)[c % 2], fT[:, c, :], b.t[:, :], tk))
                fd = [ac.last(), dv.last()]
                acc = [[banks.get() for _ in range(2)] for _ in range(4)]
                for q in range(2):
                    w, rd, slot = ring.load(A["four_w_2"][0, q * 512:(q + 1) * 512, :].rearrange("(c p) n -> p c n", p=P),
                                            4096)
                    w = w.rearrange("p (c n) -> p c n", n=1024)
                    for jj in range(4):
                        j = 4 * q + jj
                        for t in range(4):
                            for h in range(2):
                                b = acc[t][h]
                                tk = mm(b.t[:, :], fT[:, j, t * 128:(t + 1) * 128], w[:, jj, h * 512:(h + 1) * 512],
                                        rd, fd, b.free, start=j == 0, stop=False, mark=(jj == 3))
                    ring.free(slot, tk)
                for t in range(4):
                    for h in range(2):
                        b = acc[t][h]
                        b.tok = mm(b.t[:, :], onesrow, row[0:1, h * 512:(h + 1) * 512], start=False, mark=True)
                finish = add_gated(both, gb, Zf[:, 0:1024].rearrange("p (c n) -> p c n", c=2), gd)
                for t in range(4):
                    for h in range(2):
                        b = acc[t][h]
                        b.done(finish(t, h, b.t[:, :], b.tok))

            def retention(l):
                top[0] = ctx_off
                barrier()
                hT, yT = area3(8, 512), area3(16, 256)
                mark_ = top[0]
                xs, junk = area3(4, 1024), area(1024)
                modulated(l, 1, both, hT, xs, junk)
                top[0] = mark_
                barrier()
                cs = area3(2, 256)
                Dc = area4(4, 2, 256)
                cr = area3(2, 256)
                ex = area3(1, 8)[:, 0, :]
                load("ret", cs, A["c_rope"], *[q.last() for q in (pe, dv, po)])
                load("ret", Dc, A["c_ret"])
                load("ret", cr, A["c_row"].broadcast_to([P, 512]).rearrange("p (a b) -> p a b", a=2))
                load("ret", ex[:, 0:4], A["c_col"])
                qk = area4(2, 2, 256)
                qr = area4(2, 2, 256)
                t1 = area4(2, 2, 256)
                kc = area3(2, 256)
                kfb = area4(2, 2, 256)
                v = area4(2, 2, 512)
                g = area3(2, 512)
                S = area4(2, 2, 512)
                MD = area3(2, 256)
                qd = t1
                rw = area3(2, 256)
                y = area3(2, 512)
                Pm = kc
                barrier(small["ret"])
                for h in range(4):
                    if h:
                        barrier()
                    lf, lb = lg[:, h:h + 1], lg[:, 4 + h:5 + h]
                    act(MD, Dc[:, 0], ACT.Exp, scale=lf)
                    e0 = act(y[:, :, 0:256], Dc[:, 1], ACT.Exp, scale=lb)
                    act(rw[:, 0, :], cr[:, 0, :], ACT.Exp, scale=lf)
                    act(rw[:, 1, :], cr[:, 1, :], ACT.Exp, scale=lb)
                    dc = st[:, 280:284]
                    act(dc[:, 0:2], ex[:, 0:2], ACT.Exp, scale=lf)
                    e1 = act(dc[:, 2:4], ex[:, 2:4], ACT.Exp, scale=lb)
                    tt(dv, MD, MD, Dc[:, 2], ALU.mult, e0)
                    tt(dv, y[:, :, 0:256], y[:, :, 0:256], Dc[:, 3], ALU.mult)
                    tt(dv, MD, MD, y[:, :, 0:256], ALU.add)
                    w, rd, slot = ring.load(A["ret_w_in_2"][3 * h], 4096)
                    w = w.rearrange("p (k n) -> p k n", k=8)
                    for a in range(2):
                        b = banks.get()
                        for m in range(2):
                            for k in range(8):
                                n0 = a * 256 + m * 128
                                tk = mm(b.t[:, m * 256:(m + 1) * 256], w[:, k, n0:n0 + 128], hT[:, k, 0:256], rd, b.free,
                                        start=k == 0, stop=k == 7, mark=(k == 7 and m == 1))
                        qe = evac(ac, qk[:, a], v256(b), tk, scale=None if a == 0 else 0.0625)
                        b.done(qe)
                    b = banks.get()
                    for t in range(2):
                        for k in range(8):
                            tk = mm(b.t[:, t * 256:(t + 1) * 256], hT[:, k, 256 + t * 128:384 + t * 128],
                                    w[:, k, 256:512], b.free, start=k == 0, stop=k == 7, mark=(k == 7 and t == 1))
                    ring.free(slot, tk)
                    ke = evac(ac, kc, v256(b), tk, scale=0.0625)
                    b.done(ke)
                    for i in range(2):
                        w, rd, slot = ring.load(A["ret_w_in_2"][3 * h + 1 + i], 4096)
                        w = w.rearrange("p (k n) -> p k n", k=8)
                        for t in (range(4) if i == 0 else range(2)):
                            b = banks.get()
                            for k in range(8):
                                tk = mm(b.t[:, :], hT[:, k, t * 128:(t + 1) * 128], w[:, k, :], rd, b.free,
                                        start=k == 0, stop=k == 7, mark=(k == 7))
                            if i == 0:
                                ve = cp(ac, v[:, t // 2, t % 2, :], b.t[:, :], tk)
                                b.done(ve)
                            else:
                                ge = act(g[:, t, :], b.t[:, :], ACT.Silu, tk)
                                b.done(ge)
                        ring.free(slot, tk)
                    for m in range(2):
                        ts(dv, kfb[:, 0, m, :], kc[:, m, :], dc[:, m:m + 1], None, ALU.mult, None, ke, e1)
                        kd = ts(dv, kfb[:, 1, m, :], kc[:, m, :], dc[:, 2 + m:3 + m], None, ALU.mult, None)
                    c2, s2 = bc(cs[:, 0, :], 2), bc(cs[:, 1, :], 2)
                    tt(dv, qr[:, :, 0, :], qk[:, :, 0, :], c2, ALU.mult, qe)
                    tt(dv, t1[:, :, 0, :], qk[:, :, 1, :], s2, ALU.mult)
                    tt(dv, qr[:, :, 0, :], qr[:, :, 0, :], t1[:, :, 0, :], ALU.subtract)
                    tt(dv, qr[:, :, 1, :], qk[:, :, 1, :], c2, ALU.mult)
                    tt(dv, t1[:, :, 0, :], qk[:, :, 0, :], s2, ALU.mult)
                    tt(dv, qr[:, :, 1, :], qr[:, :, 1, :], t1[:, :, 0, :], ALU.add)
                    for d in range(2):
                        qx = tt(dv, qd[:, d], qr[:, 0], bc(rw[:, d, :], 2), ALU.mult)
                    for d in range(2):
                        for m in range(2):
                            b = banks.get()
                            for t in range(2):
                                tk = mm(b.t[:, :], kfb[:, d, t, m * 128:(m + 1) * 128], v[:, 1, t, :], kd, ve, b.free,
                                        start=t == 0, stop=t == 1, mark=(t == 1))
                            se = cp(ac, S[:, d, m, :], b.t[:, :], tk)
                            b.done(se)
                    b = banks.get()
                    for tj in range(2):
                        for m in range(2):
                            tk = mm(b.t[:, tj * 256:(tj + 1) * 256], qr[:, 1, m, tj * 128:(tj + 1) * 128], qr[:, 0, m, :],
                                    qx, b.free, start=m == 0, stop=m == 1, mark=(m == 1 and tj == 1))
                    pm = tt(dv, Pm, v256(b), MD, ALU.mult, tk)
                    b.done(pm)
                    for t in range(2):
                        s = slice(t * 128, (t + 1) * 128)
                        b = banks.get()
                        for d in range(2):
                            for m in range(2):
                                mm(b.t[:, :], qd[:, d, m, s], S[:, d, m, :], se, b.free, start=(d == 0 and m == 0),
                                   stop=False)
                        for tj in range(2):
                            tk = mm(b.t[:, :], Pm[:, tj, s], v[:, 0, tj, :], pm, start=False, stop=tj == 1,
                                    mark=(tj == 1))
                        b.done(cp(dv, y[:, t, :], b.t[:, :], tk))
                    mu, va = st[:, 284:286], st[:, 286:288]
                    red(mu, y, ALU.add)
                    ts(dv, mu, mu, 1.0 / 512, None, ALU.mult, None)
                    for t in range(2):
                        e = ts(dv, y[:, t, :], y[:, t, :], mu[:, t:t + 1], None, ALU.subtract, None)
                    r = rstd([y[:, 0, :], y[:, 1, :]], va, 2, 512, 1e-6, S[:, 0, 0, :], e, tk)
                    for t in range(2):
                        e = stt(y[:, t, :], y[:, t, :], va[:, t:t + 1], g[:, t, :], ALU.mult, ALU.mult, r, ge)
                    for q in range(2):
                        b = banks.get()
                        for m in range(2):
                            for t in range(2):
                                c = 2 * q + m
                                tk = tr(b.t[:, (2 * m + t) * 128:(2 * m + t + 1) * 128], y[:, t, c * 128:(c + 1) * 128],
                                        e, b.free, mark=(m == 1 and t == 1))
                        yd = cp(ac, yT[:, 4 * h + 2 * q:4 * h + 2 * q + 2, :], v256(b), tk)
                        b.done(yd)
                barrier()
                gb = S.rearrange("p a b c -> p (a b) c")[:, 0:2, :].rearrange("p a c -> p (a c)").unsqueeze(1)
                gd = gate(l, 1, gb, v.rearrange("p a b c -> p (a b c)")[:, 0:1024].rearrange("p (c n) -> p c n", c=8),
                          1, 1.0)
                acc = [[banks.get() for _ in range(2)] for _ in range(2)]
                for q in range(4):
                    w, rd, slot = ring.load(A["ret_w_out_2"][0, q * 512:(q + 1) * 512, :].rearrange("(c p) n -> p c n", p=P),
                                            4096)
                    w = w.rearrange("p (c n) -> p c n", n=1024)
                    for jj in range(4):
                        j = 4 * q + jj
                        for T in range(2):
                            for hh in range(2):
                                b = acc[T][hh]
                                tk = b.tok = mm(b.t[:, :], yT[:, j, T * 128:(T + 1) * 128],
                                                w[:, jj, hh * 512:(hh + 1) * 512], rd, yd, b.free, start=j == 0,
                                                stop=j == 15, mark=(j == 15 or jj == 3))
                    ring.free(slot, tk)
                finish = add_gated(xa, gb, y, gd)
                for T in range(2):
                    for hh in range(2):
                        b = acc[T][hh]
                        b.done(finish(T, hh, b.t[:, :], b.tok))

            e = act(lg, lg, ACT.Abs)
            ts(dv, lg, lg, -1.0, None, ALU.mult, None, e)
            half_ffn(0, 0, 4)
            fourier(0)
            half_ffn(0, 2, 4)
            half_ffn(1, 0, 4)
            retention(1)
            half_ffn(1, 2, 2)
            top[0] = 0
            barrier()
            fg, junk = area(1024), area(1024)
            load("fg", fg, A["final_g_2"].unsqueeze(0).broadcast_to([P, 1024]), *[q.last() for q in (pe, dv, po)])
            r = rstd(xa, st[:, 0:2], 2, 1024, 1e-6, junk)
            for t in range(2):
                e = stt(xa[t], xa[t], st[:, t:t + 1], fg, ALU.mult, ALU.mult, r, small["fg"])
            sp.wait(e)
            sp.items.append((lambda e: e.dma_start(out.rearrange("o (t p) d -> p (o t) d", p=P), xt[:, :, :]), s_out))
            sp.items.append((s_out, 16))

        s_out = sem("s_out")
        FILL = 0
        for l in range(2):
            ffn1(l, 1)
            mixers(l)
            ffn1(l, 2)
        second()

        block = ctx.enter_context(nc.Block())

        @block.sync
        def _(eng):
            sp.emit(eng)

        @block.tensor
        def _(eng):
            pe.emit(eng)

        @block.scalar
        def _(eng):
            ac.emit(eng)

        @block.vector
        def _(eng):
            dv.emit(eng)

        @block.gpsimd
        def _(eng):
            po.emit(eng)


def constants():
    f = np.float32
    i = np.arange(128)
    a, b = np.meshgrid(i, i, indexing="ij")
    ch = a // 64 == b // 64

    def level(n):
        h = n // 2
        return ((a // n == b // n) & (a % n < h) & (b % n >= h)).astype(f)

    m = dict(ident=np.eye(128), tri=a <= b, ones=np.ones((128, 128)), negT=np.where(a <= b, 0, -1e30),
             neg=np.where(b <= a, 0, -1e30), bones=ch, l2=level(2).T, l2t=level(2), l4=level(4), l8=level(8),
             l16=level(16), l32=level(32), l64=level(64), i2=np.hstack([np.eye(128)[:, :64] + np.eye(128)[:, 64:]] * 2))
    c = {"c_msk": np.stack([np.asarray(m[n], f) for n in MASKS], 1)}
    strict, incl = (ch & (a < b)).astype(f), (ch & (a <= b)).astype(f)
    c["c_mask4"] = np.stack([strict, incl, strict, incl], 1)
    c["c_scan"] = np.broadcast_to((np.arange(256) % 64 != 0).astype(f), (128, 256)).copy()
    n = np.arange(256)
    ang = 2 * np.pi * ((n[:, None] * n[None, :]) % 256) / 256
    C, S = np.cos(ang), np.sin(ang)
    d1 = np.concatenate([C, S], 1).astype(f)
    d2 = (np.concatenate([C, -S], 1) / 256).astype(f)
    c["c_dft1"] = d1.reshape(2, 128, 512).transpose(1, 0, 2).copy()
    c["c_dft2"] = d2.reshape(2, 128, 512).transpose(1, 0, 2).copy()
    inv = (f(10000.0) ** (-np.arange(64, dtype=f) / f(64))).astype(f)
    row, colm = (n // 64).astype(f), (n % 64).astype(f)
    g = np.concatenate([row[:, None] * inv, colm[:, None] * inv], 1).astype(f)
    c["c_rope"] = np.stack([np.cos(g).T, np.sin(g).T], 1).astype(f)
    j = np.arange(256)
    dif = (j[None, :] - j[:, None])
    t = np.stack([np.maximum(dif, 0), np.maximum(-dif, 0), dif >= 0, dif <= 0]).astype(f)
    c["c_ret"] = t.reshape(4, 2, 128, 256).transpose(2, 0, 1, 3).copy()
    c["c_row"] = np.concatenate([j + 1, 256 - j]).astype(f)[None, :]
    p = np.arange(128)
    c["c_col"] = np.stack([255 - p, 127 - p, p, p + 128], 1).astype(f)
    return c


def layout(x):
    col = lambda a: np.ascontiguousarray(a).reshape(-1, 128).T
    d = {}

    def tiles(w, n):
        m = w.shape[1] // n
        return np.ascontiguousarray(w.reshape(8, 128, m, n).transpose(2, 1, 0, 3)).reshape(m, 128, 8 * n)

    def gate_up(g, u):
        w = np.stack([g.reshape(8, 128, 11, 256), u.reshape(8, 128, 11, 256)])
        return np.ascontiguousarray(w.transpose(3, 2, 1, 0, 4)).reshape(11, 128, 4096)

    for k in (1, 2):
        w = x[f"ffn{k}_w_gate_up"]
        d[f"ffn{k}_w_gate_up"] = np.stack([gate_up(w[l][:, :2816], w[l][:, 2816:]) for l in range(2)])
        d[f"ffn{k}_w_down"] = x[f"ffn{k}_w_down"]
    g, u = x["ffn_w_gate_2"], x["ffn_w_up_2"]
    d["ffn_gu_2"] = np.stack([np.stack([gate_up(g[l, j], u[l, j]) for j in range(2)]) for l in range(2)])
    d["ffn_w_down_2"] = x["ffn_w_down_2"]
    w = x["w_in"]
    t_cols = np.r_[3352:5144, 1024:2304, 2320:2832]
    n_cols = np.r_[0:1024, 2832:3344]
    s_cols = np.r_[2304:2320, 3344:3352]
    d["w_in_t"] = np.stack([tiles(w[l][:, t_cols], 256) for l in range(2)])
    d["w_in_n"] = np.stack([tiles(w[l][:, n_cols], 512) for l in range(2)])
    d["w_in_s"] = np.stack([tiles(w[l][:, s_cols], 24)[0] for l in range(2)])
    d["ada_w_2"] = np.stack([tiles(x["ada_w_2"][l], 512) for l in range(2)])
    w = x["ret_w_in_2"][0]
    q, k, v, gg = w[:, :1024], w[:, 1024:2048], w[:, 2048:4096], w[:, 4096:]
    cat = [a for h in range(4) for a in (q[:, h * 256:(h + 1) * 256], k[:, h * 256:(h + 1) * 256],
                                         v[:, h * 512:(h + 1) * 512], gg[:, h * 512:(h + 1) * 512])]
    d["ret_w_in_2"] = tiles(np.concatenate(cat, 1), 512)
    for n in ("x", "mlstm_wq", "mlstm_wk", "mlstm_wv", "rwkv_w_up", "rwkv_a_up", "rwkv_g_up", "w_out", "ctx_2",
              "final_norm", "final_g_2", "four_w_2", "four_b_2", "ret_w_out_2"):
        d[n] = x[n]
    cc = []
    for l in range(2):
        cw = np.concatenate([x["ssd_conv_w"][l], x["mlstm_conv_w"][l]], 1)
        cw = cw.reshape(4, 14, 128).transpose(2, 1, 0).reshape(128, 56)
        cb = np.concatenate([x["ssd_conv_b"][l], x["mlstm_conv_b"][l]])
        one = {"n1": x["ffn1_norm"][l], "nm": x["mix_norm"][l], "n2": x["ffn2_norm"][l], "cb": cb,
               "sn": x["ssd_norm"][l], "mn": x["mlstm_norm"][l], "mu": x["rwkv_shift_mu"][l], "w0": x["rwkv_w0"][l],
               "a0": x["rwkv_a0"][l], "kk": x["rwkv_k_k"][l], "ka": x["rwkv_k_a"][l],
               "rk": x["rwkv_r_k"][l], "lw": x["rwkv_ln_w"][l], "lb": x["rwkv_ln_b"][l]}
        cc += [cw if n == "cw" else col(one[n]) for n, _ in COLS1]
    cc += [col(x["norm_g_2"]), col(x["ada_b_2"])]
    two = np.stack([col(x["c_2"][0]), col(x["c_ctx_2"])], 2).reshape(128, 16)
    d["c_cols"] = np.ascontiguousarray(np.concatenate(cc + [two], 1))
    r = [x[n][l] for l in range(2) for n in ("ssd_dt_bias", "ssd_a_log", "ssd_d", "mlstm_gate_bias")]
    d["c_rows"] = np.concatenate(r + [x["ret_decay_2"].reshape(-1)])[None, :]
    d.update(constants())
    return d


def kernel(**inputs):
    import concourse.bacc as _bacc
    from concourse.bass_utils import run_bass_kernel_spmd as _run

    nc = _bacc.Bacc("TRN2", target_bir_lowering=False, num_devices=1)
    arrays, A = {}, {}
    for name, a in layout({k: np.asarray(v) for k, v in inputs.items()}).items():
        a = np.ascontiguousarray(a)
        arrays["in_" + name] = a
        A[name] = nc.dram_tensor("in_" + name, a.shape, mybir.dt.from_np(a.dtype), kind="ExternalInput").ap()
    out = nc.dram_tensor("out_0", (1, 256, 1024), F32, kind="ExternalOutput").ap()
    build(nc, A, out)
    r = _run(nc, [arrays], core_ids=[0])
    return r.results[0]["out_0"]
```

```python
from contextlib import ExitStack

import numpy as np

import concourse.bass as bass
from concourse import mybir

F32 = mybir.dt.float32
F32R = mybir.dt.float32r
ALU = mybir.AluOpType
ACT = mybir.ActivationFunctionType
AX = mybir.AxisListType.X
P = 128
NSLOT = 6
SLOT = 2048
DECAY = float(np.exp(-0.5))

COLS1 = [("n1", 8), ("nm", 8), ("n2", 8), ("cw", 56), ("cb", 14), ("sn", 8), ("mn", 4), ("mu", 14),
         ("w0", 4), ("a0", 4), ("kk", 4), ("ka", 4), ("rk", 4), ("lw", 4), ("lb", 4)]
NCOL1 = sum(n for _, n in COLS1)
NCOLS = 2 * NCOL1 + 2 * 24 + 2 * 72 + 16
MASKS = ["ident", "tri", "ones", "negT", "neg", "bones", "l2", "l2t", "l4", "l8", "l16", "l32", "l64", "i2"]


class Queue:

    def __init__(self, name, sem, chained):
        self.name, self.sem, self.chained = name, sem, chained
        self.items, self.n, self.seen, self.pending = [], 0, {}, []

    def wait(self, *tokens):
        for t in tokens:
            if t is None:
                continue
            if isinstance(t, list):
                self.wait(*t)
                continue
            sem, n, key = t
            if n > self.seen.get(key, 0):
                self.seen[key] = n
                self.items.append((sem, n))

    def __call__(self, fn, *after, mark=True):
        if self.pending:
            self.wait(*self.pending)
            self.pending = []
        self.wait(*after)
        if self.chained and self.n:
            self.wait((self.sem, self.n, self.name))
        if mark:
            self.n += 1
        self.items.append((fn, mark))
        return (self.sem, self.n, self.name) if mark else None

    def last(self):
        return (self.sem, self.n, self.name) if self.n else None

    def emit(self, eng):
        for a, b in self.items:
            if callable(a):
                ins = a(eng)
                if b is True:
                    ins.then_inc(self.sem, 1)
                elif b:
                    ins.then_inc(b, 16)
            else:
                eng.wait_ge(a, b)


class Bank:
    def __init__(self, t, i):
        self.t, self.i, self.free, self.busy = t, i, None, False

    def done(self, token):
        self.free, self.busy = token, False


class Banks:
    def __init__(self, tensors):
        self.banks = [Bank(t, i) for i, t in enumerate(tensors)]
        self.at = 0

    def get(self):
        b = self.banks[self.at % len(self.banks)]
        self.at += 1
        assert not b.busy
        b.busy = True
        return b


class Ring:

    def __init__(self, tensor, sems, sp):
        self.t, self.sems, self.sp = tensor, sems, sp
        self.at, self.count, self.owner = 0, [0] * NSLOT, [None] * NSLOT

    def load(self, src, width):
        i = self.at % NSLOT
        self.at += 1
        assert self.owner[i] != "busy"
        dst = self.t[:, i, 0:width]
        if len(src.shape) == 3:
            dst = dst.rearrange("p (c n) -> p c n", n=src.shape[2])
        self.sp.wait(self.owner[i])
        sem = self.sems[i]
        self.sp.items.append((lambda e: e.dma_start(dst, src, max_dma_last_dim=16384), sem))
        self.owner[i] = "busy"
        self.count[i] += 16
        return self.t[:, i, 0:width], (sem, self.count[i], f"ring{i}"), i

    def free(self, i, token):
        self.owner[i] = token


def build(nc, A, out):
    with ExitStack() as ctx:
        sbt = lambda name, shape: ctx.enter_context(nc.sbuf_tensor(name, shape, F32))
        sem = lambda name: ctx.enter_context(nc.semaphore(name))

        ring_t = sbt("ring", [P, NSLOT, SLOT])
        xt = sbt("xt", [P, 2, 1024])
        msk = sbt("msk", [P, len(MASKS), 128])
        mask4 = sbt("mask4", [P, 4, 128])
        scanm = sbt("scanm", [P, 256])
        cols = sbt("cols", [P, NCOLS])
        rows = sbt("rows", [P, 120])
        mods = sbt("mods", [P, 2, 72, 2])
        sil = sbt("sil", [P, 8, 2])
        st = sbt("st", [P, 512])
        acc = sbt("acc", [P, 2, 512])
        psums = [ctx.enter_context(nc.psum_tensor(f"ps{i}", [P, 512], F32)) for i in range(8)]

        pe = Queue("pe", sem("s_pe"), False)
        ac = Queue("ac", sem("s_ac"), True)
        dv = Queue("dv", sem("s_dv"), True)
        po = Queue("po", sem("s_po"), True)
        sp = Queue("sp", sem("s_sp"), False)
        ring = Ring(ring_t, [sem(f"s_ring{i}") for i in range(NSLOT)], sp)
        banks = Banks(psums)

        ident, tri, ones, negT, neg, bones, l2, l2t = (msk[:, i, :] for i in range(8))
        lvl = [msk[:, 8 + i, :] for i in range(5)]
        i2 = msk[:, 13, 0:64]
        onesrow = msk[0:1, 2, :]

        def mm(o, l, r, *after, start=True, stop=True, mark=False):
            return pe(lambda e: e.matmul(o, l, r, start=start, stop=stop, skip_group_check=True), *after, mark=mark)

        def tr(o, i, *after, mark=False):
            return pe(lambda e: e.transpose(o, i, ident), *after, mark=mark)

        def act(o, i, f, *after, **kw):
            return ac(lambda e: e.activation(o, i, f, **kw), *after)

        def tt(q, o, a, b, op, *after):
            return q(lambda e: e.tensor_tensor(o, a, b, op), *after)

        def ts(q, o, a, s1, s2, op0, op1, *after):
            if s2 is None:
                return q(lambda e: e.tensor_scalar(o, a, s1, None, op0), *after)
            return q(lambda e: e.tensor_scalar(o, a, s1, s2, op0, op1), *after)

        def stt(o, a, s, b, op0, op1, *after):
            return dv(lambda e: e.scalar_tensor_tensor(out=o, in0=a, scalar=s, in1=b, op0=op0, op1=op1), *after)

        def cp(q, o, a, *after):
            if q is ac:
                return act(o, a, ACT.Copy, *after)
            return q(lambda e: e.tensor_copy(o, a), *after)

        def red(o, a, op, *after):
            return dv(lambda e: e.tensor_reduce(o, a, AX, op), *after)

        def rcp(o, a, *after):
            return dv(lambda e: e.reciprocal(o, a), *after)

        def zero(o):
            return dv(lambda e: e.memset(o, 0.0))

        small = {}

        def load(name, dst, src, *after):
            s, n, _ = small.get(name) or (sem("s_" + name), 0, None)
            ac.wait(*ac.pending, *after)
            ac.pending = []
            ac.wait(ac.last())
            ac.items.append((lambda e: e.dma_start(dst, src), s))
            small[name] = (s, n + 16, "load_" + name)

        def barrier(*more):
            toks = [q.last() for q in (pe, ac, dv, po)] + list(more)
            for q in (pe, ac, dv, po):
                q.pending += [t for t in toks if t and t[2] != q.name]

        scopes = []
        names = [0]

        def enter():
            scopes.append(ExitStack())

        def leave():
            scopes.pop().close()

        def area(*shape, dt=F32):
            names[0] += 1
            t = scopes[-1].enter_context(nc.sbuf_tensor(f"a{names[0]}", [P, *shape], dt))
            return t[tuple(slice(None) for _ in range(len(shape) + 1))]

        area3 = area4 = area

        class Rot:

            def __init__(self, t):
                self.t, self.n, self.at, self.tok = t, t.shape[1], -1, [None] * t.shape[1]

            def get(self):
                self.at = (self.at + 1) % self.n
                return self.t[:, self.at, :], self.tok[self.at], self.at

            def put(self, i, token):
                self.tok[i] = token

        class Split:

            def __init__(self, *shape):
                self.h, self.l = area(*shape, dt=F32R), area(*shape, dt=F32R)

            def put(self, ix, src, *after):
                h, lo = self.h[ix], self.l[ix]
                a = act(h, src, ACT.Copy, *after)
                return tt(dv, lo, src, h.bitcast(F32), ALU.subtract, a, *after)

        class Weights:

            def __init__(self, srcs, bufs=2, first=1):
                self.srcs, self.n, self.bufs = srcs, 0, bufs
                self.b = [Split(2048) for _ in range(bufs)]
                self.freed = [None] * bufs
                self.ready = []
                for _ in range(first):
                    self.more()

            def more(self):
                if self.n < len(self.srcs):
                    src, width = self.srcs[self.n]
                    i = self.n % self.bufs
                    w, rd, slot = ring.load(src, width)
                    tk = self.b[i].put((slice(None), slice(0, width)), w, rd, self.freed[i])
                    ring.free(slot, tk)
                    self.ready.append(tk)
                    self.n += 1

            def get(self, k):
                while self.n < min(k + self.bufs, len(self.srcs)):
                    self.more()
                width = self.srcs[k][1]
                b = self.b[k % self.bufs]
                return b.h[:, 0:width], b.l[:, 0:width], self.ready[k]

            def free(self, k, token):
                self.freed[k % self.bufs] = token
                if self.bufs > 2:
                    self.more()

        def mm3(o, wh, wl, xh, xl, *after, start, stop, mark=False):
            mm(o, wh, xh, *after, start=start, stop=False)
            mm(o, wh, xl, start=False, stop=False)
            return mm(o, wl, xh, start=False, stop=stop, mark=mark)

        def col(l, name, i=0, n=1):
            at = l * NCOL1
            for nm, w in COLS1:
                if nm == name:
                    break
                at += w
            return cols[:, at + i:at + i + n]

        C2 = 2 * NCOL1
        ng2 = cols[:, C2:C2 + 48].rearrange("p (l j c) -> p l j c", l=2, j=3)
        ab2 = cols[:, C2 + 48:C2 + 192].rearrange("p (l c) -> p l c", l=2)
        cc2 = cols[:, C2 + 192:C2 + 208].rearrange("p (c v) -> p c v", v=2)

        load("const", msk[:, :, :], A["c_msk"])
        load("const", cols[:, :], A["c_cols"])
        load("const", rows[:, :], A["c_rows"].broadcast_to([P, 120]))
        load("x", xt[:, :, :], A["x"].rearrange("o (t p) d -> p (o t) d", p=P))
        load("const", mask4[:, :, :], A["c_mask4"])
        load("const", scanm[:, :], A["c_scan"])
        cst = dv(lambda e: e.memset(st[:, 500:501], -0.5))
        barrier(small["const"], small["x"])

        ac_sil = act(sil[:, :, :], cc2, ACT.Silu)

        def modulation():
            read = None
            for l in range(2):
                for t in range(18):
                    for h in range(2):
                        w, ready, slot = ring.load(A["ada_w_2"][l, t, h], 2048)
                        w = w.rearrange("p (k n) -> p k n", k=4)
                        for k in range(4):
                            for v in range(2):
                                s = sil[:, 4 * h + k, v:v + 1]
                                if h == 0 and k == 0:
                                    e = ts(dv, acc[:, v, :], w[:, k, :], s, None, ALU.mult, None, ready, read, ac_sil)
                                else:
                                    e = stt(acc[:, v, :], w[:, k, :], s, acc[:, v, :], ALU.mult, ALU.add, ready)
                            if k == 1:
                                yield
                        ring.free(slot, e)
                        yield
                    b = banks.get()
                    for i in range(4):
                        for v in range(2):
                            read = mm(b.t[:, 2 * i + v:2 * i + v + 1], acc[:, v, i * 128:(i + 1) * 128], ones[:, 0:1],
                                      e, b.free, mark=(i == 3 and v == 1))
                    bias = ab2[:, l, 4 * t:4 * t + 4].unsqueeze(2).broadcast_to([P, 4, 2])
                    b.done(tt(dv, mods[:, l, 4 * t:4 * t + 4, :],
                              b.t[:, 0:8].rearrange("p (a b) -> p a b", b=2), bias, ALU.add, read))
                    filled[0] = 18 * l + t + 1

        mod = modulation()
        filled, steps = [0], [0]

        def fill(n):
            for _ in range(n):
                steps[0] += 1
                if next(mod, 1):
                    return

        def fill_slot():
            if steps[0] % 2:
                fill(1)

        def fill_to(tiles):
            while filled[0] < tiles:
                fill(1)
            fill_slot()

        def power(o, v, n):
            return po(lambda e: e.tensor_tensor(o, v, st[:, 500:501].broadcast_to([P, n]), ALU.pow))

        def rstd(tiles, o, n, width, eps, junk, *after):
            for i, a in enumerate(tiles):
                t = ac(lambda e, a=a, i=i: e.activation(junk[:, 0:width], a, ACT.Square,
                                                       accum_out=o[:, i:i + 1]), *after)
            ts(po, o[:, 0:n], o[:, 0:n], 1.0 / width, eps, ALU.mult, ALU.add, t)
            return power(o[:, 0:n], o[:, 0:n], n)

        def norm_t(tiles, hs, hT, scale, bias, W):
            n = len(tiles)
            enter()
            xs = area(n, 1024)
            rot = Rot(area(3, 512))
            ready = []
            r = rstd(tiles, st[:, 0:n], n, 1024, 1e-6, xs[:, 0, :])
            done = [ts(dv, xs[:, i, :], tiles[i], st[:, i:i + 1], None, ALU.mult, None, r) for i in range(n)]
            if W:
                W.more()
            jobs = [(c, s) for c in range(8) for s in range(n // 2)]
            for j in range(0, len(jobs), 2):
                b = banks.get()
                for m, (c, s) in enumerate(jobs[j:j + 2]):
                    for t in range(2):
                        o = (2 * m + t) * 128
                        tk = tr(b.t[:, o:o + 128], xs[:, 2 * s + t, c * 128:(c + 1) * 128], done[2 * s + t], b.free,
                                mark=(m == 1 and t == 1))
                o, free, ri = rot.get()
                for m, (c, s) in enumerate(jobs[j:j + 2]):
                    sc, bi = scale(c, s), bias(c, s) if bias else None
                    i = b.t[:, m * 256:(m + 1) * 256]
                    if bi is None:
                        e = ts(dv, o[:, m * 256:(m + 1) * 256], i, sc, None, ALU.mult, None, tk, free)
                    else:
                        e = ts(dv, o[:, m * 256:(m + 1) * 256], i, sc, bi, ALU.mult, ALU.add, tk, free)
                b.done(e)
                c = jobs[j][0]
                if n == 2:
                    ix, src = (slice(None), slice(c, c + 2), slice(None)), o.rearrange("p (a b) -> p a b", b=256)
                else:
                    ix, src = (slice(None), c, slice(None)), o
                if hT is not None:
                    cp(ac, hT[:, c, :], o, e)
                d = hs.put(ix, src, e)
                rot.put(ri, d)
                ready += [d] * (2 if n == 2 else 1)
            leave()
            return ready

        def ffn(hs, ready, W, hf, rot, nt, parts, finish, rate=2):
            N = nt * 128
            tile, j0 = 0, 0
            last = dv.last()
            for count in parts:
                hfd = []
                for j in range(count):
                    wh, wl, rd = W.get(tile)
                    wh = wh.rearrange("p (k h n) -> p k h n", k=8, h=2)
                    wl = wl.rearrange("p (k h n) -> p k h n", k=8, h=2)
                    if nt == 2:
                        b1 = b2 = banks.get()
                        o1, o2 = b1.t[:, 0:256], b1.t[:, 256:512]
                    else:
                        b1, b2 = banks.get(), banks.get()
                        o1, o2 = b1.t[:, :], b2.t[:, :]
                    for h, (b, o) in enumerate(((b1, o1), (b2, o2))):
                        for k in range(8):
                            tk = mm3(o, wh[:, k, h, :], wl[:, k, h, :], hs.h[:, k, 0:N], hs.l[:, k, 0:N], rd, ready[k],
                                     b.free, start=k == 0, stop=k == 7, mark=(h == 1 and k == 7))
                    s, free, ri = rot.get()
                    s = s[:, 0:N]
                    a = act(s, o1, ACT.Silu, tk, free)
                    d = tt(dv, s, s, o2, ALU.mult, a, tk)
                    b1.done(d)
                    if b2 is not b1:
                        b2.done(d)
                    if tile % 3 < rate:
                        fill(1)
                    W.free(tile, tk)
                    tile += 1
                    hfd.append(hf.put((slice(None), j, slice(0, N)), s, d, last))
                    rot.put(ri, hfd[-1])
                out_b = [[banks.get() for _ in range(2)] for _ in range(nt)]
                for q in range(0, count, 2):
                    nj = min(2, count - q)
                    wh, wl, rd = W.get(tile)
                    wh = wh.rearrange("p (c n) -> p c n", n=1024)
                    wl = wl.rearrange("p (c n) -> p c n", n=1024)
                    for jj in range(nj):
                        j = q + jj
                        for t in range(nt):
                            ts_ = slice(t * 128, (t + 1) * 128)
                            for h in range(2):
                                b = out_b[t][h]
                                n_ = slice(h * 512, (h + 1) * 512)
                                b.tok = tk = mm3(b.t[:, :], hf.h[:, j, ts_], hf.l[:, j, ts_], wh[:, jj, n_],
                                                 wl[:, jj, n_], rd, hfd[j], b.free, start=j == 0, stop=j == count - 1,
                                                 mark=(j == count - 1 or (jj == nj - 1 and t == nt - 1 and h == 1)))
                    W.free(tile, tk)
                    tile += 1
                    if nt == 2 and tile % 2:
                        fill(1)
                for t in range(nt):
                    for h in range(2):
                        b = out_b[t][h]
                        b.done(finish(t, h, b.t[:, :], b.tok))
                last = tk
            assert tile == len(W.srcs)
            fill_slot()

        def ffn_weights(gu, down, parts, bufs):
            srcs, j = [], 0
            for count in parts:
                srcs += [(gu[j + i], 2048) for i in range(count)]
                srcs += [(down[(j + q) * 128:(j + q + min(2, count - q)) * 128, :].rearrange("(c p) n -> p c n", p=P),
                          min(2, count - q) * 1024) for q in range(0, count, 2)]
                j += count
            return Weights(srcs, bufs, 0)

        xa = [xt[:, t, :] for t in range(2)]

        def ffn1(l, which):
            enter()
            barrier()
            hs = Split(8, 256)
            rot = Rot(area(3, 256))
            W = ffn_weights(A[f"ffn{which}_w_gate_up"][l], A[f"ffn{which}_w_down"][l], [22], 3)
            nm = "n1" if which == 1 else "n2"
            ready = norm_t(xa, hs, None, lambda c, s: col(l, nm, c), None, W)
            hf = Split(22, 256)
            ffn(hs, ready, W, hf, rot, 2, [22],
                lambda t, h, p, tk: stt(xt[:, t, h * 512:(h + 1) * 512], p, 0.5, xt[:, t, h * 512:(h + 1) * 512],
                                        ALU.mult, ALU.add, tk))
            leave()

        def load_small(l, smallw, *after):
            sw = smallw[:, 0:1536].rearrange("p (w h e) -> p w h e", w=3, h=4)
            for i, nm in enumerate(("mlstm_wq", "mlstm_wk", "mlstm_wv")):
                load(f"sm{l}", sw[:, i], A[nm][l].rearrange("h d e -> d h e"), *after)
            load(f"sm{l}", smallw[0:64, 1536:2048], A["rwkv_w_up"][l])
            load(f"sm{l}", smallw[64:128, 1536:2048], A["rwkv_a_up"][l])
            load(f"sm{l}", smallw[:, 2048:2560], A["rwkv_g_up"][l])

        def evac(q, o, i, *after, scale=None):
            if q is ac:
                return act(o, i, ACT.Copy, *after, scale=1.0 if scale is None else scale)
            if scale is not None:
                return ts(q, o, i, scale, None, ALU.mult, None, *after)
            return cp(q, o, i, *after)

        def v256(b):
            return b.t[:, :].rearrange("p (a b) -> p a b", b=256)

        def v128(b):
            return b.t[:, :].rearrange("p (a b) -> p a b", b=128)

        def v64(b):
            return b.t[:, :].rearrange("p (a b) -> p a b", b=64)

        def bc(a, n):
            return a.unsqueeze(1).broadcast_to([a.shape[0], n, a.shape[1]])

        def bl(a, n):
            return a.unsqueeze(2).broadcast_to([a.shape[0], a.shape[1], n])

        def project_out(W, ys, yd, finish):
            ob = [[banks.get() for _ in range(2)] for _ in range(2)]
            for q in range(8):
                wh, wl, rd = W.get(q)
                wh = wh.rearrange("p (c n) -> p c n", n=1024)
                wl = wl.rearrange("p (c n) -> p c n", n=1024)
                for jj in range(2):
                    j = 2 * q + jj
                    for T in range(2):
                        c = slice(T * 128, (T + 1) * 128)
                        for h in range(2):
                            b = ob[T][h]
                            n_ = slice(h * 512, (h + 1) * 512)
                            tk = b.tok = mm3(b.t[:, :], ys.h[:, j, c], ys.l[:, j, c], wh[:, jj, n_], wl[:, jj, n_],
                                             rd, yd[j // 4], b.free, start=j == 0, stop=j == 15,
                                             mark=(j == 15 or jj == 1))
                W.free(q, tk)
            for T in range(2):
                for h in range(2):
                    b = ob[T][h]
                    b.done(finish(T, h, b.t[:, :], b.tok))

        def mixers(l):
            enter()
            barrier()
            yT = area(16, 256)
            enter()
            smallw = area(2560)
            load_small(l, smallw)
            hx = Split(8, 256)
            ready = norm_t(xa, hx, None, lambda c, s: col(l, "nm", c), None, None)
            sw = smallw[:, 0:1536].rearrange("p (w h e) -> p w h e", w=3, h=4)

            def pairs(first):
                return [(A["w_in_t"][l, first + q], 2048) for q in range(7)]

            def project_t(W, uT, pad):
                for q in range(7):
                    wh, wl, rd = W.get(q)
                    wh = wh.rearrange("p (k n) -> p k n", k=8)
                    wl = wl.rearrange("p (k n) -> p k n", k=8)
                    b = banks.get()
                    for m in range(2):
                        for k in range(8):
                            c = slice(m * 128, (m + 1) * 128)
                            tk = mm3(b.t[:, m * 256:(m + 1) * 256], wh[:, k, c], wl[:, k, c], hx.h[:, k, :],
                                     hx.l[:, k, :], rd, ready[k], b.free, start=k == 0, stop=k == 7,
                                     mark=(m == 1 and k == 7))
                    W.free(q, tk)
                    b.done(cp((ac, dv)[q % 2], uT[:, 2 * q:2 * q + 2, pad:pad + 256], v256(b), tk))
                    fill(1)

            enter()
            KR = area4(8, 2, 128)
            be, ch = area3(4, 256), area3(4, 256)
            KBV = area3(16, 128)
            bet, cht, vt = area3(2, 512), area3(2, 512), area3(2, 512)
            gl = area(256)
            Wc = area3(4, 4)
            enter()
            uT = area3(14, 257)
            enter()
            W = Weights(pairs(0))
            zero(uT[:, :, 0:1])
            project_t(W, uT, 1)
            leave()
            barrier(small[f"sm{l}"])
            us = area3(14, 256)
            ab = area3(4, 256)
            cwb = area3(4, 256)
            tm = [area3(4, 256) for _ in range(2)]
            uev = [ac.last(), dv.last()]
            tt(dv, us[:, :, :], uT[:, :, 0:256], uT[:, :, 1:257], ALU.subtract, uev)
            for i in range(14):
                stt(us[:, i, :], us[:, i, :], col(l, "mu", i), uT[:, i, 1:257], ALU.mult, ALU.add)
            r_, k_, v_ = us[:, 0:4, :], us[:, 4:8, :], us[:, 8:12, :]
            usd = dv.last()
            sgw = uT[:, 0:4, 1:257]
            act(us[0:64, 12, :], us[0:64, 12, :], ACT.Tanh, usd)
            th = act(gl, us[:, 13, :], ACT.Sigmoid)
            bw = [banks.get(), banks.get()]
            ba = [banks.get(), banks.get()]
            for c in range(4):
                o = slice((c % 2) * 256, (c % 2) * 256 + 256)
                cs = slice(1536 + c * 128, 1664 + c * 128)
                mm(bw[c // 2].t[:, o], smallw[0:64, cs], us[0:64, 12, :], th, bw[c // 2].free)
            for c in range(4):
                o = slice((c % 2) * 256, (c % 2) * 256 + 256)
                cs = slice(1536 + c * 128, 1664 + c * 128)
                tk = mm(ba[c // 2].t[:, o], smallw[64:128, cs], us[64:128, 12, :], ba[c // 2].free, mark=True)
            for c in range(4):
                o = slice((c % 2) * 256, (c % 2) * 256 + 256)
                e = act(sgw[:, c, :], bw[c // 2].t[:, o], ACT.Sigmoid, tk, bias=col(l, "w0", c))
                bw[c // 2].done(e)
            for c in range(4):
                o = slice((c % 2) * 256, (c % 2) * 256 + 256)
                e = act(ab[:, c, :], ba[c // 2].t[:, o], ACT.Sigmoid, tk, bias=col(l, "a0", c))
                ba[c // 2].done(e)
            sgd = e
            kk = tm[0]
            for c in range(4):
                ts(dv, kk[:, c, :], k_[:, c, :], col(l, "kk", c), None, ALU.mult, None)
            sq = act(tm[1], kk, ACT.Square, dv.last())
            bs = [banks.get(), banks.get()]
            for c in range(4):
                o = slice((c % 2) * 256, (c % 2) * 256 + 256)
                tk = mm(bs[c // 2].t[:, o], bones, tm[1][:, c, :], sq, bs[c // 2].free, mark=True)
            for i in range(2):
                e = act(tm[1][:, 2 * i:2 * i + 2, :], bs[i].t[:, :].rearrange("p (a b) -> p a b", b=256), ACT.Sqrt, tk)
                bs[i].done(e)
            ts(dv, tm[1], tm[1], 1e-6, None, ALU.max, None, e)
            rcp(tm[1], tm[1])
            tt(dv, kk, kk, tm[1], ALU.mult)
            for c in range(4):
                ts(dv, tm[1][:, c, :], ab[:, c, :], 1.0, col(l, "ka", c), ALU.subtract, ALU.mult, sgd)
            stt(k_, tm[1], 1.0, k_, ALU.add, ALU.mult)
            for c in range(4):
                stt(tm[1][:, c, :], r_[:, c, :], col(l, "rk", c), k_[:, c, :], ALU.mult, ALU.mult)
            bs = [banks.get(), banks.get()]
            t1 = dv.last()
            for c in range(4):
                o = slice((c % 2) * 256, (c % 2) * 256 + 256)
                tk = mm(bs[c // 2].t[:, o], bones, tm[1][:, c, :], t1, bs[c // 2].free, mark=True)
            for i in range(2):
                e = tt(dv, yT[:, 12 + 2 * i:14 + 2 * i, :], bs[i].t[:, :].rearrange("p (a b) -> p a b", b=256),
                       v_[:, 2 * i:2 * i + 2, :], ALU.mult, tk)
                bs[i].done(e)
            tt(dv, ab, kk, ab, ALU.mult)
            for c in range(4):
                dv(lambda e, o=cwb[:, c, :], i=sgw[:, c, :]: e.tensor_tensor_scan(o, scanm[:, :], i, 0.0,
                                                       ALU.mult, ALU.add))
            cw4 = cwb.rearrange("p c (a b) -> p (c a) b", b=64)
            cwd = dv.last()
            ww = tm[1]
            t8 = lambda a: a.rearrange("p c (t n) -> p (c t) n", n=128)
            w1 = act(ww, cwb, ACT.Exp, cwd, scale=-DECAY)
            d1 = tt(dv, KR[:, :, 1, :], t8(ww), t8(r_), ALU.mult, w1)
            d2 = tt(dv, sgw, cwb, sgw, ALU.subtract)
            w2 = act(ww, sgw, ACT.Exp, d1, d2, scale=-DECAY)
            d3 = tt(dv, KR[:, :, 0, :], t8(ww), t8(kk), ALU.mult, w2)
            w3 = act(ww, cwb, ACT.Exp, d3, scale=DECAY)
            tt(dv, be, ab, ww, ALU.mult, w3)
            tt(dv, ch, k_, ww, ALU.mult)
            w4 = act(Wc.rearrange("p c a -> p (c a)").unsqueeze(2), cw4[:, :, 63:64], ACT.Exp, scale=-DECAY)
            d4 = tt(dv, sgw2 := tm[0].rearrange("p c (a b) -> p (c a) b", b=64), cw4,
                    cw4[:, :, 63:64].broadcast_to([P, 16, 64]), ALU.subtract)
            w5 = act(tm[0], tm[0], ACT.Exp, d4, scale=DECAY)
            d5 = tt(dv, ab, ab, tm[0], ALU.mult, w5)
            d6 = tt(dv, k_, k_, tm[0], ALU.mult)
            for q, (src, dst) in enumerate(((lambda c, T: KR[:, 2 * c + T, 0, :], None),
                                            (lambda c, T: ab[:, c, T * 128:T * 128 + 128], bet),
                                            (lambda c, T: k_[:, c, T * 128:T * 128 + 128], cht),
                                            (lambda c, T: v_[:, c, T * 128:T * 128 + 128], vt))):
                for T in range(2):
                    b = banks.get()
                    for c in range(4):
                        tk = tr(b.t[:, c * 128:(c + 1) * 128], src(c, T), d6, b.free, mark=(c == 3))
                    o = KBV[:, T * 8:T * 8 + 8, 0:64] if dst is None else dst[:, T, :]
                    b.done(cp((ac, dv)[T], o, v64(b) if dst is None else b.t[:, :], tk))

            leave()
            enter()
            barrier()
            GH = area4(16, 2, 128)
            nT = area3(16, 128)
            nTT = area3(4, 256)
            MT = area4(2, 4, 64)
            enter()
            Tm, TT, X, CT = (area3(8, 128) for _ in range(4))
            yf = yT[:, 0:12, :].rearrange("p a b -> p (a b)")
            AB = yf[:, 0:2048].rearrange("p (u w n) -> p u w n", u=8, w=2)
            NN = yf[:, 2048:2816].rearrange("p (c h n) -> p c h n", c=3, h=4)
            for T in range(2):
                for h in range(8):
                    c, j = h // 2, h % 2
                    js = slice(64 * j, 64 * j + 64)
                    b = banks.get()
                    kr = KR[js, 2 * c + T, :, :].rearrange("p a b -> p (a b)")
                    mm(b.t[:, 0:256], be[js, c, T * 128:T * 128 + 128], kr, b.free)
                    tk = mm(b.t[:, 256:512], ch[js, c, T * 128:T * 128 + 128], kr, mark=True)
                    g4 = b.t[:, :].rearrange("p (a b n) -> p a b n", a=2, b=2)
                    m4 = mask4[:, :, :].rearrange("p (a b) n -> p a b n", b=2)
                    tt(dv, AB[:, 4 * j + c, :, :], g4[:, :, 0, :], m4[:, :, 0, :], ALU.mult, tk)
                    b.done(tt(dv, GH[:, T * 8 + h, :, :], g4[:, :, 1, :], m4[:, :, 1, :], ALU.mult))
                abd = dv.last()
                for j in range(2):
                    js = slice(64 * j, 64 * j + 64)
                    b = banks.get()
                    for c in range(4):
                        tk = mm(b.t[:, c * 128:(c + 1) * 128], KR[js, 2 * c + T, 0, :],
                                be[js, c, T * 128:T * 128 + 128], b.free, mark=(c == 3))
                    gs = slice(4 * j, 4 * j + 4)
                    b.done(tt(dv, Tm[:, gs, :], v128(b), bc(l2, 4), ALU.mult, tk))
                    tt(dv, Tm[:, gs, :], bc(ident, 4), Tm[:, gs, :], ALU.subtract)
                    tt(po, TT[:, gs, :], AB[:, gs, 0, :], bc(l2t, 4), ALU.mult, abd)
                    tt(po, TT[:, gs, :], bc(ident, 4), TT[:, gs, :], ALU.subtract)
                tdone = [[dv.last(), po.last()]] * 2
                xd = [None, None]
                cts = [tt(po, CT[:, 4 * j:4 * j + 4, :], AB[:, 4 * j:4 * j + 4, 0, :], bc(lvl[0], 4), ALU.mult, abd)
                       for j in range(2)]
                for L in range(5):
                    for j in range(2):
                        gs = slice(4 * j, 4 * j + 4)
                        b = banks.get()
                        for c in range(4):
                            u = 4 * j + c
                            tk = mm(b.t[:, c * 128:(c + 1) * 128], CT[:, u, :], Tm[:, u, :], cts[j], tdone[j], b.free,
                                    mark=(c == 3))
                        xd[j] = cp(ac, X[:, gs, :], v128(b), tk)
                        if L < 4:
                            cts[j] = tt(po, CT[:, gs, :], AB[:, gs, 0, :], bc(lvl[L + 1], 4), ALU.mult, tk)
                        b.done(xd[j])
                    for j in range(2):
                        gs = slice(4 * j, 4 * j + 4)
                        b2, b3 = banks.get(), banks.get()
                        for c in range(4):
                            u = 4 * j + c
                            tk = mm(b3.t[:, c * 128:(c + 1) * 128], X[:, u, :], TT[:, u, :], xd[j], b3.free,
                                    mark=(c == 3))
                        if L < 4:
                            for c in range(4):
                                u = 4 * j + c
                                tk = mm(b2.t[:, c * 128:(c + 1) * 128], TT[:, u, :], X[:, u, :], b2.free,
                                        mark=(c == 3))
                            b2.done(tt(dv, Tm[:, gs, :], Tm[:, gs, :], v128(b2), ALU.subtract, tk))
                        else:
                            b2.done(b2.free)
                        tdone[j] = tt(dv, TT[:, gs, :], TT[:, gs, :], v128(b3), ALU.subtract, tk)
                        b3.done(tdone[j])
                    fill(1)
                b = banks.get()
                for h in range(8):
                    c, j = h // 2, h % 2
                    tk = mm(b.t[:, h * 64:(h + 1) * 64], AB[:, 4 * j + c, 1, :], vt[:, T, h * 64:(h + 1) * 64],
                            b.free, mark=(h == 7))
                bv = cp(dv, KBV[:, T * 8:T * 8 + 8, 64:128], v64(b), tk)
                b.done(bv)
                for q in range(2):
                    b = banks.get()
                    for m in range(4):
                        h = 4 * q + m
                        c, j = h // 2, h % 2
                        tk = mm(b.t[:, m * 128:(m + 1) * 128], TT[:, 4 * j + c, :], KBV[:, T * 8 + h, :], bv, tdone,
                                b.free, mark=(m == 3))
                    nt_ = evac(ac, nT[:, T * 8 + 4 * q:T * 8 + 4 * q + 4, :], v128(b), tk, scale=-1.0)
                    b.done(nt_)
                b = banks.get()
                for h in range(8):
                    c, j = h // 2, h % 2
                    tk = mm(b.t[64 * j:64 * j + 64, c * 128:(c + 1) * 128], KBV[:, T * 8 + h, 0:64],
                            TT[:, 4 * j + c, :], b.free, mark=(h == 7))
                b.done(evac(ac, nTT[:, :, T * 128:T * 128 + 128], v128(b), tk, scale=-1.0))
                for i in range(2):
                    cc = 2 * T + i
                    if cc == 3:
                        continue
                    rs = slice(64 * i, 64 * i + 64)
                    b = banks.get()
                    for h in range(8):
                        c, j = h // 2, h % 2
                        hs = slice(h * 64, (h + 1) * 64)
                        os = slice(64 * j, 64 * j + 64)
                        mm(b.t[os, c * 128:c * 128 + 64], nT[rs, T * 8 + h, 0:64], bet[rs, T, hs], nt_, b.free)
                        mm(b.t[os, c * 128 + 64:c * 128 + 128], cht[rs, T, hs], vt[rs, T, hs], start=True, stop=False)
                        tk = mm(b.t[os, c * 128 + 64:c * 128 + 128], bet[rs, T, hs], nT[rs, T * 8 + h, 64:128],
                                start=False, stop=True, mark=(h == 7))
                    if cc:
                        for c in range(4):
                            stt(MT[:, cc - 1, c, :], i2, Wc[:, c, cc:cc + 1], b.t[:, c * 128:c * 128 + 64],
                                ALU.mult, ALU.add, tk)
                    b.done(cp(dv, NN[:, cc, :, :], v128(b)[:, :, 64:128], tk))

            leave()
            barrier()
            S = area4(4, 4, 64)
            SA = area3(16, 64)
            Yb = area3(16, 64)
            Yc = area3(16, 64)
            zero(S[:, 0, :, :])
            sd = cp(dv, S[:, 1, :, :], NN[:, 0, :, :])
            for cc in (1, 2):
                bj = [banks.get(), banks.get()]
                for j in range(2):
                    js = slice(64 * j, 64 * j + 64)
                    for c in range(4):
                        tk = mm(bj[j].t[js, c * 64:(c + 1) * 64], MT[js, cc - 1, c, :], S[js, cc, c, :], sd,
                                bj[j].free, mark=(c == 3))
                for j in range(2):
                    js = slice(64 * j, 64 * j + 64)
                    sd = tt(dv, S[js, cc + 1, :, :], v64(bj[j])[js, 0:4, :], NN[js, cc, :, :], ALU.add, tk)
                    bj[j].done(sd)
            bj = [banks.get(), banks.get()]
            for j in range(2):
                js = slice(64 * j, 64 * j + 64)
                for cc in range(4):
                    for c in range(4):
                        T, i = cc // 2, cc % 2
                        tk = mm(bj[j].t[64 * i:64 * i + 64, (T * 4 + c) * 64:(T * 4 + c + 1) * 64],
                                nTT[js, c, cc * 64:cc * 64 + 64], S[js, cc, c, :], sd, bj[j].free,
                                mark=(cc == 3 and c == 3))
            SAj = SA.rearrange("p (a j) n -> p a j n", j=2)
            nTj = nT.rearrange("p (a j) n -> p a j n", j=2)
            Ybj = Yb.rearrange("p (a j) n -> p a j n", j=2)
            for j in range(2):
                sad = tt(dv, SAj[:, :, j, :], v64(bj[j]), nTj[:, :, j, 64:128], ALU.add, tk)
                bj[j].done(sad)
            for j in range(2):
                js = slice(64 * j, 64 * j + 64)
                b = banks.get()
                for T in range(2):
                    for c in range(4):
                        u = T * 8 + 2 * c + j
                        rg = slice((T * 4 + c) * 64, (T * 4 + c + 1) * 64)
                        mm(b.t[:, rg], GH[:, u, 0, :], SA[:, u, :], sad, b.free, start=True, stop=False)
                        mm(b.t[:, rg], GH[:, u, 1, :], vt[:, T, (2 * c + j) * 64:(2 * c + j + 1) * 64],
                           start=False, stop=False)
                        for i in range(2):
                            tk = mm(b.t[64 * i:64 * i + 64, rg], KR[js, 2 * c + T, 1, 64 * i:64 * i + 64],
                                    S[js, 2 * T + i, c, :], start=False, stop=True,
                                    mark=(T == 1 and c == 3 and i == 1))
                b.done(cp(dv, Ybj[:, :, j, :], v64(b), tk))
            mu = st[:, 16:32]
            va = st[:, 32:48]
            red(mu, Yb, ALU.add)
            ts(dv, mu, mu, 1.0 / 64, None, ALU.mult, None)
            yc = tt(dv, Yc, Yb, bl(mu, 64), ALU.subtract)
            s2 = act(Yb, Yc, ACT.Square, yc)
            r2 = red(va, Yb, ALU.add, s2)
            ts(po, va, va, 1.0 / 64, 64e-5, ALU.mult, ALU.add, r2)
            pw = power(va, va, 16)
            yn = tt(dv, Yc, Yc, bl(va, 64), ALU.mult, pw)
            Ycf = Yc.rearrange("p (t h) n -> p t (h n)", t=2)
            for q in range(2):
                b, bg = banks.get(), banks.get()
                for m in range(2):
                    c = 2 * q + m
                    for T in range(2):
                        tr(b.t[:, (2 * m + T) * 128:(2 * m + T + 1) * 128], Ycf[:, T, c * 128:(c + 1) * 128], yn, b.free)
                for m in range(2):
                    c = 2 * q + m
                    tk = mm(bg.t[:, m * 256:(m + 1) * 256], smallw[:, 2048 + c * 128:2176 + c * 128], gl, bg.free,
                            mark=True)
                tmp = Yb.rearrange("p a b -> p (a b)")[:, 0:512].rearrange("p (a b) -> p a b", b=256)
                for m in range(2):
                    c = 2 * q + m
                    ts(dv, tmp[:, m, :], b.t[:, m * 256:(m + 1) * 256], col(l, "lw", c), col(l, "lb", c),
                       ALU.mult, ALU.add, tk)
                ys = yT[:, 12 + 2 * q:14 + 2 * q, :]
                b.done(tt(dv, ys, tmp, ys, ALU.add))
                bg.done(tt(dv, ys, ys, v256(bg), ALU.mult))

            leave()
            leave()
            barrier()
            uT = area3(14, 259)
            zt = area3(2, 1024)
            ot = area3(2, 512)
            dg = area3(2, 24)
            enter()
            zero(uT[:, :, 0:3])
            W = Weights(pairs(7) + [(A["w_in_n"][l, q, kh], 2048) for q in range(3) for kh in range(2)]
                        + [(A["w_in_s"][l], 192)])
            project_t(W, uT, 3)
            cvd = [ac.last(), dv.last()]
            for q in range(3):
                bb = [banks.get(), banks.get()]
                for kh in range(2):
                    i = 7 + 2 * q + kh
                    wh, wl, rd = W.get(i)
                    wh = wh.rearrange("p (k n) -> p k n", k=4)
                    wl = wl.rearrange("p (k n) -> p k n", k=4)
                    for T in range(2):
                        for k in range(4):
                            kk_ = 4 * kh + k
                            c = slice(T * 128, (T + 1) * 128)
                            tk = mm3(bb[T].t[:, :], hx.h[:, kk_, c], hx.l[:, kk_, c], wh[:, k, :], wl[:, k, :], rd,
                                     bb[T].free, start=kk_ == 0, stop=kk_ == 7, mark=(k == 3))
                    W.free(i, tk)
                for T in range(2):
                    if q < 2:
                        e = act(zt[:, T, q * 512:(q + 1) * 512], bb[T].t[:, :], ACT.Silu, tk)
                    else:
                        e = act(ot[:, T, :], bb[T].t[:, :], ACT.Sigmoid, tk)
                    bb[T].done(e)
            wh, wl, rd = W.get(13)
            wh = wh.rearrange("p (k n) -> p k n", k=8)
            wl = wl.rearrange("p (k n) -> p k n", k=8)
            for T in range(2):
                b = banks.get()
                c = slice(T * 128, (T + 1) * 128)
                for k in range(8):
                    tk = mm3(b.t[:, 0:24], hx.h[:, k, c], hx.l[:, k, c], wh[:, k, :], wl[:, k, :], rd, b.free,
                             start=k == 0, stop=k == 7, mark=(k == 7))
                b.done(cp(ac, dg[:, T, :], b.t[:, 0:24], tk))
            leave()
            barrier()
            xc = area3(14, 256)
            enter()
            for c in range(14):
                ts(dv, xc[:, c, :], uT[:, c, 0:256], col(l, "cw", 4 * c), None, ALU.mult, None, cvd)
                for k in range(1, 4):
                    stt(xc[:, c, :], uT[:, c, k:k + 256], col(l, "cw", 4 * c + k), xc[:, c, :], ALU.mult, ALU.add)
            cd = dv.last()
            for c in range(14):
                xcd = act(xc[:, c, :], xc[:, c, :], ACT.Silu, cd, bias=col(l, "cb", c))

            def softplus(o, x, n, *after):
                t = st[:, 440:440 + n]
                a = act(t, x, ACT.Abs, dv.last(), *after)
                a = act(t, t, ACT.Exp, scale=-1.0)
                a = act(t, t, ACT.Ln, a, bias=1.0)
                return stt(o, x, 0.0, t, ALU.max, ALU.add, a)

            R0 = 56 * l
            Xt = area3(2, 1024)
            xd_ = area3(2, 1024)
            xw = area(1024)
            Bt = area(128)
            Ss = area(512)
            cb = area4(2, 2, 128)
            Ms = [area3(4, 128) for _ in range(3)]
            yy = area3(2, 1024)
            dt = st[:, 64:96].rearrange("p (t h) -> p t h", t=2)
            ad = st[:, 96:128].rearrange("p (t h) -> p t h", t=2)
            acu = st[:, 128:160].rearrange("p (t h) -> p t h", t=2)
            nac = st[:, 160:192].rearrange("p (t h) -> p t h", t=2)
            en = st[:, 192:208]
            wd = st[:, 208:224]
            xa1 = st[:, 224:240]
            nA = st[:, 240:256]
            gm = st[:, 256:264]
            w = act(nA, rows[:, R0 + 16:R0 + 32], ACT.Exp, cd)
            ts(dv, nA, nA, -1.0, None, ALU.mult, None, w)
            tt(dv, dt, dg[:, :, 0:16], bc(rows[:, R0:R0 + 16], 2), ALU.add, ac.last())
            softplus(st[:, 64:96], st[:, 64:96], 32)
            a_ = tt(dv, ad, dt, bc(nA, 2), ALU.mult)
            b = banks.get()
            for T in range(2):
                mm(b.t[:, T * 16:T * 16 + 16], tri, ad[:, T, :], a_, b.free)
            tk = mm(b.t[:, 32:48], ones, ad[:, 0, :], mark=True)
            cp(dv, st[:, 128:160], b.t[:, 0:32], tk)
            ts(dv, st[:, 160:192], b.t[:, 0:32], -1.0, None, ALU.mult, None)
            e = tt(dv, en, b.t[:, 32:48], acu[:, 0, :], ALU.subtract)
            b.done(e)
            w = act(wd, en, ACT.Exp, e)
            w = act(xa1, acu[:, 1, :], ACT.Exp)
            for T in range(2):
                for q in range(2):
                    b = banks.get()
                    for c in range(4):
                        tk = tr(b.t[:, c * 128:(c + 1) * 128], xc[:, 4 * q + c, T * 128:(T + 1) * 128], xcd, b.free,
                                mark=(c == 3))
                    b.done(cp(ac, Xt[:, T, q * 512:(q + 1) * 512], b.t[:, :], tk))
            b = banks.get()
            tk = tr(b.t[:, 0:128], xc[:, 8, 0:128], b.free, mark=True)
            b.done(cp(ac, Bt, b.t[:, 0:128], tk))
            xd = ac.last()
            h64 = lambda a: a.rearrange("p (h n) -> p h n", n=64)
            for T in range(2):
                tt(dv, h64(xd_[:, T, :]), h64(Xt[:, T, :]), bl(dt[:, T, :], 64), ALU.mult, xd)
            xwd = tt(dv, h64(xw), h64(xd_[:, 0, :]), bl(wd, 64), ALU.mult)
            bg = [banks.get(), banks.get()]
            for g in range(2):
                for T in range(2):
                    s = slice(T * 128, (T + 1) * 128)
                    tk = mm(bg[g].t[:, s], xc[64 * g:64 * g + 64, 8, s], xc[64 * g:64 * g + 64, 9, s], xcd,
                            bg[g].free, mark=(T == 1))
            for g in range(2):
                bg[g].done(cp(ac, cb[:, g, :, :], bg[g].t[:, 0:256].rearrange("p (a b) -> p a b", b=128), tk))
            b = banks.get()
            for g in range(2):
                tk = mm(b.t[64 * g:64 * g + 64, :], Bt[:, 64 * g:64 * g + 64], xw[:, g * 512:(g + 1) * 512], xwd, xd,
                        b.free, mark=(g == 1))
            ssd = cp(ac, Ss, b.t[:, :], tk)
            b.done(ssd)
            n = 0
            hold = [None] * 3
            for T in range(2):
                for g in range(2):
                    by = banks.get()
                    for q in range(2):
                        b = banks.get()
                        for m in range(4):
                            h = 8 * g + 4 * q + m
                            tk = mm(b.t[:, m * 128:(m + 1) * 128], ad[:, T, h:h + 1].broadcast_to([P, 128]), tri,
                                    b.free, mark=(m == 3))
                        M = Ms[n % 3]
                        for m in range(4):
                            h = 8 * g + 4 * q + m
                            e = stt(M[:, m, :], b.t[:, m * 128:(m + 1) * 128], nac[:, T, h:h + 1], negT, ALU.add,
                                    ALU.add, tk, hold[n % 3])
                        b.done(e)
                        x = act(M, M, ACT.Exp, e)
                        e = tt(dv, M, M, bc(cb[:, g, T, :], 4), ALU.mult, x)
                        for m in range(4):
                            h = 8 * g + 4 * q + m
                            hold[n % 3] = tk = mm(by.t[:, (4 * q + m) * 64:(4 * q + m + 1) * 64], M[:, m, :],
                                                  xd_[:, T, h * 64:(h + 1) * 64], e, by.free, mark=(m == 3))
                        n += 1
                    ys = yy[:, T, g * 512:(g + 1) * 512]
                    by.done(cp(dv, ys, by.t[:, :], tk))
                    fill(1)
                    if T == 1:
                        b = banks.get()
                        tk = mm(b.t[:, :], xc[64 * g:64 * g + 64, 9, 128:256], Ss[64 * g:64 * g + 64, :], ssd, b.free,
                                mark=True)
                        tmp = xw[:, g * 512:(g + 1) * 512]
                        e = tt(dv, h64(tmp), v64(b), bl(xa1[:, 8 * g:8 * g + 8], 64), ALU.mult, tk)
                        b.done(e)
                        tt(dv, ys, ys, tmp, ALU.add)
            for T in range(2):
                tt(dv, h64(Xt[:, T, :]), h64(Xt[:, T, :]), bl(rows[:, R0 + 32:R0 + 48], 64), ALU.mult)
                tt(dv, yy[:, T, :], yy[:, T, :], Xt[:, T, :], ALU.add)
                e = tt(dv, yy[:, T, :], yy[:, T, :], zt[:, T, :], ALU.mult)
            tiles = [yy[:, T, g * 512:(g + 1) * 512] for T in range(2) for g in range(2)]
            r = rstd(tiles, gm, 4, 512, 1e-6, Xt[:, 0, :], e)
            for i, a in enumerate(tiles):
                e = ts(dv, a, a, gm[:, i:i + 1], None, ALU.mult, None, r)

            def back(src, first, count, name, *after):
                for c in range(0, count, 2):
                    b = banks.get()
                    for m in range(2):
                        for T in range(2):
                            tk = tr(b.t[:, (2 * m + T) * 128:(2 * m + T + 1) * 128],
                                    src[:, T, (c + m) * 128:(c + m + 1) * 128], b.free, *after, mark=(m == 1 and T == 1))
                    for m in range(2):
                        e = ts(dv, yT[:, first + c + m, :], b.t[:, m * 256:(m + 1) * 256], col(l, name, c + m), None,
                               ALU.mult, None, tk)
                    b.done(e)

            back(yy, 0, 8, "sn", e)

            leave()
            barrier()
            qT, kT = area3(4, 256), area3(4, 256)
            kt, vt, vw = area3(4, 128), area4(2, 4, 128), area3(4, 128)
            Dm = [area3(4, 128) for _ in range(2)]
            PT = [area3(4, 128) for _ in range(2)]
            Cs = area3(4, 128)
            nv = area(4)
            hh = area3(2, 512)
            s4 = lambda i: st[:, 64 + 8 * i:72 + 8 * i].rearrange("p (t h) -> p t h", t=2)
            li, lf, bcu, mi, il, mt, wi, em, den = (s4(i) for i in range(9))
            nl = st[:, 136:144].rearrange("p (t h) -> p t h", t=2)
            g8 = st[:, 144:160].rearrange("p (t h) -> p t h", t=2)
            bend, mpv, wend, t4 = (st[:, 160 + 4 * i:164 + 4 * i] for i in range(4))
            nmt = st[:, 176:184].rearrange("p (t h) -> p t h", t=2)
            gm = st[:, 184:192]
            xm = uT[:, 10:14, 3:259]
            xcc = xc[:, 10:14, :]
            sc = 128 ** -0.5
            for i, (o, scale) in enumerate(((qT, None), (kT, sc))):
                for q in range(2):
                    b = banks.get()
                    for m in range(2):
                        tk = mm(b.t[:, m * 256:(m + 1) * 256], sw[:, i, 2 * q + m, :], xcc[:, 2 * q + m, :], b.free,
                                mark=(m == 1))
                    b.done(evac(ac, o[:, 2 * q:2 * q + 2, :], v256(b), tk, scale=scale))
            b = banks.get()
            for h in range(4):
                tk = mm(b.t[:, h * 128:(h + 1) * 128], xcc[:, h, 0:128], sw[:, 1, h, :], b.free, mark=(h == 3))
            b.done(evac(ac, kt, v128(b), tk, scale=sc))
            for T in range(2):
                b = banks.get()
                for h in range(4):
                    tk = mm(b.t[:, h * 128:(h + 1) * 128], xm[:, h, T * 128:(T + 1) * 128], sw[:, 2, h, :], b.free,
                            mark=(h == 3))
                b.done(cp(ac, vt[:, T, :, :], v128(b), tk))
            projd = ac.last()
            tt(dv, g8, dg[:, :, 16:24], bc(rows[:, R0 + 48:R0 + 56], 2), ALU.add)
            cp(dv, li, g8[:, :, 0:4])
            ts(dv, lf, g8[:, :, 4:8], -1.0, None, ALU.mult, None)
            lff = st[:, 72:80]
            softplus(lff, lff, 8)
            cp(dv, nl, lf)
            ld = ts(dv, lff, lff, -1.0, None, ALU.mult, None)
            b = banks.get()
            for T in range(2):
                mm(b.t[:, 4 * T:4 * T + 4], tri, lf[:, T, :], ld, b.free)
            tk = mm(b.t[:, 8:12], ones, lf[:, 0, :], mark=True)
            cp(dv, st[:, 80:88], b.t[:, 0:8], tk)
            e = cp(dv, bend, b.t[:, 8:12])
            b.done(e)
            be_ = []
            for T in range(2):
                b = banks.get()
                for h in range(4):
                    hs = slice(h * 128, (h + 1) * 128)
                    mm(b.t[:, hs], nl[:, T, h:h + 1].broadcast_to([P, 128]), tri, b.free, stop=False)
                    tk = mm(b.t[:, hs], li[:, T, h:h + 1].broadcast_to([P, 128]), ident, start=False, mark=(h == 3))
                if T == 0:
                    red(t4, v128(b), ALU.max, tk)
                    tt(dv, t4, t4, bend, ALU.add)
                    tt(dv, mpv, bend, t4, ALU.max)
                    tt(dv, wend, li[:, 0, :], bcu[:, 0, :], ALU.subtract)
                    tt(dv, wend, wend, bend, ALU.add)
                    e = tt(dv, wend, wend, mpv, ALU.subtract)
                    we = act(wend, wend, ACT.Exp, e)
                for h in range(4):
                    e = stt(Dm[T][:, h, :], b.t[:, h * 128:(h + 1) * 128], bcu[:, T, h:h + 1], neg, ALU.add, ALU.add, tk)
                b.done(e)
                red(mi[:, T, :], Dm[T], ALU.max)
            cp(dv, il[:, 0, :], bcu[:, 0, :])
            tt(dv, il[:, 1, :], bcu[:, 1, :], mpv, ALU.add)
            tt(dv, st[:, 104:112], st[:, 96:104], st[:, 88:96], ALU.max)
            tt(dv, st[:, 112:120], st[:, 96:104], st[:, 104:112], ALU.subtract)
            e = ts(dv, st[:, 176:184], st[:, 104:112], -1.0, None, ALU.mult, None)
            act(st[:, 112:120], st[:, 112:120], ACT.Exp, e)
            act(st[:, 120:128], st[:, 176:184], ACT.Exp)
            for T in range(2):
                for h in range(4):
                    wx = act(Dm[T][:, h, :], Dm[T][:, h, :], ACT.Exp, bias=nmt[:, T, h:h + 1])
            vwd = tt(dv, vw, vt[:, 0, :, :], bl(wend, 128), ALU.mult, we, projd)
            b = banks.get()
            for h in range(4):
                tk = mm(b.t[:, h * 128:(h + 1) * 128], kt[:, h, :], vw[:, h, :], vwd, projd, b.free, mark=(h == 3))
            csd = cp(ac, Cs, v128(b), tk)
            b.done(csd)
            b = banks.get()
            for h in range(4):
                tk = mm(b.t[:, h:h + 1], kt[:, h, :], wend[:, h:h + 1], b.free, mark=(h == 3))
            csd = cp(ac, nv, b.t[:, 0:4], tk)
            b.done(csd)
            for T in range(2):
                b = banks.get()
                for h in range(4):
                    s = slice(T * 128, (T + 1) * 128)
                    tk = mm(b.t[:, h * 128:(h + 1) * 128], qT[:, h, s], kT[:, h, s], projd, b.free, mark=(h == 3))
                e = tt(dv, Dm[T], v128(b), Dm[T], ALU.mult, tk, wx)
                b.done(e)
                red(den[:, T, :], Dm[T], ALU.add)
                b = banks.get()
                for h in range(4):
                    tk = tr(b.t[:, h * 128:(h + 1) * 128], Dm[T][:, h, :], e, b.free, mark=(h == 3))
                pt = cp(ac, PT[T], v128(b), tk)
                b.done(pt)
                b = banks.get()
                for h in range(4):
                    tk = mm(b.t[:, h * 128:(h + 1) * 128], PT[T][:, h, :], vt[:, T, h, :], pt, b.free, mark=(h == 3))
                h4 = hh[:, T, :].rearrange("p (h n) -> p h n", h=4)
                b.done(cp(dv, h4, v128(b), tk))
                if T == 1:
                    b, b2 = banks.get(), banks.get()
                    for h in range(4):
                        mm(b.t[:, h * 128:(h + 1) * 128], qT[:, h, 128:256], Cs[:, h, :], csd, b.free)
                    for h in range(4):
                        tk = mm(b2.t[:, h:h + 1], qT[:, h, 128:256], nv[:, h:h + 1], b2.free, mark=(h == 3))
                    e = tt(dv, vw, v128(b), bl(wi[:, 1, :], 128), ALU.mult, tk)
                    b.done(e)
                    tt(dv, h4, h4, vw, ALU.add)
                    e = tt(dv, t4, b2.t[:, 0:4], wi[:, 1, :], ALU.mult)
                    b2.done(e)
                    tt(dv, den[:, 1, :], den[:, 1, :], t4, ALU.add)
            dn = st[:, 128:136]
            e = act(dn, dn, ACT.Abs, dv.last())
            tt(dv, dn, dn, st[:, 120:128], ALU.max, e)
            rcp(dn, dn)
            for T in range(2):
                h4 = hh[:, T, :].rearrange("p (h n) -> p h n", h=4)
                tt(dv, h4, h4, bl(den[:, T, :], 128), ALU.mult)
                e = tt(dv, hh[:, T, :], hh[:, T, :], ot[:, T, :], ALU.mult)
            tiles = [hh[:, T, h * 128:(h + 1) * 128] for T in range(2) for h in range(4)]
            r = rstd(tiles, gm, 8, 128, 1e-6, Dm[0][:, 0, :], e)
            for i, a in enumerate(tiles):
                e = ts(dv, a, a, gm[:, i:i + 1], None, ALU.mult, None, r)
            back(hh, 8, 4, "mn", e)
            yd = [dv.last(), ac.last()]
            leave()
            enter()
            barrier()
            W = Weights([(A["w_out"][l, q * 256:(q + 1) * 256, :].rearrange("(c p) n -> p c n", p=P), 2048)
                         for q in range(8)])
            ys = Split(16, 256)
            yd = [ys.put((slice(None), slice(4 * q, 4 * q + 4), slice(None)), yT[:, 4 * q:4 * q + 4, :])
                  for q in range(4)]
            project_out(W, ys, yd, lambda t, h, p, tk: tt(dv, xt[:, t, h * 512:(h + 1) * 512], p,
                                                          xt[:, t, h * 512:(h + 1) * 512], ALU.add, tk))
            leave()
            leave()

        def second():
            lg = rows[:, 112:120]
            ctx_off = 2048

            def gate(l, j, gb, dg, n, half):
                for v in range(n):
                    for c in range(8):
                        e = ts(dv, dg[:, c, :], ident, mods[:, l, 8 * (3 * j + 2) + c, v:v + 1], half, ALU.mult, ALU.mult)
                    for q in range(2):
                        b = banks.get()
                        for m in range(4):
                            tk = mm(b.t[:, m * 128:(m + 1) * 128], ones, dg[:, 4 * q + m, :], e, b.free, mark=(m == 3))
                        t = cp(ac, gb[:, v, q * 512:(q + 1) * 512], b.t[:, :], tk)
                        b.done(t)
                        dv.wait(tk)
                return t

            def modulated(l, j, tiles, hs, W):
                sct = st[:, 256:272].rearrange("p (c v) -> p c v", v=2)
                s = 8 * (3 * j + 1)
                stt(sct, mods[:, l, s:s + 8, :], 1.0, bl(ng2[:, l, j, :], 2), ALU.add, ALU.mult)
                return norm_t(tiles, hs, None, lambda c, v: sct[:, c, v:v + 1],
                              lambda c, v: mods[:, l, 8 * 3 * j + c, v:v + 1], W)

            def add_gated(tiles, gb, rot, gd):
                def finish(t, h, p, tk):
                    s = slice(h * 512, (h + 1) * 512)
                    o, free, ri = rot.get()
                    m = tt(dv, o, p, gb[:, t // 2, s], ALU.mult, tk, gd, free)
                    q = (po, dv)[h]
                    rot.put(ri, tt(q, tiles[t][:, s], tiles[t][:, s], o, ALU.add, m))
                    return m
                return finish

            enter()
            barrier()
            ct = area3(2, 1024)
            enter()
            fn = area(1024)
            junk = area(1024)
            load("ctx", ct, A["ctx_2"].rearrange("o (t p) d -> p (o t) d", p=P))
            load("fn", fn, A["final_norm"].unsqueeze(0).broadcast_to([P, 1024]))
            fill_to(18)
            r = rstd(xa, st[:, 0:2], 2, 1024, 1e-6, junk)
            for t in range(2):
                stt(xa[t], xa[t], st[:, t:t + 1], fn, ALU.mult, ALU.mult, r, small["fn"])
            leave()
            barrier(small["ctx"])
            both = xa + [ct[:, t, :] for t in range(2)]

            def half_ffn(l, j, nt, parts):
                fill_to(18 * (l + 1))
                enter()
                barrier()
                hs = Split(8, nt * 128)
                rot, gb = Rot(area(3, 512)), area(nt // 2, 1024)
                W = ffn_weights(A["ffn_gu_2"][l, j // 2], A["ffn_w_down_2"][l, j // 2], parts, 3 if nt == 2 else 2)
                tiles = both[:nt]
                ready = modulated(l, j, tiles, hs, W)
                enter()
                gd = gate(l, j, gb, area(8, 128), nt // 2, 0.5)
                leave()
                hf = Split(max(parts), nt * 128)
                ffn(hs, ready, W, hf, rot, nt, parts, add_gated(tiles, gb, rot, gd))
                leave()

            def fourier(l):
                enter()
                barrier()
                W = Weights([(A["four_w_2"][0, q * 256:(q + 1) * 256, :].rearrange("(c p) n -> p c n", p=P), 2048)
                             for q in range(4)])
                fs = Split(8, 512)
                gb, row, rot = area3(2, 1024), area(1024), Rot(area(2, 512))
                load("four", row[0:1, :], A["four_b_2"])
                d2, Z = area3(2, 512), None
                load("four", d2, A["c_dft2"])
                enter()
                gd = gate(l, 1, gb, area(8, 128), 2, 1.0)
                leave()
                for s in range(2):
                    enter()
                    d1, hT, Z = area3(2, 512), area(8, 256), area4(2, 4, 512)
                    load(f"dft{s}", d1, A["c_dft1"])
                    sct = st[:, 256:272].rearrange("p (c v) -> p c v", v=2)
                    stt(sct, mods[:, l, 32:40, :], 1.0, bl(ng2[:, l, 1, :], 2), ALU.add, ALU.mult)
                    r = rstd(both[2 * s:2 * s + 2], st[:, 0:2], 2, 1024, 1e-6, Z[:, 0, 0:2, :].rearrange("p a b -> p (a b)"))
                    xs = Z.rearrange("p a b c -> p a (b c)")[:, :, 0:1024]
                    for t in range(2):
                        xd = ts(dv, xs[:, t, :], both[2 * s + t], st[:, t:t + 1], None, ALU.mult, None, r)
                    for c in range(8):
                        b = banks.get()
                        for t in range(2):
                            tk = tr(b.t[:, t * 128:(t + 1) * 128], xs[:, t, c * 128:(c + 1) * 128], xd, b.free,
                                    mark=(t == 1))
                        if c % 2:
                            e = act(hT[:, c, :], b.t[:, 0:256], ACT.Identity, tk, scale=sct[:, c, s:s + 1],
                                    bias=mods[:, l, 24 + c, s:s + 1])
                        else:
                            e = ts(dv, hT[:, c, :], b.t[:, 0:256], sct[:, c, s:s + 1], mods[:, l, 24 + c, s:s + 1],
                                   ALU.mult, ALU.add, tk)
                        b.done(e)
                    hd = [ac.last(), dv.last(), small[f"dft{s}"]]
                    for t in range(2):
                        for g in range(4):
                            b = banks.get()
                            for m in range(2):
                                tk = mm(b.t[:, :], hT[:, 2 * g + m, t * 128:(t + 1) * 128], d1[:, m, :], hd, b.free,
                                        start=m == 0, stop=m == 1, mark=(m == 1))
                            b.done(cp((ac, dv)[g % 2], Z[:, t, g, :], b.t[:, :], tk))
                    zd = [ac.last(), dv.last(), small["four"]]
                    for c in range(8):
                        b = banks.get()
                        i = 0
                        for m in range(2):
                            for h in range(2):
                                o = h * 256 + (c % 2) * 128
                                tk = mm(b.t[:, 0:256], Z[:, m, c // 2, o:o + 128], d2[:, m, h * 256:(h + 1) * 256], zd,
                                        b.free, start=i == 0, stop=i == 3, mark=(i == 3))
                                i += 1
                        o, free, ri = rot.get()
                        e = cp(dv, o[:, 0:256], b.t[:, 0:256], tk, free)
                        b.done(e)
                        fd = fs.put((slice(None), c, slice(s * 256, (s + 1) * 256)), o[:, 0:256], e)
                        rot.put(ri, fd)
                    leave()
                    barrier()
                ob = [[banks.get() for _ in range(2)] for _ in range(4)]
                for q in range(4):
                    wh, wl, rd = W.get(q)
                    wh = wh.rearrange("p (c n) -> p c n", n=1024)
                    wl = wl.rearrange("p (c n) -> p c n", n=1024)
                    for jj in range(2):
                        j = 2 * q + jj
                        for t in range(4):
                            c = slice(t * 128, (t + 1) * 128)
                            for h in range(2):
                                b = ob[t][h]
                                n_ = slice(h * 512, (h + 1) * 512)
                                tk = mm3(b.t[:, :], fs.h[:, j, c], fs.l[:, j, c], wh[:, jj, n_], wl[:, jj, n_],
                                         rd, fd, b.free, start=j == 0, stop=False, mark=(jj == 1))
                    W.free(q, tk)
                for t in range(4):
                    for h in range(2):
                        b = ob[t][h]
                        b.tok = mm(b.t[:, :], onesrow, row[0:1, h * 512:(h + 1) * 512], start=False, mark=True)
                finish = add_gated(both, gb, rot, gd)
                for t in range(4):
                    for h in range(2):
                        b = ob[t][h]
                        b.done(finish(t, h, b.t[:, :], b.tok))
                leave()

            def retention(l):
                enter()
                barrier()
                yT = area(16, 256)
                enter()
                hs = Split(8, 512)
                W = Weights([(A["ret_w_in_2"][i, kh], 2048) for i in range(12) for kh in range(2)], 2, 0)
                ready = modulated(l, 1, both, hs, W)
                barrier()
                cs = area3(2, 256)
                cr = area3(2, 256)
                ex = area3(1, 8)[:, 0, :]
                load("ret", cs, A["c_rope"])
                load("ret", cr, A["c_row"].broadcast_to([P, 512]).rearrange("p (a b) -> p a b", a=2))
                load("ret", ex[:, 0:4], A["c_col"])
                qk = area4(2, 2, 256)
                qr = area4(2, 2, 256)
                t1 = area4(2, 2, 256)
                kc = area3(2, 256)
                kfb = area4(2, 2, 256)
                v = area4(2, 2, 512)
                g = area3(2, 512)
                S = area4(2, 2, 512)
                MD = area3(2, 256)
                qd = t1
                rw = qk[:, 0]
                y = ct.rearrange("p a b -> p (a b)")[:, 0:1024].rearrange("p (a b) -> p a b", b=512)
                rot = Rot(ct.rearrange("p a b -> p (a b)")[:, 1024:2048].rearrange("p (a b) -> p a b", b=512))
                Dc = S.rearrange("p a b c -> p (a b c)").rearrange("p (a b c) -> p a b c", a=4, b=2)
                Pm = kc
                barrier(small["ret"])
                for h in range(4):
                    barrier()
                    load(f"dec{h}", Dc, A["c_ret"])
                    lf, lb = lg[:, h:h + 1], lg[:, 4 + h:5 + h]
                    act(MD, Dc[:, 0], ACT.Exp, small[f"dec{h}"], scale=lf)
                    e0 = act(y[:, :, 0:256], Dc[:, 1], ACT.Exp, scale=lb)
                    dc = st[:, 280:284]
                    act(dc[:, 0:2], ex[:, 0:2], ACT.Exp, scale=lf)
                    e1 = act(dc[:, 2:4], ex[:, 2:4], ACT.Exp, scale=lb)
                    tt(dv, MD, MD, Dc[:, 2], ALU.mult, e0)
                    tt(dv, y[:, :, 0:256], y[:, :, 0:256], Dc[:, 3], ALU.mult)
                    md = tt(dv, MD, MD, y[:, :, 0:256], ALU.add)
                    ba, bk = [banks.get(), banks.get()], banks.get()
                    for kh in range(2):
                        i = 6 * h + kh
                        wh, wl, rd = W.get(i)
                        wh = wh.rearrange("p (k n) -> p k n", k=4)
                        wl = wl.rearrange("p (k n) -> p k n", k=4)
                        for a in range(2):
                            for m in range(2):
                                for k in range(4):
                                    n0 = a * 256 + m * 128
                                    kk_ = 4 * kh + k
                                    mm3(ba[a].t[:, m * 256:(m + 1) * 256], wh[:, k, n0:n0 + 128], wl[:, k, n0:n0 + 128],
                                        hs.h[:, kk_, 0:256], hs.l[:, kk_, 0:256], rd, ready[kk_], ba[a].free,
                                        start=(kk_ == 0 and m == 0), stop=kk_ == 7)
                        for t in range(2):
                            for k in range(4):
                                kk_ = 4 * kh + k
                                c = slice(256 + t * 128, 384 + t * 128)
                                tk = mm3(bk.t[:, t * 256:(t + 1) * 256], hs.h[:, kk_, c], hs.l[:, kk_, c],
                                         wh[:, k, 256:512], wl[:, k, 256:512], bk.free,
                                         start=(kk_ == 0 and t == 0), stop=kk_ == 7, mark=(t == 1 and k == 3))
                        W.free(i, tk)
                    for a in range(2):
                        qe = evac(ac, qk[:, a], v256(ba[a]), tk, scale=None if a == 0 else 0.0625)
                        ba[a].done(qe)
                    ke = evac(ac, kc, v256(bk), tk, scale=0.0625)
                    bk.done(ke)
                    for vg in range(2):
                        bb = [banks.get() for _ in range(4 - 2 * vg)]
                        for kh in range(2):
                            i = 6 * h + 2 + 2 * vg + kh
                            wh, wl, rd = W.get(i)
                            wh = wh.rearrange("p (k n) -> p k n", k=4)
                            wl = wl.rearrange("p (k n) -> p k n", k=4)
                            for t, b in enumerate(bb):
                                c = slice(t * 128, (t + 1) * 128)
                                for k in range(4):
                                    kk_ = 4 * kh + k
                                    tk = mm3(b.t[:, :], hs.h[:, kk_, c], hs.l[:, kk_, c], wh[:, k, :], wl[:, k, :],
                                             rd, b.free, start=kk_ == 0, stop=kk_ == 7, mark=(k == 3))
                            W.free(i, tk)
                        for t, b in enumerate(bb):
                            if vg == 0:
                                ve = cp(ac, v[:, t // 2, t % 2, :], b.t[:, :], tk)
                                b.done(ve)
                            else:
                                ge = act(g[:, t, :], b.t[:, :], ACT.Silu, tk)
                                b.done(ge)
                    for m in range(2):
                        ts(dv, kfb[:, 0, m, :], kc[:, m, :], dc[:, m:m + 1], None, ALU.mult, None, ke, e1)
                        kd = ts(dv, kfb[:, 1, m, :], kc[:, m, :], dc[:, 2 + m:3 + m], None, ALU.mult, None)
                    c2, s2 = bc(cs[:, 0, :], 2), bc(cs[:, 1, :], 2)
                    tt(dv, qr[:, :, 0, :], qk[:, :, 0, :], c2, ALU.mult, qe)
                    tt(dv, t1[:, :, 0, :], qk[:, :, 1, :], s2, ALU.mult)
                    tt(dv, qr[:, :, 0, :], qr[:, :, 0, :], t1[:, :, 0, :], ALU.subtract)
                    tt(dv, qr[:, :, 1, :], qk[:, :, 1, :], c2, ALU.mult)
                    tt(dv, t1[:, :, 0, :], qk[:, :, 0, :], s2, ALU.mult)
                    rp = tt(dv, qr[:, :, 1, :], qr[:, :, 1, :], t1[:, :, 0, :], ALU.add)
                    act(rw[:, 0, :], cr[:, 0, :], ACT.Exp, rp, scale=lf)
                    rx = act(rw[:, 1, :], cr[:, 1, :], ACT.Exp, scale=lb)
                    for d in range(2):
                        qx = tt(dv, qd[:, d], qr[:, 0], bc(rw[:, d, :], 2), ALU.mult, rx)
                    for d in range(2):
                        for m in range(2):
                            b = banks.get()
                            for t in range(2):
                                tk = mm(b.t[:, :], kfb[:, d, t, m * 128:(m + 1) * 128], v[:, 1, t, :], kd, ve, b.free,
                                        start=t == 0, stop=t == 1, mark=(t == 1))
                            se = cp(ac, S[:, d, m, :], b.t[:, :], tk, md)
                            b.done(se)
                    b = banks.get()
                    for tj in range(2):
                        for m in range(2):
                            tk = mm(b.t[:, tj * 256:(tj + 1) * 256], qr[:, 1, m, tj * 128:(tj + 1) * 128], qr[:, 0, m, :],
                                    qx, b.free, start=m == 0, stop=m == 1, mark=(m == 1 and tj == 1))
                    pm = tt(dv, Pm, v256(b), MD, ALU.mult, tk)
                    b.done(pm)
                    for t in range(2):
                        s = slice(t * 128, (t + 1) * 128)
                        b = banks.get()
                        for d in range(2):
                            for m in range(2):
                                mm(b.t[:, :], qd[:, d, m, s], S[:, d, m, :], se, b.free, start=(d == 0 and m == 0),
                                   stop=False)
                        for tj in range(2):
                            tk = mm(b.t[:, :], Pm[:, tj, s], v[:, 0, tj, :], pm, start=False, stop=tj == 1,
                                    mark=(tj == 1))
                        b.done(cp(dv, y[:, t, :], b.t[:, :], tk))
                    mu, va = st[:, 284:286], st[:, 286:288]
                    red(mu, y, ALU.add)
                    ts(dv, mu, mu, 1.0 / 512, None, ALU.mult, None)
                    for t in range(2):
                        e = ts(dv, y[:, t, :], y[:, t, :], mu[:, t:t + 1], None, ALU.subtract, None)
                    r = rstd([y[:, 0, :], y[:, 1, :]], va, 2, 512, 1e-6, S[:, 0, 0, :], e, tk)
                    for t in range(2):
                        e = stt(y[:, t, :], y[:, t, :], va[:, t:t + 1], g[:, t, :], ALU.mult, ALU.mult, r, ge)
                    for q in range(2):
                        b = banks.get()
                        for m in range(2):
                            for t in range(2):
                                c = 2 * q + m
                                tk = tr(b.t[:, (2 * m + t) * 128:(2 * m + t + 1) * 128], y[:, t, c * 128:(c + 1) * 128],
                                        e, b.free, mark=(m == 1 and t == 1))
                        yd = cp(ac, yT[:, 4 * h + 2 * q:4 * h + 2 * q + 2, :], v256(b), tk)
                        b.done(yd)
                leave()
                enter()
                barrier()
                gb, rot = area(1, 1024), Rot(area(2, 512))
                W = Weights([(A["ret_w_out_2"][0, q * 256:(q + 1) * 256, :].rearrange("(c p) n -> p c n", p=P), 2048)
                             for q in range(8)])
                ys = Split(16, 256)
                enter()
                gd = gate(l, 1, gb, area(8, 128), 1, 1.0)
                leave()
                yd = [ys.put((slice(None), slice(4 * q, 4 * q + 4), slice(None)), yT[:, 4 * q:4 * q + 4, :])
                      for q in range(4)]
                project_out(W, ys, yd, add_gated(xa, gb, rot, gd))
                leave()
                leave()

            e = act(lg, lg, ACT.Abs)
            ts(dv, lg, lg, -1.0, None, ALU.mult, None, e)
            half_ffn(0, 0, 4, [11, 11])
            fourier(0)
            half_ffn(0, 2, 4, [11, 11])
            half_ffn(1, 0, 4, [11, 11])
            retention(1)
            half_ffn(1, 2, 2, [22])
            leave()
            enter()
            barrier()
            fg, junk = area(1024), area(1024)
            load("fg", fg, A["final_g_2"].unsqueeze(0).broadcast_to([P, 1024]))
            r = rstd(xa, st[:, 0:2], 2, 1024, 1e-6, junk)
            for t in range(2):
                e = stt(xa[t], xa[t], st[:, t:t + 1], fg, ALU.mult, ALU.mult, r, small["fg"])
            sp.wait(e)
            sp.items.append((lambda e: e.dma_start(out.rearrange("o (t p) d -> p (o t) d", p=P), xt[:, :, :]), s_out))
            sp.items.append((s_out, 16))
            leave()

        s_out = sem("s_out")
        FILL = 0
        for l in range(2):
            ffn1(l, 1)
            mixers(l)
            ffn1(l, 2)
        second()

        block = ctx.enter_context(nc.Block())

        @block.sync
        def _(eng):
            sp.emit(eng)

        @block.tensor
        def _(eng):
            pe.emit(eng)

        @block.scalar
        def _(eng):
            ac.emit(eng)

        @block.vector
        def _(eng):
            dv.emit(eng)

        @block.gpsimd
        def _(eng):
            po.emit(eng)


def constants():
    f = np.float32
    i = np.arange(128)
    a, b = np.meshgrid(i, i, indexing="ij")
    ch = a // 64 == b // 64

    def level(n):
        h = n // 2
        return ((a // n == b // n) & (a % n < h) & (b % n >= h)).astype(f)

    m = dict(ident=np.eye(128), tri=a <= b, ones=np.ones((128, 128)), negT=np.where(a <= b, 0, -1e30),
             neg=np.where(b <= a, 0, -1e30), bones=ch, l2=level(2).T, l2t=level(2), l4=level(4), l8=level(8),
             l16=level(16), l32=level(32), l64=level(64), i2=np.hstack([np.eye(128)[:, :64] + np.eye(128)[:, 64:]] * 2))
    c = {"c_msk": np.stack([np.asarray(m[n], f) for n in MASKS], 1)}
    strict, incl = (ch & (a < b)).astype(f), (ch & (a <= b)).astype(f)
    c["c_mask4"] = np.stack([strict, incl, strict, incl], 1)
    c["c_scan"] = np.broadcast_to((np.arange(256) % 64 != 0).astype(f), (128, 256)).copy()
    n = np.arange(256)
    ang = 2 * np.pi * ((n[:, None] * n[None, :]) % 256) / 256
    C, S = np.cos(ang), np.sin(ang)
    d1 = np.concatenate([C, S], 1).astype(f)
    d2 = (np.concatenate([C, -S], 1) / 256).astype(f)
    c["c_dft1"] = d1.reshape(2, 128, 512).transpose(1, 0, 2).copy()
    c["c_dft2"] = d2.reshape(2, 128, 512).transpose(1, 0, 2).copy()
    inv = (f(10000.0) ** (-np.arange(64, dtype=f) / f(64))).astype(f)
    row, colm = (n // 64).astype(f), (n % 64).astype(f)
    g = np.concatenate([row[:, None] * inv, colm[:, None] * inv], 1).astype(f)
    c["c_rope"] = np.stack([np.cos(g).T, np.sin(g).T], 1).astype(f)
    j = np.arange(256)
    dif = (j[None, :] - j[:, None])
    t = np.stack([np.maximum(dif, 0), np.maximum(-dif, 0), dif >= 0, dif <= 0]).astype(f)
    c["c_ret"] = t.reshape(4, 2, 128, 256).transpose(2, 0, 1, 3).copy()
    c["c_row"] = np.concatenate([j + 1, 256 - j]).astype(f)[None, :]
    p = np.arange(128)
    c["c_col"] = np.stack([255 - p, 127 - p, p, p + 128], 1).astype(f)
    return c


def layout(x):
    col = lambda a: np.ascontiguousarray(a).reshape(-1, 128).T
    d = {}

    def tiles(w, n):
        m = w.shape[1] // n
        return np.ascontiguousarray(w.reshape(8, 128, m, n).transpose(2, 1, 0, 3)).reshape(m, 128, 8 * n)

    def gate_up(g, u):
        w = np.stack([g.reshape(8, 128, 22, 128), u.reshape(8, 128, 22, 128)])
        return np.ascontiguousarray(w.transpose(3, 2, 1, 0, 4)).reshape(22, 128, 2048)

    def halves(w):
        m = w.shape[1] // 512
        return np.ascontiguousarray(w.reshape(2, 4, 128, m, 512).transpose(3, 0, 2, 1, 4)).reshape(m, 2, 128, 2048)

    for k in (1, 2):
        w = x[f"ffn{k}_w_gate_up"]
        d[f"ffn{k}_w_gate_up"] = np.stack([gate_up(w[l][:, :2816], w[l][:, 2816:]) for l in range(2)])
        d[f"ffn{k}_w_down"] = x[f"ffn{k}_w_down"]
    g, u = x["ffn_w_gate_2"], x["ffn_w_up_2"]
    d["ffn_gu_2"] = np.stack([np.stack([gate_up(g[l, j], u[l, j]) for j in range(2)]) for l in range(2)])
    d["ffn_w_down_2"] = x["ffn_w_down_2"]
    w = x["w_in"]
    t_cols = np.r_[3352:5144, 1024:2304, 2320:2832]
    n_cols = np.r_[0:1024, 2832:3344]
    s_cols = np.r_[2304:2320, 3344:3352]
    d["w_in_t"] = np.stack([tiles(w[l][:, t_cols], 256) for l in range(2)])
    d["w_in_n"] = np.stack([halves(w[l][:, n_cols]) for l in range(2)])
    d["w_in_s"] = np.stack([tiles(w[l][:, s_cols], 24)[0] for l in range(2)])
    d["ada_w_2"] = np.stack([halves(x["ada_w_2"][l]) for l in range(2)])
    w = x["ret_w_in_2"][0]
    q, k, v, gg = w[:, :1024], w[:, 1024:2048], w[:, 2048:4096], w[:, 4096:]
    cat = [a for h in range(4) for a in (q[:, h * 256:(h + 1) * 256], k[:, h * 256:(h + 1) * 256],
                                         v[:, h * 512:(h + 1) * 512], gg[:, h * 512:(h + 1) * 512])]
    d["ret_w_in_2"] = halves(np.concatenate(cat, 1))
    for n in ("x", "mlstm_wq", "mlstm_wk", "mlstm_wv", "rwkv_w_up", "rwkv_a_up", "rwkv_g_up", "w_out", "ctx_2",
              "final_norm", "final_g_2", "four_w_2", "four_b_2", "ret_w_out_2"):
        d[n] = x[n]
    cc = []
    for l in range(2):
        cw = np.concatenate([x["ssd_conv_w"][l], x["mlstm_conv_w"][l]], 1)
        cw = cw.reshape(4, 14, 128).transpose(2, 1, 0).reshape(128, 56)
        cb = np.concatenate([x["ssd_conv_b"][l], x["mlstm_conv_b"][l]])
        one = {"n1": x["ffn1_norm"][l], "nm": x["mix_norm"][l], "n2": x["ffn2_norm"][l], "cb": cb,
               "sn": x["ssd_norm"][l], "mn": x["mlstm_norm"][l], "mu": x["rwkv_shift_mu"][l], "w0": x["rwkv_w0"][l],
               "a0": x["rwkv_a0"][l], "kk": x["rwkv_k_k"][l], "ka": x["rwkv_k_a"][l],
               "rk": x["rwkv_r_k"][l], "lw": x["rwkv_ln_w"][l], "lb": x["rwkv_ln_b"][l]}
        cc += [cw if n == "cw" else col(one[n]) for n, _ in COLS1]
    cc += [col(x["norm_g_2"]), col(x["ada_b_2"])]
    two = np.stack([col(x["c_2"][0]), col(x["c_ctx_2"])], 2).reshape(128, 16)
    d["c_cols"] = np.ascontiguousarray(np.concatenate(cc + [two], 1))
    r = [x[n][l] for l in range(2) for n in ("ssd_dt_bias", "ssd_a_log", "ssd_d", "mlstm_gate_bias")]
    d["c_rows"] = np.concatenate(r + [x["ret_decay_2"].reshape(-1)])[None, :]
    d.update(constants())
    return d


def kernel(**inputs):
    import concourse.bacc as _bacc
    from concourse.bass_utils import run_bass_kernel_spmd as _run

    nc = _bacc.Bacc("TRN2", target_bir_lowering=False, num_devices=1)
    arrays, A = {}, {}
    for name, a in layout({k: np.asarray(v) for k, v in inputs.items()}).items():
        a = np.ascontiguousarray(a)
        arrays["in_" + name] = a
        A[name] = nc.dram_tensor("in_" + name, a.shape, mybir.dt.from_np(a.dtype), kind="ExternalInput").ap()
    out = nc.dram_tensor("out_0", (1, 256, 1024), F32, kind="ExternalOutput").ap()
    build(nc, A, out)
    r = _run(nc, [arrays], core_ids=[0])
    return r.results[0]["out_0"]
```

```python
from contextlib import ExitStack

import numpy as np

import concourse.bass as bass
from concourse import mybir

F32 = mybir.dt.float32
F32R = mybir.dt.float32r
ALU = mybir.AluOpType
ACT = mybir.ActivationFunctionType
AX = mybir.AxisListType.X
P = 128
NSLOT = 6
SLOT = 2048
DECAY = float(np.exp(-0.5))

COLS1 = [("n1", 8), ("nm", 8), ("n2", 8), ("cw", 56), ("cb", 14), ("sn", 8), ("mn", 4), ("mu", 14),
         ("w0", 4), ("a0", 4), ("kk", 4), ("ka", 4), ("rk", 4), ("lw", 4), ("lb", 4)]
NCOL1 = sum(n for _, n in COLS1)
NCOLS = 2 * NCOL1 + 2 * 24 + 2 * 72 + 16
MASKS = ["ident", "tri", "ones", "negT", "neg", "bones", "l2", "l2t", "l4", "l8", "l16", "l32", "l64", "i2"]


class Queue:

    def __init__(self, name, sem, chained):
        self.name, self.sem, self.chained = name, sem, chained
        self.items, self.n, self.seen, self.pending = [], 0, {}, []

    def wait(self, *tokens):
        for t in tokens:
            if t is None:
                continue
            if isinstance(t, list):
                self.wait(*t)
                continue
            sem, n, key = t
            if n > self.seen.get(key, 0):
                self.seen[key] = n
                self.items.append((sem, n))

    def __call__(self, fn, *after, mark=True):
        if self.pending:
            self.wait(*self.pending)
            self.pending = []
        self.wait(*after)
        if self.chained and self.n:
            self.wait((self.sem, self.n, self.name))
        if mark:
            self.n += 1
        self.items.append((fn, mark))
        return (self.sem, self.n, self.name) if mark else None

    def last(self):
        return (self.sem, self.n, self.name) if self.n else None

    def emit(self, eng):
        for a, b in self.items:
            if callable(a):
                ins = a(eng)
                if b is True:
                    ins.then_inc(self.sem, 1)
                elif b:
                    ins.then_inc(b, 16)
            else:
                eng.wait_ge(a, b)


class Bank:
    def __init__(self, t, i):
        self.t, self.i, self.free, self.busy = t, i, None, False

    def done(self, token):
        self.free, self.busy = token, False


class Banks:
    def __init__(self, tensors):
        self.banks = [Bank(t, i) for i, t in enumerate(tensors)]
        self.at = 0

    def get(self):
        b = self.banks[self.at % len(self.banks)]
        self.at += 1
        assert not b.busy
        b.busy = True
        return b


class Ring:

    def __init__(self, tensor, sems, sp):
        self.t, self.sems, self.sp = tensor, sems, sp
        self.at, self.count, self.owner = 0, [0] * NSLOT, [None] * NSLOT

    def load(self, src, width):
        i = self.at % NSLOT
        self.at += 1
        assert self.owner[i] != "busy"
        dst = self.t[:, i, 0:width]
        if len(src.shape) == 3:
            dst = dst.rearrange("p (c n) -> p c n", n=src.shape[2])
        self.sp.wait(self.owner[i])
        sem = self.sems[i]
        self.sp.items.append((lambda e: e.dma_start(dst, src, max_dma_last_dim=16384), sem))
        self.owner[i] = "busy"
        self.count[i] += 16
        return self.t[:, i, 0:width], (sem, self.count[i], f"ring{i}"), i

    def free(self, i, token):
        self.owner[i] = token


def build(nc, A, out):
    with ExitStack() as ctx:
        sbt = lambda name, shape: ctx.enter_context(nc.sbuf_tensor(name, shape, F32))
        sem = lambda name: ctx.enter_context(nc.semaphore(name))

        ring_t = sbt("ring", [P, NSLOT, SLOT])
        xt = sbt("xt", [P, 2, 1024])
        msk = sbt("msk", [P, len(MASKS), 128])
        mask4 = sbt("mask4", [P, 4, 128])
        scanm = sbt("scanm", [P, 256])
        cols = sbt("cols", [P, NCOLS])
        rows = sbt("rows", [P, 120])
        mods = sbt("mods", [P, 2, 72, 2])
        sil = sbt("sil", [P, 8, 2])
        st = sbt("st", [P, 512])
        acc = sbt("acc", [P, 2, 512])
        psums = [ctx.enter_context(nc.psum_tensor(f"ps{i}", [P, 512], F32)) for i in range(8)]

        pe = Queue("pe", sem("s_pe"), False)
        ac = Queue("ac", sem("s_ac"), True)
        dv = Queue("dv", sem("s_dv"), True)
        po = Queue("po", sem("s_po"), True)
        sp = Queue("sp", sem("s_sp"), False)
        ring = Ring(ring_t, [sem(f"s_ring{i}") for i in range(NSLOT)], sp)
        banks = Banks(psums)

        ident, tri, ones, negT, neg, bones, l2, l2t = (msk[:, i, :] for i in range(8))
        lvl = [msk[:, 8 + i, :] for i in range(5)]
        i2 = msk[:, 13, 0:64]
        onesrow = msk[0:1, 2, :]

        def mm(o, l, r, *after, start=True, stop=True, mark=False):
            return pe(lambda e: e.matmul(o, l, r, start=start, stop=stop, skip_group_check=True), *after, mark=mark)

        def tr(o, i, *after, mark=False):
            return pe(lambda e: e.transpose(o, i, ident), *after, mark=mark)

        def act(o, i, f, *after, **kw):
            return ac(lambda e: e.activation(o, i, f, **kw), *after)

        def tt(q, o, a, b, op, *after):
            return q(lambda e: e.tensor_tensor(o, a, b, op), *after)

        def ts(q, o, a, s1, s2, op0, op1, *after):
            if s2 is None:
                return q(lambda e: e.tensor_scalar(o, a, s1, None, op0), *after)
            return q(lambda e: e.tensor_scalar(o, a, s1, s2, op0, op1), *after)

        def stt(o, a, s, b, op0, op1, *after):
            return dv(lambda e: e.scalar_tensor_tensor(out=o, in0=a, scalar=s, in1=b, op0=op0, op1=op1), *after)

        def cp(q, o, a, *after):
            if q is ac:
                return act(o, a, ACT.Copy, *after)
            return q(lambda e: e.tensor_copy(o, a), *after)

        def red(o, a, op, *after):
            return dv(lambda e: e.tensor_reduce(o, a, AX, op), *after)

        def rcp(o, a, *after):
            return dv(lambda e: e.reciprocal(o, a), *after)

        def zero(o):
            return dv(lambda e: e.memset(o, 0.0))

        small = {}

        def load(name, dst, src, *after):
            s, n, _ = small.get(name) or (sem("s_" + name), 0, None)
            ac.wait(*ac.pending, *after)
            ac.pending = []
            ac.wait(ac.last())
            ac.items.append((lambda e: e.dma_start(dst, src), s))
            small[name] = (s, n + 16, "load_" + name)

        def barrier(*more, waits=(pe, ac, dv, po)):
            toks = [q.last() for q in (pe, ac, dv, po)] + list(more)
            for q in waits:
                q.pending += [t for t in toks if t and t[2] != q.name]

        scopes = []
        names = [0]

        def enter():
            scopes.append(ExitStack())

        def leave():
            scopes.pop().close()

        def area(*shape, dt=F32):
            names[0] += 1
            t = scopes[-1].enter_context(nc.sbuf_tensor(f"a{names[0]}", [P, *shape], dt))
            return t[tuple(slice(None) for _ in range(len(shape) + 1))]

        area3 = area4 = area

        class Rot:

            def __init__(self, t):
                self.t, self.n, self.at, self.tok = t, t.shape[1], -1, [None] * t.shape[1]

            def get(self):
                self.at = (self.at + 1) % self.n
                return self.t[:, self.at, :], self.tok[self.at], self.at

            def put(self, i, token):
                self.tok[i] = token

        class Split:

            def __init__(self, *shape):
                self.h, self.l = area(*shape, dt=F32R), area(*shape, dt=F32R)

            def put(self, ix, src, *after):
                return self.low(ix, src, self.high(ix, src, *after), *after)

            def high(self, ix, src, *after):
                return act(self.h[ix], src, ACT.Copy, *after)

            def low(self, ix, src, *after):
                return tt(dv, self.l[ix], src, self.h[ix].bitcast(F32), ALU.subtract, *after)

        class Weights:

            def __init__(self, srcs, bufs=2, first=1):
                self.srcs, self.n, self.bufs = srcs, 0, bufs
                self.b = [Split(2048) for _ in range(bufs)]
                self.freed = [None] * bufs
                self.ready = []
                for _ in range(first):
                    self.more()

            def more(self):
                if self.n < len(self.srcs):
                    src, width = self.srcs[self.n]
                    i = self.n % self.bufs
                    w, rd, slot = ring.load(src, width)
                    tk = self.b[i].put((slice(None), slice(0, width)), w, rd, self.freed[i])
                    ring.free(slot, tk)
                    self.ready.append(tk)
                    self.n += 1

            def get(self, k):
                while self.n < min(k + self.bufs, len(self.srcs)):
                    self.more()
                width = self.srcs[k][1]
                b = self.b[k % self.bufs]
                return b.h[:, 0:width], b.l[:, 0:width], self.ready[k]

            def free(self, k, token):
                self.freed[k % self.bufs] = token
                if self.bufs > 2:
                    self.more()

        def mm3(o, wh, wl, xh, xl, *after, start, stop, mark=False):
            mm(o, wh, xh, *after, start=start, stop=False)
            mm(o, wh, xl, start=False, stop=False)
            return mm(o, wl, xh, start=False, stop=stop, mark=mark)

        def col(l, name, i=0, n=1):
            at = l * NCOL1
            for nm, w in COLS1:
                if nm == name:
                    break
                at += w
            return cols[:, at + i:at + i + n]

        C2 = 2 * NCOL1
        ng2 = cols[:, C2:C2 + 48].rearrange("p (l j c) -> p l j c", l=2, j=3)
        ab2 = cols[:, C2 + 48:C2 + 192].rearrange("p (l c) -> p l c", l=2)
        cc2 = cols[:, C2 + 192:C2 + 208].rearrange("p (c v) -> p c v", v=2)

        load("x", xt[:, :, :], A["x"].rearrange("o (t p) d -> p (o t) d", p=P))
        load("const", msk[:, :, :], A["c_msk"])
        load("const", cols[:, :], A["c_cols"])
        load("const", rows[:, :], A["c_rows"].broadcast_to([P, 120]))
        load("late", mask4[:, :, :], A["c_mask4"])
        load("late", scanm[:, :], A["c_scan"])
        sp.wait(small["const"], small["x"])
        cst = dv(lambda e: e.memset(st[:, 500:501], -0.5))
        barrier(small["const"], small["x"])

        ac_sil = act(sil[:, :, :], cc2, ACT.Silu)

        def modulation():
            read = None
            for l in range(2):
                for t in range(18):
                    for h in range(2):
                        w, ready, slot = ring.load(A["ada_w_2"][l, t, h], 2048)
                        w = w.rearrange("p (k n) -> p k n", k=4)
                        for k in range(4):
                            for v in range(2):
                                s = sil[:, 4 * h + k, v:v + 1]
                                if h == 0 and k == 0:
                                    e = ts(dv, acc[:, v, :], w[:, k, :], s, None, ALU.mult, None, ready, read, ac_sil)
                                else:
                                    e = stt(acc[:, v, :], w[:, k, :], s, acc[:, v, :], ALU.mult, ALU.add, ready)
                            if k == 1:
                                yield
                        ring.free(slot, e)
                        yield
                    b = banks.get()
                    for i in range(4):
                        for v in range(2):
                            read = mm(b.t[:, 2 * i + v:2 * i + v + 1], acc[:, v, i * 128:(i + 1) * 128], ones[:, 0:1],
                                      e, b.free, mark=(i == 3 and v == 1))
                    bias = ab2[:, l, 4 * t:4 * t + 4].unsqueeze(2).broadcast_to([P, 4, 2])
                    b.done(tt(dv, mods[:, l, 4 * t:4 * t + 4, :],
                              b.t[:, 0:8].rearrange("p (a b) -> p a b", b=2), bias, ALU.add, read))
                    filled[0] = 18 * l + t + 1

        mod = modulation()
        filled, steps = [0], [0]

        def fill(n):
            for _ in range(n):
                steps[0] += 1
                if next(mod, 1):
                    return

        def fill_slot():
            if steps[0] % 2:
                fill(1)

        def fill_to(tiles):
            while filled[0] < tiles:
                fill(1)
            fill_slot()

        def power(o, v, n):
            return po(lambda e: e.tensor_tensor(o, v, st[:, 500:501].broadcast_to([P, n]), ALU.pow))

        def rstd(tiles, o, n, width, eps, junk, *after):
            for i, a in enumerate(tiles):
                t = ac(lambda e, a=a, i=i: e.activation(junk[:, 0:width], a, ACT.Square,
                                                       accum_out=o[:, i:i + 1]), *after)
            ts(po, o[:, 0:n], o[:, 0:n], 1.0 / width, eps, ALU.mult, ALU.add, t)
            return power(o[:, 0:n], o[:, 0:n], n)

        def norm_t(tiles, hs, scale, bias, W):
            n = len(tiles)
            enter()
            xs = area(n, 1024)
            rot = Rot(area(3, 512))
            ready = []
            r = rstd(tiles, st[:, 0:n], n, 1024, 1e-6, xs[:, 0, :])
            done = [ts(dv, xs[:, i, :], tiles[i], st[:, i:i + 1], None, ALU.mult, None, r) for i in range(n)]
            if W:
                W.more()
            jobs = [(c, s) for c in range(8) for s in range(n // 2)]
            late = None

            def low():
                ix, src, a, ri = late
                d = hs.low(ix, src, a)
                rot.put(ri, d)
                ready.extend([d] * (2 if n == 2 else 1))

            for j in range(0, len(jobs), 2):
                pair, took = [banks.get(), banks.get()], []
                for b, (c, s) in zip(pair, jobs[j:j + 2]):
                    for t in range(2):
                        tk = tr(b.t[:, t * 128:(t + 1) * 128], xs[:, 2 * s + t, c * 128:(c + 1) * 128],
                                done[2 * s + t], b.free, mark=(t == 1))
                    took.append(tk)
                o, free, ri = rot.get()
                e = []
                for m, (c, s) in enumerate(jobs[j:j + 2]):
                    sc, bi = scale(c, s), bias(c, s) if bias else None
                    i, om, tk = pair[m].t[:, 0:256], o[:, m * 256:(m + 1) * 256], took[m]
                    if m == 0 and bias:
                        e.append(ts(dv, om, i, sc, bi, ALU.mult, ALU.add, tk, free))
                    elif m == 0:
                        e.append(ts(dv, om, i, sc, None, ALU.mult, None, tk, free))
                    elif bias:
                        e.append(act(om, i, ACT.Identity, tk, free, scale=sc, bias=bi))
                    else:
                        e.append(act(om, i, ACT.Copy, tk, free, scale=sc))
                    pair[m].done(e[m])
                c = jobs[j][0]
                if n == 2:
                    ix, src = (slice(None), slice(c, c + 2), slice(None)), o.rearrange("p (a b) -> p a b", b=256)
                else:
                    ix, src = (slice(None), c, slice(None)), o
                if late:
                    low()
                late = (ix, src, hs.high(ix, src, e), ri)
            low()
            leave()
            return ready

        def back_products(W, tile, count, out_b, x, xtok, final, between):
            n = (count + 1) // 2
            groups = [[i] for i in range(n)]
            if final:
                groups[-2:] = [[n - 2, n - 1]]
            for group in groups:
                parts = []
                for i in group:
                    wh, wl, rd = W.get(tile + i)
                    wh = wh.rearrange("p (c n) -> p c n", n=1024)
                    wl = wl.rearrange("p (c n) -> p c n", n=1024)
                    parts += [(2 * i + jj, wh[:, jj, :], wl[:, jj, :], rd) for jj in range(min(2, count - 2 * i))]
                if len(group) > 1:
                    order = [(p, t) for t in range(len(out_b)) for p in parts]
                else:
                    order = [(p, t) for p in parts for t in range(len(out_b))]
                for at, ((j, wh, wl, rd), t) in enumerate(order):
                    rows_ = slice(t * 128, (t + 1) * 128)
                    for h in range(2):
                        b = out_b[t][h]
                        n_ = slice(h * 512, (h + 1) * 512)
                        b.tok = tk = mm3(b.t[:, :], x.h[:, j, rows_], x.l[:, j, rows_], wh[:, n_], wl[:, n_], rd,
                                         xtok(j), b.free, start=j == 0, stop=j == count - 1,
                                         mark=(j == count - 1 or (at == len(order) - 1 and h == 1)))
                for i in group:
                    W.free(tile + i, tk)
                    between(i)
            return tk

        def ffn(hs, ready, W, hf, rot, nt, parts, finish, side=None):
            N = nt * 128
            tile, j0 = 0, 0
            last = dv.last()
            for count in parts:
                hfd = []
                for j in range(count):
                    wh, wl, rd = W.get(tile)
                    wh = wh.rearrange("p (k h n) -> p k h n", k=8, h=2)
                    wl = wl.rearrange("p (k h n) -> p k h n", k=8, h=2)
                    if nt == 2:
                        b1 = b2 = banks.get()
                        o1, o2 = b1.t[:, 0:256], b1.t[:, 256:512]
                    else:
                        b1, b2 = banks.get(), banks.get()
                        o1, o2 = b1.t[:, :], b2.t[:, :]
                    for h, (b, o) in enumerate(((b1, o1), (b2, o2))):
                        for k in range(8):
                            tk = mm3(o, wh[:, k, h, :], wl[:, k, h, :], hs.h[:, k, 0:N], hs.l[:, k, 0:N], rd, ready[k],
                                     b.free, start=k == 0, stop=k == 7, mark=(h == 1 and k == 7))
                    s, free, ri = rot.get()
                    s = s[:, 0:N]
                    a = act(s, o1, ACT.Silu, tk, free)
                    d = tt(dv, s, s, o2, ALU.mult, a, tk)
                    b1.done(d)
                    if b2 is not b1:
                        b2.done(d)
                    if nt == 4 or tile % 3 < 2:
                        fill(1)
                    if side:
                        next(side, None)
                    W.free(tile, tk)
                    tile += 1
                    hfd.append(hf.put((slice(None), j, slice(0, N)), s, d, last))
                    if nt == 4:
                        fill(1)
                    rot.put(ri, hfd[-1])
                out_b = [[banks.get() for _ in range(2)] for _ in range(nt)]

                def between(q):
                    if nt == 2 and q % 3 == 0:
                        fill(1)

                tk = back_products(W, tile, count, out_b, hf, lambda j: hfd[j], tile + (count + 1) // 2 == len(W.srcs),
                                   between)
                tile += (count + 1) // 2
                if tile == len(W.srcs) and nt == 2:
                    fill_slot()
                for t in range(nt):
                    for h in range(2):
                        b = out_b[t][h]
                        b.done(finish(t, h, b.t[:, :], b.tok))
                if nt == 4:
                    fill_slot()
                last = tk
            assert tile == len(W.srcs)

        def ffn_weights(gu, down, parts, bufs):
            srcs, j = [], 0
            for count in parts:
                srcs += [(gu[j + i], 2048) for i in range(count)]
                srcs += [(down[(j + q) * 128:(j + q + min(2, count - q)) * 128, :].rearrange("(c p) n -> p c n", p=P),
                          min(2, count - q) * 1024) for q in range(0, count, 2)]
                j += count
            return Weights(srcs, bufs, 0)

        xa = [xt[:, t, :] for t in range(2)]

        def ffn1(l, which):
            enter()
            barrier()
            hs = Split(8, 256)
            rot = Rot(area(3, 256))
            W = ffn_weights(A[f"ffn{which}_w_gate_up"][l], A[f"ffn{which}_w_down"][l], [22], 3)
            nm = "n1" if which == 1 else "n2"
            ready = norm_t(xa, hs, lambda c, s: col(l, nm, c), None, W)
            hf = Split(22, 256)
            ffn(hs, ready, W, hf, rot, 2, [22],
                lambda t, h, p, tk: stt(xt[:, t, h * 512:(h + 1) * 512], p, 0.5, xt[:, t, h * 512:(h + 1) * 512],
                                        ALU.mult, ALU.add, tk))
            leave()

        def load_small(l, smallw, *after):
            sw = smallw[:, 0:1536].rearrange("p (w h e) -> p w h e", w=3, h=4)
            for i, nm in enumerate(("mlstm_wq", "mlstm_wk", "mlstm_wv")):
                load(f"sm{l}", sw[:, i], A[nm][l].rearrange("h d e -> d h e"), *after)
            load(f"sm{l}", smallw[0:64, 1536:2048], A["rwkv_w_up"][l])
            load(f"sm{l}", smallw[64:128, 1536:2048], A["rwkv_a_up"][l])
            load(f"sm{l}", smallw[:, 2048:2560], A["rwkv_g_up"][l])

        def evac(q, o, i, *after, scale=None):
            if q is ac:
                return act(o, i, ACT.Copy, *after, scale=1.0 if scale is None else scale)
            if scale is not None:
                return ts(q, o, i, scale, None, ALU.mult, None, *after)
            return cp(q, o, i, *after)

        def v256(b):
            return b.t[:, :].rearrange("p (a b) -> p a b", b=256)

        def v128(b):
            return b.t[:, :].rearrange("p (a b) -> p a b", b=128)

        def v64(b):
            return b.t[:, :].rearrange("p (a b) -> p a b", b=64)

        def bc(a, n):
            return a.unsqueeze(1).broadcast_to([a.shape[0], n, a.shape[1]])

        def bl(a, n):
            return a.unsqueeze(2).broadcast_to([a.shape[0], a.shape[1], n])

        def project_out(W, ys, yd, finish, side=None):
            ob = [[banks.get() for _ in range(2)] for _ in range(2)]
            back_products(W, 0, 16, ob, ys, lambda j: yd[j // 4], True, lambda q: next(side, None) if side else None)
            for T in range(2):
                for h in range(2):
                    b = ob[T][h]
                    b.done(finish(T, h, b.t[:, :], b.tok))

        def mixers(l):
            enter()
            barrier()
            yT = area(16, 256)
            enter()
            smallw = area(2560)
            hx = Split(8, 256)
            ready = norm_t(xa, hx, lambda c, s: col(l, "nm", c), None, None)
            sw = smallw[:, 0:1536].rearrange("p (w h e) -> p w h e", w=3, h=4)

            def pairs(first):
                return [(A["w_in_t"][l, first + q], 2048) for q in range(7)]

            def project_t(W, take):
                for q in range(7):
                    wh, wl, rd = W.get(q)
                    wh = wh.rearrange("p (k n) -> p k n", k=8)
                    wl = wl.rearrange("p (k n) -> p k n", k=8)
                    b = banks.get()
                    for m in range(2):
                        for k in range(8):
                            c = slice(m * 128, (m + 1) * 128)
                            tk = mm3(b.t[:, m * 256:(m + 1) * 256], wh[:, k, c], wl[:, k, c], hx.h[:, k, :],
                                     hx.l[:, k, :], rd, ready[k], b.free, start=k == 0, stop=k == 7,
                                     mark=(m == 1 and k == 7))
                    W.free(q, tk)
                    b.done(take(q, b, tk))

            enter()
            KR = area4(8, 2, 128)
            be, ch = area3(4, 256), area3(4, 256)
            KBV = area3(16, 128)
            bet, cht, vt = area3(2, 512), area3(2, 512), area3(2, 512)
            gl = area(256)
            Wc = area3(4, 4)
            enter()
            us = area3(14, 256)
            enter()
            W = Weights(pairs(0))
            ts(dv, st[:, 300:314], col(l, "mu", 0, 14), -1.0, 1.0, ALU.mult, ALU.add)
            nmu = dv.last()

            def mixed(q, b, tk):
                if q == 0:
                    load_small(l, smallw)
                for m in range(2):
                    i = 2 * q + m
                    a = act(us[:, i, :], b.t[:, m * 256:(m + 1) * 256], ACT.Copy, tk, nmu, scale=st[:, 300 + i:301 + i])
                for m in range(2):
                    i = 2 * q + m
                    e = stt(us[:, i, 1:256], b.t[:, m * 256:m * 256 + 255], col(l, "mu", i), us[:, i, 1:256],
                            ALU.mult, ALU.add, a, tk)
                return e

            project_t(W, mixed)
            leave()
            barrier(small[f"sm{l}"], small["late"])
            sgw, ab, cwb, t0, t1, t2, t3 = (area3(4, 256) for _ in range(7))
            r_, k_, v_ = us[:, 0:4, :], us[:, 4:8, :], us[:, 8:12, :]
            half = lambda c: slice((c % 2) * 256, (c % 2) * 256 + 256)
            act(us[0:64, 12, :], us[0:64, 12, :], ACT.Tanh)
            th = act(gl, us[:, 13, :], ACT.Sigmoid)
            kk = t0
            for c in range(4):
                kd = ts(dv, kk[:, c, :], k_[:, c, :], col(l, "kk", c), None, ALU.mult, None)
            sq = act(t1, kk, ACT.Square, kd)
            bs = [banks.get(), banks.get()]
            for c in range(4):
                tks = mm(bs[c // 2].t[:, half(c)], bones, t1[:, c, :], sq, bs[c // 2].free, mark=True)
            bw = [banks.get(), banks.get()]
            ba = [banks.get(), banks.get()]
            tw, ta = [], []
            for c in range(4):
                cs = slice(1536 + c * 128, 1664 + c * 128)
                tw.append(mm(bw[c // 2].t[:, half(c)], smallw[0:64, cs], us[0:64, 12, :], th, bw[c // 2].free,
                             mark=True))
            for c in range(4):
                cs = slice(1536 + c * 128, 1664 + c * 128)
                ta.append(mm(ba[c // 2].t[:, half(c)], smallw[64:128, cs], us[64:128, 12, :], ba[c // 2].free,
                             mark=True))
            for i in range(2):
                e = act(t1[:, 2 * i:2 * i + 2, :], v256(bs[i]), ACT.Sqrt, tks)
                bs[i].done(e)
            ts(dv, t1, t1, 1e-6, None, ALU.max, None, e)
            rcp(t1, t1)
            tt(dv, kk, kk, t1, ALU.mult)
            for c in range(4):
                bw[c // 2].done(act(sgw[:, c, :], bw[c // 2].t[:, half(c)], ACT.Sigmoid, tw[c | 1],
                                    bias=col(l, "w0", c)))
            sgwd = ac.last()
            for c in range(4):
                ba[c // 2].done(act(ab[:, c, :], ba[c // 2].t[:, half(c)], ACT.Sigmoid, ta[c | 1],
                                    bias=col(l, "a0", c)))
            sgd = ac.last()
            for c in range(4):
                dv(lambda e, o=cwb[:, c, :], i=sgw[:, c, :]: e.tensor_tensor_scan(o, scanm[:, :], i, 0.0,
                                                       ALU.mult, ALU.add), sgwd)
            cw4 = cwb.rearrange("p c (a b) -> p (c a) b", b=64)
            cwd = dv.last()
            d2 = tt(dv, sgw, cwb, sgw, ALU.subtract)
            d4 = tt(dv, t3.rearrange("p c (a b) -> p (c a) b", b=64), cw4,
                    cw4[:, :, 63:64].broadcast_to([P, 16, 64]), ALU.subtract)
            for c in range(4):
                ts(dv, t1[:, c, :], ab[:, c, :], 1.0, col(l, "ka", c), ALU.subtract, ALU.mult, sgd)
            stt(k_, t1, 1.0, k_, ALU.add, ALU.mult)
            for c in range(4):
                stt(t1[:, c, :], r_[:, c, :], col(l, "rk", c), k_[:, c, :], ALU.mult, ALU.mult)
            bs = [banks.get(), banks.get()]
            td = dv.last()
            for c in range(4):
                tk = mm(bs[c // 2].t[:, half(c)], bones, t1[:, c, :], td, bs[c // 2].free, mark=True)
            tt(dv, ab, kk, ab, ALU.mult)
            t8 = lambda a: a.rearrange("p c (t n) -> p (c t) n", n=128)
            w2 = act(sgw, sgw, ACT.Exp, d2, scale=-DECAY)
            w3 = act(t2, cwb, ACT.Exp, scale=DECAY)
            w5 = act(t3, t3, ACT.Exp, d4, scale=DECAY)
            w4 = act(Wc.rearrange("p c a -> p (c a)").unsqueeze(2), cw4[:, :, 63:64], ACT.Exp, scale=-DECAY)
            w1 = act(cwb, cwb, ACT.Exp, scale=-DECAY)
            tt(dv, KR[:, :, 0, :], t8(sgw), t8(kk), ALU.mult, w2)
            tt(dv, be, ab, t2, ALU.mult, w3)
            tt(dv, ch, k_, t2, ALU.mult)
            d5 = tt(dv, ab, ab, t3, ALU.mult, w5)
            d6 = tt(dv, k_, k_, t3, ALU.mult)
            tt(dv, KR[:, :, 1, :], t8(cwb), t8(r_), ALU.mult, w1)
            for i in range(2):
                e = tt(dv, yT[:, 12 + 2 * i:14 + 2 * i, :], v256(bs[i]), v_[:, 2 * i:2 * i + 2, :], ALU.mult, tk)
                bs[i].done(e)
            for q, (src, dst) in enumerate(((lambda c, T: KR[:, 2 * c + T, 0, :], None),
                                            (lambda c, T: ab[:, c, T * 128:T * 128 + 128], bet),
                                            (lambda c, T: k_[:, c, T * 128:T * 128 + 128], cht),
                                            (lambda c, T: v_[:, c, T * 128:T * 128 + 128], vt))):
                for T in range(2):
                    b = banks.get()
                    for c in range(4):
                        tk = tr(b.t[:, c * 128:(c + 1) * 128], src(c, T), d6, b.free, mark=(c == 3))
                    o = KBV[:, T * 8:T * 8 + 8, 0:64] if dst is None else dst[:, T, :]
                    b.done(cp((ac, dv)[T], o, v64(b) if dst is None else b.t[:, :], tk))

            leave()
            enter()
            barrier()
            GH = area4(16, 2, 128)
            nT = area3(16, 128)
            nTT = area3(4, 256)
            MT = area4(2, 4, 64)
            enter()
            Tm, TT, X, CT = (area3(8, 128) for _ in range(4))
            yf = yT[:, 0:12, :].rearrange("p a b -> p (a b)")
            AB = yf[:, 0:2048].rearrange("p (u w n) -> p u w n", u=8, w=2)
            NN = yf[:, 2048:2816].rearrange("p (c h n) -> p c h n", c=3, h=4)
            for T in range(2):
                for h in range(8):
                    c, j = h // 2, h % 2
                    js = slice(64 * j, 64 * j + 64)
                    b = banks.get()
                    kr = KR[js, 2 * c + T, :, :].rearrange("p a b -> p (a b)")
                    mm(b.t[:, 0:256], be[js, c, T * 128:T * 128 + 128], kr, b.free)
                    tk = mm(b.t[:, 256:512], ch[js, c, T * 128:T * 128 + 128], kr, mark=True)
                    g4 = b.t[:, :].rearrange("p (a b n) -> p a b n", a=2, b=2)
                    m4 = mask4[:, :, :].rearrange("p (a b) n -> p a b n", b=2)
                    tt(dv, AB[:, 4 * j + c, :, :], g4[:, :, 0, :], m4[:, :, 0, :], ALU.mult, tk)
                    b.done(tt(dv, GH[:, T * 8 + h, :, :], g4[:, :, 1, :], m4[:, :, 1, :], ALU.mult))
                abd, ttd = dv.last(), [None, None]
                for j in range(2):
                    js = slice(64 * j, 64 * j + 64)
                    b = banks.get()
                    for c in range(4):
                        tk = mm(b.t[:, c * 128:(c + 1) * 128], KR[js, 2 * c + T, 0, :],
                                be[js, c, T * 128:T * 128 + 128], b.free, mark=(c == 3))
                    gs = slice(4 * j, 4 * j + 4)
                    b.done(tt(dv, Tm[:, gs, :], v128(b), bc(l2, 4), ALU.mult, tk))
                    tt(dv, Tm[:, gs, :], bc(ident, 4), Tm[:, gs, :], ALU.subtract)
                tdone = [dv.last(), dv.last()]
                xd = [None, None]
                cts = [tt(po, CT[:, 4 * j:4 * j + 4, :], AB[:, 4 * j:4 * j + 4, 0, :], bc(lvl[0], 4), ALU.mult, abd)
                       for j in range(2)]
                for j, q in enumerate((dv, po)):
                    gs = slice(4 * j, 4 * j + 4)
                    tt(q, TT[:, gs, :], AB[:, gs, 0, :], bc(l2t, 4), ALU.mult, abd)
                    ttd[j] = tt(q, TT[:, gs, :], bc(ident, 4), TT[:, gs, :], ALU.subtract)
                for L in range(5):
                    for j in range(2):
                        gs = slice(4 * j, 4 * j + 4)
                        b = banks.get()
                        for c in range(4):
                            u = 4 * j + c
                            tk = mm(b.t[:, c * 128:(c + 1) * 128], CT[:, u, :], Tm[:, u, :], cts[j], tdone[j], b.free,
                                    mark=(c == 3))
                        xd[j] = cp(ac, X[:, gs, :], v128(b), tk)
                        if L < 4:
                            cts[j] = tt(po, CT[:, gs, :], AB[:, gs, 0, :], bc(lvl[L + 1], 4), ALU.mult, tk)
                        b.done(xd[j])
                    for j in range(2):
                        gs = slice(4 * j, 4 * j + 4)
                        b2, b3 = banks.get(), banks.get()
                        for c in range(4):
                            u = 4 * j + c
                            tk = mm(b3.t[:, c * 128:(c + 1) * 128], X[:, u, :], TT[:, u, :], xd[j], ttd[j], b3.free,
                                    mark=(c == 3))
                        if L < 4:
                            for c in range(4):
                                u = 4 * j + c
                                tk = mm(b2.t[:, c * 128:(c + 1) * 128], TT[:, u, :], X[:, u, :], b2.free,
                                        mark=(c == 3))
                            b2.done(tt(dv, Tm[:, gs, :], Tm[:, gs, :], v128(b2), ALU.subtract, tk))
                        else:
                            b2.done(b2.free)
                        tdone[j] = tt(dv, TT[:, gs, :], TT[:, gs, :], v128(b3), ALU.subtract, tk)
                        b3.done(tdone[j])
                b = banks.get()
                for h in range(8):
                    c, j = h // 2, h % 2
                    tk = mm(b.t[:, h * 64:(h + 1) * 64], AB[:, 4 * j + c, 1, :], vt[:, T, h * 64:(h + 1) * 64],
                            b.free, mark=(h == 7))
                bv = cp(dv, KBV[:, T * 8:T * 8 + 8, 64:128], v64(b), tk)
                b.done(bv)
                for q in range(2):
                    b = banks.get()
                    for m in range(4):
                        h = 4 * q + m
                        c, j = h // 2, h % 2
                        tk = mm(b.t[:, m * 128:(m + 1) * 128], TT[:, 4 * j + c, :], KBV[:, T * 8 + h, :], bv, tdone,
                                b.free, mark=(m == 3))
                    nt_ = evac(ac, nT[:, T * 8 + 4 * q:T * 8 + 4 * q + 4, :], v128(b), tk, scale=-1.0)
                    b.done(nt_)
                b = banks.get()
                for h in range(8):
                    c, j = h // 2, h % 2
                    tk = mm(b.t[64 * j:64 * j + 64, c * 128:(c + 1) * 128], KBV[:, T * 8 + h, 0:64],
                            TT[:, 4 * j + c, :], b.free, mark=(h == 7))
                b.done(evac(ac, nTT[:, :, T * 128:T * 128 + 128], v128(b), tk, scale=-1.0))
                for i in range(2):
                    cc = 2 * T + i
                    if cc == 3:
                        continue
                    rs = slice(64 * i, 64 * i + 64)
                    b = banks.get()
                    for h in range(8):
                        c, j = h // 2, h % 2
                        hs = slice(h * 64, (h + 1) * 64)
                        os = slice(64 * j, 64 * j + 64)
                        mm(b.t[os, c * 128:c * 128 + 64], nT[rs, T * 8 + h, 0:64], bet[rs, T, hs], nt_, b.free)
                        mm(b.t[os, c * 128 + 64:c * 128 + 128], cht[rs, T, hs], vt[rs, T, hs], start=True, stop=False)
                        tk = mm(b.t[os, c * 128 + 64:c * 128 + 128], bet[rs, T, hs], nT[rs, T * 8 + h, 64:128],
                                start=False, stop=True, mark=(h == 7))
                    if cc:
                        for c in range(4):
                            stt(MT[:, cc - 1, c, :], i2, Wc[:, c, cc:cc + 1], b.t[:, c * 128:c * 128 + 64],
                                ALU.mult, ALU.add, tk)
                    b.done(cp(dv, NN[:, cc, :, :], v128(b)[:, :, 64:128], tk))

            leave()
            barrier()
            S = area4(4, 4, 64)
            SA = area3(16, 64)
            Yb = area3(16, 64)
            Yc = area3(16, 64)
            zero(S[:, 0, :, :])
            sd = cp(dv, S[:, 1, :, :], NN[:, 0, :, :])
            for cc in (1, 2):
                bj = [banks.get(), banks.get()]
                for j in range(2):
                    js = slice(64 * j, 64 * j + 64)
                    for c in range(4):
                        tk = mm(bj[j].t[js, c * 64:(c + 1) * 64], MT[js, cc - 1, c, :], S[js, cc, c, :], sd,
                                bj[j].free, mark=(c == 3))
                for j in range(2):
                    js = slice(64 * j, 64 * j + 64)
                    sd = tt(dv, S[js, cc + 1, :, :], v64(bj[j])[js, 0:4, :], NN[js, cc, :, :], ALU.add, tk)
                    bj[j].done(sd)
            bj = [banks.get(), banks.get()]
            for j in range(2):
                js = slice(64 * j, 64 * j + 64)
                for cc in range(4):
                    for c in range(4):
                        T, i = cc // 2, cc % 2
                        tk = mm(bj[j].t[64 * i:64 * i + 64, (T * 4 + c) * 64:(T * 4 + c + 1) * 64],
                                nTT[js, c, cc * 64:cc * 64 + 64], S[js, cc, c, :], sd, bj[j].free,
                                mark=(cc == 3 and c == 3))
            SAj = SA.rearrange("p (a j) n -> p a j n", j=2)
            nTj = nT.rearrange("p (a j) n -> p a j n", j=2)
            Ybj = Yb.rearrange("p (a j) n -> p a j n", j=2)
            for j in range(2):
                sad = tt(dv, SAj[:, :, j, :], v64(bj[j]), nTj[:, :, j, 64:128], ALU.add, tk)
                bj[j].done(sad)
            for j in range(2):
                js = slice(64 * j, 64 * j + 64)
                b = banks.get()
                for T in range(2):
                    for c in range(4):
                        u = T * 8 + 2 * c + j
                        rg = slice((T * 4 + c) * 64, (T * 4 + c + 1) * 64)
                        mm(b.t[:, rg], GH[:, u, 0, :], SA[:, u, :], sad, b.free, start=True, stop=False)
                        mm(b.t[:, rg], GH[:, u, 1, :], vt[:, T, (2 * c + j) * 64:(2 * c + j + 1) * 64],
                           start=False, stop=False)
                        for i in range(2):
                            tk = mm(b.t[64 * i:64 * i + 64, rg], KR[js, 2 * c + T, 1, 64 * i:64 * i + 64],
                                    S[js, 2 * T + i, c, :], start=False, stop=True,
                                    mark=(T == 1 and c == 3 and i == 1))
                b.done(cp(dv, Ybj[:, :, j, :], v64(b), tk))
            mu = st[:, 16:32]
            va = st[:, 32:48]
            red(mu, Yb, ALU.add)
            ts(dv, mu, mu, 1.0 / 64, None, ALU.mult, None)
            yc = tt(dv, Yc, Yb, bl(mu, 64), ALU.subtract)
            s2 = act(Yb, Yc, ACT.Square, yc)
            r2 = red(va, Yb, ALU.add, s2)
            ts(po, va, va, 1.0 / 64, 64e-5, ALU.mult, ALU.add, r2)
            pw = power(va, va, 16)
            yn = tt(dv, Yc, Yc, bl(va, 64), ALU.mult, pw)
            Ycf = Yc.rearrange("p (t h) n -> p t (h n)", t=2)
            for q in range(2):
                b, bg = banks.get(), banks.get()
                for m in range(2):
                    c = 2 * q + m
                    for T in range(2):
                        tr(b.t[:, (2 * m + T) * 128:(2 * m + T + 1) * 128], Ycf[:, T, c * 128:(c + 1) * 128], yn, b.free)
                for m in range(2):
                    c = 2 * q + m
                    tk = mm(bg.t[:, m * 256:(m + 1) * 256], smallw[:, 2048 + c * 128:2176 + c * 128], gl, bg.free,
                            mark=True)
                tmp = Yb.rearrange("p a b -> p (a b)")[:, 0:512].rearrange("p (a b) -> p a b", b=256)
                for m in range(2):
                    c = 2 * q + m
                    ts(dv, tmp[:, m, :], b.t[:, m * 256:(m + 1) * 256], col(l, "lw", c), col(l, "lb", c),
                       ALU.mult, ALU.add, tk)
                ys = yT[:, 12 + 2 * q:14 + 2 * q, :]
                b.done(tt(dv, ys, tmp, ys, ALU.add))
                bg.done(tt(dv, ys, ys, v256(bg), ALU.mult))

            leave()
            leave()
            barrier()
            uT = area3(14, 259)
            zt = area3(2, 1024)
            ot = area3(2, 512)
            dg = area3(2, 24)
            xc = area3(14, 256)
            enter()
            zero(uT[:, :, 0:3])

            def conv(c, *after):
                ts(dv, xc[:, c, :], uT[:, c, 0:256], col(l, "cw", 4 * c), None, ALU.mult, None, *after)
                for k in range(1, 4):
                    e = stt(xc[:, c, :], uT[:, c, k:k + 256], col(l, "cw", 4 * c + k), xc[:, c, :], ALU.mult, ALU.add)
                return e

            def shifted(q, b, tk):
                a = cp(ac, uT[:, 2 * q:2 * q + 2, 3:259], v256(b), tk)
                conv(q, ua[q // 2]) if q else None
                ua.append(a)
                return a

            W = Weights(pairs(7) + [(A["w_in_n"][l, q, kh], 2048) for q in range(3) for kh in range(2)]
                        + [(A["w_in_s"][l], 192)])
            ua = []
            project_t(W, shifted)
            left = [0] + list(range(7, 14))
            for q in range(3):
                bb = [banks.get(), banks.get()]
                for kh in range(2):
                    i = 7 + 2 * q + kh
                    wh, wl, rd = W.get(i)
                    wh = wh.rearrange("p (k n) -> p k n", k=4)
                    wl = wl.rearrange("p (k n) -> p k n", k=4)
                    for T in range(2):
                        for k in range(4):
                            kk_ = 4 * kh + k
                            c = slice(T * 128, (T + 1) * 128)
                            tk = mm3(bb[T].t[:, :], hx.h[:, kk_, c], hx.l[:, kk_, c], wh[:, k, :], wl[:, k, :], rd,
                                     bb[T].free, start=kk_ == 0, stop=kk_ == 7, mark=(k == 3))
                    W.free(i, tk)
                    if q < 2:
                        conv(left.pop(0), ua[6])
                        cd = conv(left.pop(0))
                for T in range(2):
                    if q < 2:
                        e = act(zt[:, T, q * 512:(q + 1) * 512], bb[T].t[:, :], ACT.Silu, tk)
                    else:
                        e = act(ot[:, T, :], bb[T].t[:, :], ACT.Sigmoid, tk)
                    bb[T].done(e)
                if q == 1:
                    for c in range(14):
                        xcd = act(xc[:, c, :], xc[:, c, :], ACT.Silu, cd, bias=col(l, "cb", c))
            wh, wl, rd = W.get(13)
            wh = wh.rearrange("p (k n) -> p k n", k=8)
            wl = wl.rearrange("p (k n) -> p k n", k=8)
            for T in range(2):
                b = banks.get()
                c = slice(T * 128, (T + 1) * 128)
                for k in range(8):
                    tk = mm3(b.t[:, 0:24], hx.h[:, k, c], hx.l[:, k, c], wh[:, k, :], wl[:, k, :], rd, b.free,
                             start=k == 0, stop=k == 7, mark=(k == 7))
                b.done(cp(ac, dg[:, T, :], b.t[:, 0:24], tk))
            leave()
            barrier()
            enter()

            def softplus(o, x, n, *after):
                t = st[:, 440:440 + n]
                a = act(t, x, ACT.Abs, dv.last(), *after)
                a = act(t, t, ACT.Exp, scale=-1.0)
                a = act(t, t, ACT.Ln, a, bias=1.0)
                return stt(o, x, 0.0, t, ALU.max, ALU.add, a)

            R0 = 56 * l

            def back(src, first, count, name, *after):
                for c in range(0, count, 2):
                    b = banks.get()
                    for m in range(2):
                        for T in range(2):
                            tk = tr(b.t[:, (2 * m + T) * 128:(2 * m + T + 1) * 128],
                                    src[:, T, (c + m) * 128:(c + m + 1) * 128], b.free, *after, mark=(m == 1 and T == 1))
                    for m in range(2):
                        e = ts(dv, yT[:, first + c + m, :], b.t[:, m * 256:(m + 1) * 256], col(l, name, c + m), None,
                               ALU.mult, None, tk)
                    b.done(e)

            def mlstm():
                rowsT = uT.rearrange("p a b -> p (a b)")
                part = lambda a, first, n: a[:, first:first + n].rearrange("p (a b) -> p a b", b=128)
                qT, kT = yT[:, 0:4, :], yT[:, 8:12, :]
                vt = yT[:, 4:8, :].rearrange("p a b -> p (a b)").rearrange("p (t a b) -> p t a b", t=2, b=128)
                Dm = [part(rowsT, 0, 512), part(rowsT, 512, 512)]
                Cs = part(rowsT, 1024, 512)
                hh = rowsT[:, 1536:2560].rearrange("p (a b) -> p a b", b=512)
                nv = mnv
                s4 = lambda i: st[:, 310 + 8 * i:318 + 8 * i].rearrange("p (t h) -> p t h", t=2)
                li, lf, bcu, mi, il, mt, wi, em, den = (s4(i) for i in range(9))
                nl = st[:, 382:390].rearrange("p (t h) -> p t h", t=2)
                g8 = st[:, 390:406].rearrange("p (t h) -> p t h", t=2)
                bend, mpv, wend, t4 = (st[:, 406 + 4 * i:410 + 4 * i] for i in range(4))
                nmt = st[:, 422:430].rearrange("p (t h) -> p t h", t=2)
                gm = st[:, 430:438]
                xm = uT[:, 10:14, 3:259]
                xcc = xc[:, 10:14, :]
                sc = 128 ** -0.5
                for i, (o, scale) in enumerate(((qT, None), (kT, sc))):
                    for q in range(2):
                        b = banks.get()
                        for m in range(2):
                            tk = mm(b.t[:, m * 256:(m + 1) * 256], sw[:, i, 2 * q + m, :], xcc[:, 2 * q + m, :], b.free,
                                    mark=(m == 1))
                        b.done(evac(ac, o[:, 2 * q:2 * q + 2, :], v256(b), tk, scale=scale))
                        yield
                b = banks.get()
                for h in range(4):
                    tk = mm(b.t[:, h * 128:(h + 1) * 128], xcc[:, h, 0:128], sw[:, 1, h, :], b.free, mark=(h == 3))
                b.done(evac(ac, kt, v128(b), tk, scale=sc))
                yield
                for T in range(2):
                    b = banks.get()
                    for h in range(4):
                        tk = mm(b.t[:, h * 128:(h + 1) * 128], xm[:, h, T * 128:(T + 1) * 128], sw[:, 2, h, :], b.free,
                                mark=(h == 3))
                    b.done(cp(ac, vt[:, T, :, :], v128(b), tk))
                projd = ac.last()
                yield
                tt(dv, g8, dg[:, :, 16:24], bc(rows[:, R0 + 48:R0 + 56], 2), ALU.add)
                cp(dv, li, g8[:, :, 0:4])
                ts(dv, lf, g8[:, :, 4:8], -1.0, None, ALU.mult, None)
                lff = st[:, 318:326]
                softplus(lff, lff, 8)
                cp(dv, nl, lf)
                ld = ts(dv, lff, lff, -1.0, None, ALU.mult, None)
                b = banks.get()
                for T in range(2):
                    mm(b.t[:, 4 * T:4 * T + 4], tri, lf[:, T, :], ld, b.free)
                tk = mm(b.t[:, 8:12], ones, lf[:, 0, :], mark=True)
                cp(dv, st[:, 326:334], b.t[:, 0:8], tk)
                e = cp(dv, bend, b.t[:, 8:12])
                b.done(e)
                yield
                for T in range(2):
                    b = banks.get()
                    for h in range(4):
                        hs = slice(h * 128, (h + 1) * 128)
                        mm(b.t[:, hs], nl[:, T, h:h + 1].broadcast_to([P, 128]), tri, b.free, stop=False)
                        tk = mm(b.t[:, hs], li[:, T, h:h + 1].broadcast_to([P, 128]), ident, start=False, mark=(h == 3))
                    if T == 0:
                        red(t4, v128(b), ALU.max, tk)
                        tt(dv, t4, t4, bend, ALU.add)
                        tt(dv, mpv, bend, t4, ALU.max)
                        tt(dv, wend, li[:, 0, :], bcu[:, 0, :], ALU.subtract)
                        tt(dv, wend, wend, bend, ALU.add)
                        e = tt(dv, wend, wend, mpv, ALU.subtract)
                        we = act(wend, wend, ACT.Exp, e)
                    for h in range(4):
                        e = stt(Dm[T][:, h, :], b.t[:, h * 128:(h + 1) * 128], bcu[:, T, h:h + 1], neg, ALU.add, ALU.add, tk)
                    b.done(e)
                    red(mi[:, T, :], Dm[T], ALU.max)
                    yield
                cp(dv, il[:, 0, :], bcu[:, 0, :])
                tt(dv, il[:, 1, :], bcu[:, 1, :], mpv, ALU.add)
                tt(dv, st[:, 350:358], st[:, 342:350], st[:, 334:342], ALU.max)
                tt(dv, st[:, 358:366], st[:, 342:350], st[:, 350:358], ALU.subtract)
                e = ts(dv, st[:, 422:430], st[:, 350:358], -1.0, None, ALU.mult, None)
                act(st[:, 358:366], st[:, 358:366], ACT.Exp, e)
                act(st[:, 366:374], st[:, 422:430], ACT.Exp)
                yield
                for T in range(2):
                    for h in range(4):
                        wx = act(Dm[T][:, h, :], Dm[T][:, h, :], ACT.Exp, bias=nmt[:, T, h:h + 1])
                vwd = tt(dv, vw, vt[:, 0, :, :], bl(wend, 128), ALU.mult, we, projd)
                yield
                b = banks.get()
                for h in range(4):
                    tk = mm(b.t[:, h * 128:(h + 1) * 128], kt[:, h, :], vw[:, h, :], vwd, projd, b.free, mark=(h == 3))
                csd = cp(ac, Cs, v128(b), tk)
                b.done(csd)
                b = banks.get()
                for h in range(4):
                    tk = mm(b.t[:, h:h + 1], kt[:, h, :], wend[:, h:h + 1], b.free, mark=(h == 3))
                csd = cp(ac, nv, b.t[:, 0:4], tk)
                b.done(csd)
                yield
                for T in range(2):
                    b = banks.get()
                    for h in range(4):
                        s = slice(T * 128, (T + 1) * 128)
                        tk = mm(b.t[:, h * 128:(h + 1) * 128], qT[:, h, s], kT[:, h, s], projd, b.free, mark=(h == 3))
                    e = tt(dv, Dm[T], v128(b), Dm[T], ALU.mult, tk, wx)
                    b.done(e)
                    red(den[:, T, :], Dm[T], ALU.add)
                    yield
                    b = banks.get()
                    for h in range(4):
                        tk = tr(b.t[:, h * 128:(h + 1) * 128], Dm[T][:, h, :], e, b.free, mark=(h == 3))
                    pt = cp(ac, PTs[T], v128(b), tk)
                    b.done(pt)
                    yield
                    b = banks.get()
                    for h in range(4):
                        tk = mm(b.t[:, h * 128:(h + 1) * 128], PTs[T][:, h, :], vt[:, T, h, :], pt, b.free, mark=(h == 3))
                    h4 = hh[:, T, :].rearrange("p (h n) -> p h n", h=4)
                    b.done(cp(dv, h4, v128(b), tk))
                    yield
                    if T == 1:
                        b, b2 = banks.get(), banks.get()
                        for h in range(4):
                            mm(b.t[:, h * 128:(h + 1) * 128], qT[:, h, 128:256], Cs[:, h, :], csd, b.free)
                        for h in range(4):
                            tk = mm(b2.t[:, h:h + 1], qT[:, h, 128:256], nv[:, h:h + 1], b2.free, mark=(h == 3))
                        e = tt(dv, vw, v128(b), bl(wi[:, 1, :], 128), ALU.mult, tk)
                        b.done(e)
                        tt(dv, h4, h4, vw, ALU.add)
                        e = tt(dv, t4, b2.t[:, 0:4], wi[:, 1, :], ALU.mult)
                        b2.done(e)
                        tt(dv, den[:, 1, :], den[:, 1, :], t4, ALU.add)
                        yield
                rows_free.append(True)
                dn = st[:, 374:382]
                e = act(dn, dn, ACT.Abs, dv.last())
                tt(dv, dn, dn, st[:, 366:374], ALU.max, e)
                rcp(dn, dn)
                for T in range(2):
                    h4 = hh[:, T, :].rearrange("p (h n) -> p h n", h=4)
                    tt(dv, h4, h4, bl(den[:, T, :], 128), ALU.mult)
                    e = tt(dv, hh[:, T, :], hh[:, T, :], ot[:, T, :], ALU.mult)
                    yield
                tiles = [hh[:, T, h * 128:(h + 1) * 128] for T in range(2) for h in range(4)]
                r = rstd(tiles, gm, 8, 128, 1e-6, Dm[0][:, 0, :], e)
                for i, a in enumerate(tiles):
                    e = ts(dv, a, a, gm[:, i:i + 1], None, ALU.mult, None, r)
                yield
                back(hh, 8, 4, "mn", e)

            (kt, vw), PTs, mnv = (area3(4, 128) for _ in range(2)), [area3(4, 128) for _ in range(2)], area(4)
            other, rows_free = mlstm(), []

            def step(n=1):
                for _ in range(n):
                    next(other, None)

            Xt = area3(2, 1024)
            xd_ = area3(2, 1024)
            xw = area(1024)
            Bt = area(128)
            Ss = area(512)
            cb = area4(2, 2, 128)
            Ms = [area3(4, 128) for _ in range(3)]
            yy = area3(2, 1024)
            dt = st[:, 64:96].rearrange("p (t h) -> p t h", t=2)
            ad = st[:, 96:128].rearrange("p (t h) -> p t h", t=2)
            acu = st[:, 128:160].rearrange("p (t h) -> p t h", t=2)
            nac = st[:, 160:192].rearrange("p (t h) -> p t h", t=2)
            en = st[:, 192:208]
            wd = st[:, 208:224]
            xa1 = st[:, 224:240]
            nA = st[:, 240:256]
            gm = st[:, 256:264]
            w = act(nA, rows[:, R0 + 16:R0 + 32], ACT.Exp, cd)
            ts(dv, nA, nA, -1.0, None, ALU.mult, None, w)
            tt(dv, dt, dg[:, :, 0:16], bc(rows[:, R0:R0 + 16], 2), ALU.add, ac.last())
            softplus(st[:, 64:96], st[:, 64:96], 32)
            a_ = tt(dv, ad, dt, bc(nA, 2), ALU.mult)
            b = banks.get()
            for T in range(2):
                mm(b.t[:, T * 16:T * 16 + 16], tri, ad[:, T, :], a_, b.free)
            tk = mm(b.t[:, 32:48], ones, ad[:, 0, :], mark=True)
            cp(dv, st[:, 128:160], b.t[:, 0:32], tk)
            ts(dv, st[:, 160:192], b.t[:, 0:32], -1.0, None, ALU.mult, None)
            e = tt(dv, en, b.t[:, 32:48], acu[:, 0, :], ALU.subtract)
            b.done(e)
            w = act(wd, en, ACT.Exp, e)
            w = act(xa1, acu[:, 1, :], ACT.Exp)
            step(1)
            for T in range(2):
                for q in range(2):
                    b = banks.get()
                    for c in range(4):
                        tk = tr(b.t[:, c * 128:(c + 1) * 128], xc[:, 4 * q + c, T * 128:(T + 1) * 128], xcd, b.free,
                                mark=(c == 3))
                    b.done(cp(ac, Xt[:, T, q * 512:(q + 1) * 512], b.t[:, :], tk))
                    step(1)
            b = banks.get()
            tk = tr(b.t[:, 0:128], xc[:, 8, 0:128], b.free, mark=True)
            b.done(cp(ac, Bt, b.t[:, 0:128], tk))
            xd = ac.last()
            h64 = lambda a: a.rearrange("p (h n) -> p h n", n=64)
            for T in range(2):
                tt(dv, h64(xd_[:, T, :]), h64(Xt[:, T, :]), bl(dt[:, T, :], 64), ALU.mult, xd)
            xwd = tt(dv, h64(xw), h64(xd_[:, 0, :]), bl(wd, 64), ALU.mult)
            for T in range(2):
                skip = tt(po, h64(Xt[:, T, :]), h64(Xt[:, T, :]), bl(rows[:, R0 + 32:R0 + 48], 64), ALU.mult, xwd)
            bg = [banks.get(), banks.get()]
            for g in range(2):
                for T in range(2):
                    s = slice(T * 128, (T + 1) * 128)
                    tk = mm(bg[g].t[:, s], xc[64 * g:64 * g + 64, 8, s], xc[64 * g:64 * g + 64, 9, s], xcd,
                            bg[g].free, mark=(T == 1))
            for g in range(2):
                bg[g].done(cp(ac, cb[:, g, :, :], bg[g].t[:, 0:256].rearrange("p (a b) -> p a b", b=128), tk))
            b = banks.get()
            for g in range(2):
                tk = mm(b.t[64 * g:64 * g + 64, :], Bt[:, 64 * g:64 * g + 64], xw[:, g * 512:(g + 1) * 512], xwd, xd,
                        b.free, mark=(g == 1))
            ssd = cp(ac, Ss, b.t[:, :], tk)
            b.done(ssd)
            step(2)
            hold = [None] * 3

            def sums(n):
                T, g, q = n // 4, n // 2 % 2, n % 2
                b = banks.get()
                for m in range(4):
                    h = 8 * g + 4 * q + m
                    tk = mm(b.t[:, m * 128:(m + 1) * 128], ad[:, T, h:h + 1].broadcast_to([P, 128]), tri,
                            b.free, mark=(m == 3))
                return b, tk

            def decays(n, b, tk):
                T, g, q = n // 4, n // 2 % 2, n % 2
                M = Ms[n % 3]
                for m in range(4):
                    h = 8 * g + 4 * q + m
                    e = stt(M[:, m, :], b.t[:, m * 128:(m + 1) * 128], nac[:, T, h:h + 1], negT, ALU.add,
                            ALU.add, tk, hold[n % 3])
                b.done(e)
                return act(M, M, ACT.Exp, e)

            ahead, summed = decays(0, *sums(0)), sums(1)
            for T in range(2):
                for g in range(2):
                    by = banks.get()
                    for q in range(2):
                        n = 4 * T + 2 * g + q
                        x, M = ahead, Ms[n % 3]
                        if n < 7:
                            now, summed = summed, sums(n + 2) if n < 6 else None
                            ahead = decays(n + 1, *now)
                        e = tt(dv, M, M, bc(cb[:, g, T, :], 4), ALU.mult, x)
                        for m in range(4):
                            h = 8 * g + 4 * q + m
                            hold[n % 3] = tk = mm(by.t[:, (4 * q + m) * 64:(4 * q + m + 1) * 64], M[:, m, :],
                                                  xd_[:, T, h * 64:(h + 1) * 64], e, by.free, mark=(m == 3))
                        if q == 0:
                            step(1)
                    ys = yy[:, T, g * 512:(g + 1) * 512]
                    by.done(cp(dv, ys, by.t[:, :], tk))
                    step(2)
                    if T == 1:
                        b = banks.get()
                        tk = mm(b.t[:, :], xc[64 * g:64 * g + 64, 9, 128:256], Ss[64 * g:64 * g + 64, :], ssd, b.free,
                                mark=True)
                        tmp = xw[:, g * 512:(g + 1) * 512]
                        e = tt(dv, h64(tmp), v64(b), bl(xa1[:, 8 * g:8 * g + 8], 64), ALU.mult, tk)
                        b.done(e)
                        tt(dv, ys, ys, tmp, ALU.add)
            for T in range(2):
                tt(dv, yy[:, T, :], yy[:, T, :], Xt[:, T, :], ALU.add, skip)
                e = tt(dv, yy[:, T, :], yy[:, T, :], zt[:, T, :], ALU.mult)
            step(1)
            tiles = [yy[:, T, g * 512:(g + 1) * 512] for T in range(2) for g in range(2)]
            r = rstd(tiles, gm, 4, 512, 1e-6, Xt[:, 0, :], e)
            for i, a in enumerate(tiles):
                e = ts(dv, a, a, gm[:, i:i + 1], None, ALU.mult, None, r)

            step(2)
            assert rows_free
            back(yy, 0, 8, "sn", e)
            step(99)

            leave()
            yd = [dv.last(), ac.last()]
            leave()
            enter()
            barrier()
            W = Weights([(A["w_out"][l, q * 256:(q + 1) * 256, :].rearrange("(c p) n -> p c n", p=P), 2048)
                         for q in range(8)])
            ys = Split(16, 256)
            yd = [ys.put((slice(None), slice(4 * q, 4 * q + 4), slice(None)), yT[:, 4 * q:4 * q + 4, :])
                  for q in range(4)]
            project_out(W, ys, yd, lambda t, h, p, tk: tt(dv, xt[:, t, h * 512:(h + 1) * 512], p,
                                                          xt[:, t, h * 512:(h + 1) * 512], ALU.add, tk))
            leave()
            leave()

        def context():
            enter()
            barrier()
            ct = area3(2, 1024)
            enter()
            fn = area(1024)
            junk = area(1024)
            load("fn", fn, A["final_norm"].unsqueeze(0).broadcast_to([P, 1024]))
            load("ctx", ct, A["ctx_2"].rearrange("o (t p) d -> p (o t) d", p=P))
            return ct, fn, junk

        def second(ct, fn, junk):
            lg = rows[:, 112:120]

            def gates(l, j, gb, dg, n, half):
                tk = None
                for v in range(n):
                    for q in range(2):
                        for m in range(4):
                            e = ts(dv, dg[:, m, :], ident, mods[:, l, 8 * (3 * j + 2) + 4 * q + m, v:v + 1], half,
                                   ALU.mult, ALU.mult, tk)
                        yield
                        b = banks.get()
                        for m in range(4):
                            tk = mm(b.t[:, m * 128:(m + 1) * 128], ones, dg[:, m, :], e, b.free, mark=(m == 3))
                        gated[0] = cp(ac, gb[:, v, q * 512:(q + 1) * 512], b.t[:, :], tk)
                        b.done(gated[0])
                        yield

            def modulated(l, j, tiles, hs, W):
                sct = st[:, 256:272].rearrange("p (c v) -> p c v", v=2)
                s = 8 * (3 * j + 1)
                stt(sct, mods[:, l, s:s + 8, :], 1.0, bl(ng2[:, l, j, :], 2), ALU.add, ALU.mult)
                return norm_t(tiles, hs, lambda c, v: sct[:, c, v:v + 1],
                              lambda c, v: mods[:, l, 8 * 3 * j + c, v:v + 1], W)

            gated = [None]

            def add_gated(tiles, gb, rot):
                def finish(t, h, p, tk):
                    s = slice(h * 512, (h + 1) * 512)
                    o, free, ri = rot.get()
                    m = tt(dv, o, p, gb[:, t // 2, s], ALU.mult, tk, gated[0], free)
                    q = (po, dv)[h]
                    rot.put(ri, tt(q, tiles[t][:, s], tiles[t][:, s], o, ALU.add, m))
                    return m
                return finish

            barrier()
            fill_to(18)
            r = rstd(xa, st[:, 0:2], 2, 1024, 1e-6, junk)
            for t in range(2):
                stt(xa[t], xa[t], st[:, t:t + 1], fn, ALU.mult, ALU.mult, r, small["fn"])
            leave()
            barrier(small["ctx"])
            both = xa + [ct[:, t, :] for t in range(2)]

            def half_ffn(l, j, nt, parts):
                fill_to(18 * (l + 1))
                enter()
                barrier()
                hs = Split(8, nt * 128)
                rot, gb = Rot(area(3, 512)), area(nt // 2, 1024)
                W = ffn_weights(A["ffn_gu_2"][l, j // 2], A["ffn_w_down_2"][l, j // 2], parts, 3 if nt == 2 else 2)
                tiles = both[:nt]
                ready = modulated(l, j, tiles, hs, W)
                side = gates(l, j, gb, area(4, 128), nt // 2, 0.5)
                hf = Split(max(parts), nt * 128)
                ffn(hs, ready, W, hf, rot, nt, parts, add_gated(tiles, gb, rot), side)
                leave()

            def fourier(l):
                enter()
                barrier()
                W = Weights([(A["four_w_2"][0, q * 256:(q + 1) * 256, :].rearrange("(c p) n -> p c n", p=P), 2048)
                             for q in range(4)])
                fs = Split(8, 512)
                gb, row, rot = area3(2, 1024), area(1024), Rot(area(2, 512))
                load("four", row[0:1, :], A["four_b_2"])
                d2, Z = area3(2, 512), None
                load("four", d2, A["c_dft2"])
                side = gates(l, 1, gb, area(4, 128), 2, 1.0)
                for s in range(2):
                    enter()
                    d1, hT, Z = area3(2, 512), area(8, 256), area4(2, 4, 512)
                    load(f"dft{s}", d1, A["c_dft1"])
                    sct = st[:, 256:272].rearrange("p (c v) -> p c v", v=2)
                    stt(sct, mods[:, l, 32:40, :], 1.0, bl(ng2[:, l, 1, :], 2), ALU.add, ALU.mult)
                    r = rstd(both[2 * s:2 * s + 2], st[:, 0:2], 2, 1024, 1e-6, Z[:, 0, 0:2, :].rearrange("p a b -> p (a b)"))
                    xs = Z.rearrange("p a b c -> p a (b c)")[:, :, 0:1024]
                    for t in range(2):
                        xd = ts(dv, xs[:, t, :], both[2 * s + t], st[:, t:t + 1], None, ALU.mult, None, r)
                    for c in range(8):
                        b = banks.get()
                        for t in range(2):
                            tk = tr(b.t[:, t * 128:(t + 1) * 128], xs[:, t, c * 128:(c + 1) * 128], xd, b.free,
                                    mark=(t == 1))
                        if c % 2:
                            e = act(hT[:, c, :], b.t[:, 0:256], ACT.Identity, tk, scale=sct[:, c, s:s + 1],
                                    bias=mods[:, l, 24 + c, s:s + 1])
                        else:
                            e = ts(dv, hT[:, c, :], b.t[:, 0:256], sct[:, c, s:s + 1], mods[:, l, 24 + c, s:s + 1],
                                   ALU.mult, ALU.add, tk)
                        b.done(e)
                    hd = [ac.last(), dv.last(), small[f"dft{s}"]]
                    for t in range(2):
                        for g in range(4):
                            b = banks.get()
                            for m in range(2):
                                tk = mm(b.t[:, :], hT[:, 2 * g + m, t * 128:(t + 1) * 128], d1[:, m, :], hd, b.free,
                                        start=m == 0, stop=m == 1, mark=(m == 1))
                            b.done(cp((ac, dv)[g % 2], Z[:, t, g, :], b.t[:, :], tk))
                    zd = [ac.last(), dv.last(), small["four"]]
                    for c in range(8):
                        b = banks.get()
                        i = 0
                        for m in range(2):
                            for h in range(2):
                                o = h * 256 + (c % 2) * 128
                                tk = mm(b.t[:, 0:256], Z[:, m, c // 2, o:o + 128], d2[:, m, h * 256:(h + 1) * 256], zd,
                                        b.free, start=i == 0, stop=i == 3, mark=(i == 3))
                                i += 1
                        o, free, ri = rot.get()
                        e = cp(dv, o[:, 0:256], b.t[:, 0:256], tk, free)
                        b.done(e)
                        next(side, None)
                        fd = fs.put((slice(None), c, slice(s * 256, (s + 1) * 256)), o[:, 0:256], e)
                        rot.put(ri, fd)
                    leave()
                    barrier()
                ob = [[banks.get() for _ in range(2)] for _ in range(4)]
                for q in range(4):
                    wh, wl, rd = W.get(q)
                    wh = wh.rearrange("p (c n) -> p c n", n=1024)
                    wl = wl.rearrange("p (c n) -> p c n", n=1024)
                    order = [(jj, t) for jj in range(2) for t in range(4)] if q < 3 else \
                        [(jj, t) for t in range(4) for jj in range(2)]
                    for jj, t in order:
                        j = 2 * q + jj
                        c = slice(t * 128, (t + 1) * 128)
                        for h in range(2):
                            b = ob[t][h]
                            n_ = slice(h * 512, (h + 1) * 512)
                            tk = mm3(b.t[:, :], fs.h[:, j, c], fs.l[:, j, c], wh[:, jj, n_], wl[:, jj, n_],
                                     rd, fd, b.free, start=j == 0, stop=False, mark=(jj == 1))
                            if j == 7:
                                b.tok = mm(b.t[:, :], onesrow, row[0:1, n_], start=False, mark=True)
                    W.free(q, tk)
                finish = add_gated(both, gb, rot)
                for t in range(4):
                    for h in range(2):
                        b = ob[t][h]
                        b.done(finish(t, h, b.t[:, :], b.tok))
                leave()

            def retention(l):
                enter()
                barrier()
                yT = area(16, 256)
                enter()
                hs = Split(8, 512)
                W = Weights([(A["ret_w_in_2"][i, kh], 2048) for i in range(12) for kh in range(2)], 2, 0)
                ready = modulated(l, 1, both, hs, W)
                barrier()
                cs = area3(2, 256)
                cr = area3(2, 256)
                ex = area3(1, 8)[:, 0, :]
                load("ret", cs, A["c_rope"])
                load("ret", cr, A["c_row"].broadcast_to([P, 512]).rearrange("p (a b) -> p a b", a=2))
                load("ret", ex[:, 0:4], A["c_col"])
                qk = area4(2, 2, 256)
                qr = area4(2, 2, 256)
                t1 = area4(2, 2, 256)
                kc = area3(2, 256)
                kfb = area4(2, 2, 256)
                v = area4(2, 2, 512)
                g = area3(2, 512)
                S = area4(2, 2, 512)
                MD = area3(2, 256)
                qd = t1
                rw = qk[:, 0]
                y = ct.rearrange("p a b -> p (a b)")[:, 0:1024].rearrange("p (a b) -> p a b", b=512)
                rot = Rot(ct.rearrange("p a b -> p (a b)")[:, 1024:2048].rearrange("p (a b) -> p a b", b=512))
                Dc = S.rearrange("p a b c -> p (a b c)").rearrange("p (a b c) -> p a b c", a=4, b=2)
                Pm = kc
                barrier(small["ret"])
                def project(h, kh, bqk):
                    ba, bk = bqk[0:2], bqk[2]
                    i = 6 * h + kh
                    wh, wl, rd = W.get(i)
                    wh = wh.rearrange("p (k n) -> p k n", k=4)
                    wl = wl.rearrange("p (k n) -> p k n", k=4)
                    for a in range(2):
                        for m in range(2):
                            for k in range(4):
                                n0 = a * 256 + m * 128
                                kk_ = 4 * kh + k
                                mm3(ba[a].t[:, m * 256:(m + 1) * 256], wh[:, k, n0:n0 + 128], wl[:, k, n0:n0 + 128],
                                    hs.h[:, kk_, 0:256], hs.l[:, kk_, 0:256], rd, ready[kk_], ba[a].free,
                                    start=(kk_ == 0 and m == 0), stop=kk_ == 7)
                    for t in range(2):
                        for k in range(4):
                            kk_ = 4 * kh + k
                            c = slice(256 + t * 128, 384 + t * 128)
                            tk = mm3(bk.t[:, t * 256:(t + 1) * 256], hs.h[:, kk_, c], hs.l[:, kk_, c],
                                     wh[:, k, 256:512], wl[:, k, 256:512], bk.free,
                                     start=(kk_ == 0 and t == 0), stop=kk_ == 7, mark=(t == 1 and k == 3))
                    W.free(i, tk)
                    return tk

                bqk = [banks.get() for _ in range(3)]
                for kh in range(2):
                    tk = project(0, kh, bqk)
                for h in range(4):
                    barrier(waits=(ac, dv, po))
                    projected = tk
                    load(f"dec{h}", Dc, A["c_ret"])
                    lf, lb = lg[:, h:h + 1], lg[:, 4 + h:5 + h]
                    act(MD, Dc[:, 0], ACT.Exp, small[f"dec{h}"], scale=lf)
                    e0 = act(y[:, :, 0:256], Dc[:, 1], ACT.Exp, scale=lb)
                    dc = st[:, 280:284]
                    act(dc[:, 0:2], ex[:, 0:2], ACT.Exp, scale=lf)
                    e1 = act(dc[:, 2:4], ex[:, 2:4], ACT.Exp, scale=lb)
                    tt(dv, MD, MD, Dc[:, 2], ALU.mult, e0)
                    tt(dv, y[:, :, 0:256], y[:, :, 0:256], Dc[:, 3], ALU.mult)
                    md = tt(dv, MD, MD, y[:, :, 0:256], ALU.add)
                    ba, bk, tk = bqk[0:2], bqk[2], projected
                    for a in range(2):
                        qe = evac(ac, qk[:, a], v256(ba[a]), tk, scale=None if a == 0 else 0.0625)
                        ba[a].done(qe)
                    ke = evac(ac, kc, v256(bk), tk, scale=0.0625)
                    bk.done(ke)
                    for vg in range(2):
                        bb = [banks.get() for _ in range(4 - 2 * vg)]
                        for kh in range(2):
                            i = 6 * h + 2 + 2 * vg + kh
                            wh, wl, rd = W.get(i)
                            wh = wh.rearrange("p (k n) -> p k n", k=4)
                            wl = wl.rearrange("p (k n) -> p k n", k=4)
                            for t, b in enumerate(bb):
                                c = slice(t * 128, (t + 1) * 128)
                                for k in range(4):
                                    kk_ = 4 * kh + k
                                    tk = mm3(b.t[:, :], hs.h[:, kk_, c], hs.l[:, kk_, c], wh[:, k, :], wl[:, k, :],
                                             rd, b.free, start=kk_ == 0, stop=kk_ == 7, mark=(k == 3))
                            W.free(i, tk)
                            if (vg, kh) == (0, 0):
                                for m in range(2):
                                    ts(dv, kfb[:, 0, m, :], kc[:, m, :], dc[:, m:m + 1], None, ALU.mult, None, ke, e1)
                                    kd = ts(dv, kfb[:, 1, m, :], kc[:, m, :], dc[:, 2 + m:3 + m], None, ALU.mult, None)
                                c2, s2 = bc(cs[:, 0, :], 2), bc(cs[:, 1, :], 2)
                                tt(dv, qr[:, :, 0, :], qk[:, :, 0, :], c2, ALU.mult, qe)
                                tt(dv, t1[:, :, 0, :], qk[:, :, 1, :], s2, ALU.mult)
                                tt(dv, qr[:, :, 0, :], qr[:, :, 0, :], t1[:, :, 0, :], ALU.subtract)
                                tt(dv, qr[:, :, 1, :], qk[:, :, 1, :], c2, ALU.mult)
                                tt(dv, t1[:, :, 0, :], qk[:, :, 0, :], s2, ALU.mult)
                                rp = tt(dv, qr[:, :, 1, :], qr[:, :, 1, :], t1[:, :, 0, :], ALU.add)
                            if (vg, kh) == (0, 1):
                                act(rw[:, 0, :], cr[:, 0, :], ACT.Exp, rp, scale=lf)
                                rx = act(rw[:, 1, :], cr[:, 1, :], ACT.Exp, scale=lb)
                                for d in range(2):
                                    qx = tt(dv, qd[:, d], qr[:, 0], bc(rw[:, d, :], 2), ALU.mult, rx)
                        for t, b in enumerate(bb):
                            if vg == 0:
                                ve = cp(ac, v[:, t // 2, t % 2, :], b.t[:, :], tk)
                                b.done(ve)
                            else:
                                ge = act(g[:, t, :], b.t[:, :], ACT.Silu, tk)
                                b.done(ge)
                    for d in range(2):
                        for m in range(2):
                            b = banks.get()
                            for t in range(2):
                                tk = mm(b.t[:, :], kfb[:, d, t, m * 128:(m + 1) * 128], v[:, 1, t, :], kd, ve, b.free,
                                        start=t == 0, stop=t == 1, mark=(t == 1))
                            se = cp(ac, S[:, d, m, :], b.t[:, :], tk, md)
                            b.done(se)
                    b = banks.get()
                    for tj in range(2):
                        for m in range(2):
                            tk = mm(b.t[:, tj * 256:(tj + 1) * 256], qr[:, 1, m, tj * 128:(tj + 1) * 128], qr[:, 0, m, :],
                                    qx, b.free, start=m == 0, stop=m == 1, mark=(m == 1 and tj == 1))
                    pm = tt(dv, Pm, v256(b), MD, ALU.mult, tk)
                    b.done(pm)
                    for t in range(2):
                        s = slice(t * 128, (t + 1) * 128)
                        b = banks.get()
                        for d in range(2):
                            for m in range(2):
                                mm(b.t[:, :], qd[:, d, m, s], S[:, d, m, :], se, b.free, start=(d == 0 and m == 0),
                                   stop=False)
                        for tj in range(2):
                            tk = mm(b.t[:, :], Pm[:, tj, s], v[:, 0, tj, :], pm, start=False, stop=tj == 1,
                                    mark=(tj == 1))
                        b.done(cp(dv, y[:, t, :], b.t[:, :], tk))
                    out_done = tk
                    if h < 3:
                        bqk = [banks.get() for _ in range(3)]
                        tk = project(h + 1, 0, bqk)
                    mu, va = st[:, 284:286], st[:, 286:288]
                    red(mu, y, ALU.add)
                    ts(dv, mu, mu, 1.0 / 512, None, ALU.mult, None)
                    for t in range(2):
                        e = ts(dv, y[:, t, :], y[:, t, :], mu[:, t:t + 1], None, ALU.subtract, None)
                    r = rstd([y[:, 0, :], y[:, 1, :]], va, 2, 512, 1e-6, S[:, 0, 0, :], e, out_done)
                    for t in range(2):
                        e = stt(y[:, t, :], y[:, t, :], va[:, t:t + 1], g[:, t, :], ALU.mult, ALU.mult, r, ge)
                    if h < 3:
                        tk = project(h + 1, 1, bqk)
                    following = tk
                    for q in range(2):
                        b = banks.get()
                        for m in range(2):
                            for t in range(2):
                                c = 2 * q + m
                                tk = tr(b.t[:, (2 * m + t) * 128:(2 * m + t + 1) * 128], y[:, t, c * 128:(c + 1) * 128],
                                        e, b.free, mark=(m == 1 and t == 1))
                        yd = cp(ac, yT[:, 4 * h + 2 * q:4 * h + 2 * q + 2, :], v256(b), tk)
                        b.done(yd)
                    tk = following
                leave()
                enter()
                barrier()
                gb, rot = area(1, 1024), Rot(area(2, 512))
                W = Weights([(A["ret_w_out_2"][0, q * 256:(q + 1) * 256, :].rearrange("(c p) n -> p c n", p=P), 2048)
                             for q in range(8)])
                ys = Split(16, 256)
                side = gates(l, 1, gb, area(4, 128), 1, 1.0)
                yd = [ys.put((slice(None), slice(4 * q, 4 * q + 4), slice(None)), yT[:, 4 * q:4 * q + 4, :])
                      for q in range(4)]
                project_out(W, ys, yd, add_gated(xa, gb, rot), side)
                leave()
                leave()

            e = act(lg, lg, ACT.Abs)
            ts(dv, lg, lg, -1.0, None, ALU.mult, None, e)
            half_ffn(0, 0, 4, [11, 11])
            fourier(0)
            half_ffn(0, 2, 4, [11, 11])
            half_ffn(1, 0, 4, [11, 11])
            retention(1)
            half_ffn(1, 2, 2, [22])
            leave()
            enter()
            barrier()
            fg, junk = area(1024), area(1024)
            load("fg", fg, A["final_g_2"].unsqueeze(0).broadcast_to([P, 1024]))
            r = rstd(xa, st[:, 0:2], 2, 1024, 1e-6, junk)
            for t in range(2):
                e = stt(xa[t], xa[t], st[:, t:t + 1], fg, ALU.mult, ALU.mult, r, small["fg"])
            sp.wait(e)
            sp.items.append((lambda e: e.dma_start(out.rearrange("o (t p) d -> p (o t) d", p=P), xt[:, :, :]), s_out))
            sp.items.append((s_out, 16))
            leave()

        s_out = sem("s_out")
        FILL = 0
        for l in range(2):
            ffn1(l, 1)
            mixers(l)
            if l == 1:
                between = context()
            ffn1(l, 2)
        second(*between)

        block = ctx.enter_context(nc.Block())

        @block.sync
        def _(eng):
            sp.emit(eng)

        @block.tensor
        def _(eng):
            pe.emit(eng)

        @block.scalar
        def _(eng):
            ac.emit(eng)

        @block.vector
        def _(eng):
            dv.emit(eng)

        @block.gpsimd
        def _(eng):
            po.emit(eng)


def constants():
    f = np.float32
    i = np.arange(128)
    a, b = np.meshgrid(i, i, indexing="ij")
    ch = a // 64 == b // 64

    def level(n):
        h = n // 2
        return ((a // n == b // n) & (a % n < h) & (b % n >= h)).astype(f)

    m = dict(ident=np.eye(128), tri=a <= b, ones=np.ones((128, 128)), negT=np.where(a <= b, 0, -1e30),
             neg=np.where(b <= a, 0, -1e30), bones=ch, l2=level(2).T, l2t=level(2), l4=level(4), l8=level(8),
             l16=level(16), l32=level(32), l64=level(64), i2=np.hstack([np.eye(128)[:, :64] + np.eye(128)[:, 64:]] * 2))
    c = {"c_msk": np.stack([np.asarray(m[n], f) for n in MASKS], 1)}
    strict, incl = (ch & (a < b)).astype(f), (ch & (a <= b)).astype(f)
    c["c_mask4"] = np.stack([strict, incl, strict, incl], 1)
    c["c_scan"] = np.broadcast_to((np.arange(256) % 64 != 0).astype(f), (128, 256)).copy()
    n = np.arange(256)
    ang = 2 * np.pi * ((n[:, None] * n[None, :]) % 256) / 256
    C, S = np.cos(ang), np.sin(ang)
    d1 = np.concatenate([C, S], 1).astype(f)
    d2 = (np.concatenate([C, -S], 1) / 256).astype(f)
    c["c_dft1"] = d1.reshape(2, 128, 512).transpose(1, 0, 2).copy()
    c["c_dft2"] = d2.reshape(2, 128, 512).transpose(1, 0, 2).copy()
    inv = (f(10000.0) ** (-np.arange(64, dtype=f) / f(64))).astype(f)
    row, colm = (n // 64).astype(f), (n % 64).astype(f)
    g = np.concatenate([row[:, None] * inv, colm[:, None] * inv], 1).astype(f)
    c["c_rope"] = np.stack([np.cos(g).T, np.sin(g).T], 1).astype(f)
    j = np.arange(256)
    dif = (j[None, :] - j[:, None])
    t = np.stack([np.maximum(dif, 0), np.maximum(-dif, 0), dif >= 0, dif <= 0]).astype(f)
    c["c_ret"] = t.reshape(4, 2, 128, 256).transpose(2, 0, 1, 3).copy()
    c["c_row"] = np.concatenate([j + 1, 256 - j]).astype(f)[None, :]
    p = np.arange(128)
    c["c_col"] = np.stack([255 - p, 127 - p, p, p + 128], 1).astype(f)
    return c


def layout(x):
    col = lambda a: np.ascontiguousarray(a).reshape(-1, 128).T
    d = {}

    def tiles(w, n):
        m = w.shape[1] // n
        return np.ascontiguousarray(w.reshape(8, 128, m, n).transpose(2, 1, 0, 3)).reshape(m, 128, 8 * n)

    def gate_up(g, u):
        w = np.stack([g.reshape(8, 128, 22, 128), u.reshape(8, 128, 22, 128)])
        return np.ascontiguousarray(w.transpose(3, 2, 1, 0, 4)).reshape(22, 128, 2048)

    def halves(w):
        m = w.shape[1] // 512
        return np.ascontiguousarray(w.reshape(2, 4, 128, m, 512).transpose(3, 0, 2, 1, 4)).reshape(m, 2, 128, 2048)

    for k in (1, 2):
        w = x[f"ffn{k}_w_gate_up"]
        d[f"ffn{k}_w_gate_up"] = np.stack([gate_up(w[l][:, :2816], w[l][:, 2816:]) for l in range(2)])
        d[f"ffn{k}_w_down"] = x[f"ffn{k}_w_down"]
    g, u = x["ffn_w_gate_2"], x["ffn_w_up_2"]
    d["ffn_gu_2"] = np.stack([np.stack([gate_up(g[l, j], u[l, j]) for j in range(2)]) for l in range(2)])
    d["ffn_w_down_2"] = x["ffn_w_down_2"]
    w = x["w_in"]
    t_cols = np.r_[3352:5144, 1024:2304, 2320:2832]
    n_cols = np.r_[0:1024, 2832:3344]
    s_cols = np.r_[2304:2320, 3344:3352]
    d["w_in_t"] = np.stack([tiles(w[l][:, t_cols], 256) for l in range(2)])
    d["w_in_n"] = np.stack([halves(w[l][:, n_cols]) for l in range(2)])
    d["w_in_s"] = np.stack([tiles(w[l][:, s_cols], 24)[0] for l in range(2)])
    d["ada_w_2"] = np.stack([halves(x["ada_w_2"][l]) for l in range(2)])
    w = x["ret_w_in_2"][0]
    q, k, v, gg = w[:, :1024], w[:, 1024:2048], w[:, 2048:4096], w[:, 4096:]
    cat = [a for h in range(4) for a in (q[:, h * 256:(h + 1) * 256], k[:, h * 256:(h + 1) * 256],
                                         v[:, h * 512:(h + 1) * 512], gg[:, h * 512:(h + 1) * 512])]
    d["ret_w_in_2"] = halves(np.concatenate(cat, 1))
    for n in ("x", "mlstm_wq", "mlstm_wk", "mlstm_wv", "rwkv_w_up", "rwkv_a_up", "rwkv_g_up", "w_out", "ctx_2",
              "final_norm", "final_g_2", "four_w_2", "four_b_2", "ret_w_out_2"):
        d[n] = x[n]
    cc = []
    for l in range(2):
        cw = np.concatenate([x["ssd_conv_w"][l], x["mlstm_conv_w"][l]], 1)
        cw = cw.reshape(4, 14, 128).transpose(2, 1, 0).reshape(128, 56)
        cb = np.concatenate([x["ssd_conv_b"][l], x["mlstm_conv_b"][l]])
        one = {"n1": x["ffn1_norm"][l], "nm": x["mix_norm"][l], "n2": x["ffn2_norm"][l], "cb": cb,
               "sn": x["ssd_norm"][l], "mn": x["mlstm_norm"][l], "mu": x["rwkv_shift_mu"][l], "w0": x["rwkv_w0"][l],
               "a0": x["rwkv_a0"][l], "kk": x["rwkv_k_k"][l], "ka": x["rwkv_k_a"][l],
               "rk": x["rwkv_r_k"][l], "lw": x["rwkv_ln_w"][l], "lb": x["rwkv_ln_b"][l]}
        cc += [cw if n == "cw" else col(one[n]) for n, _ in COLS1]
    cc += [col(x["norm_g_2"]), col(x["ada_b_2"])]
    two = np.stack([col(x["c_2"][0]), col(x["c_ctx_2"])], 2).reshape(128, 16)
    d["c_cols"] = np.ascontiguousarray(np.concatenate(cc + [two], 1))
    r = [x[n][l] for l in range(2) for n in ("ssd_dt_bias", "ssd_a_log", "ssd_d", "mlstm_gate_bias")]
    d["c_rows"] = np.concatenate(r + [x["ret_decay_2"].reshape(-1)])[None, :]
    d.update(constants())
    return d


def kernel(**inputs):
    import concourse.bacc as _bacc
    from concourse.bass_utils import run_bass_kernel_spmd as _run

    nc = _bacc.Bacc("TRN2", target_bir_lowering=False, num_devices=1)
    arrays, A = {}, {}
    for name, a in layout({k: np.asarray(v) for k, v in inputs.items()}).items():
        a = np.ascontiguousarray(a)
        arrays["in_" + name] = a
        A[name] = nc.dram_tensor("in_" + name, a.shape, mybir.dt.from_np(a.dtype), kind="ExternalInput").ap()
    out = nc.dram_tensor("out_0", (1, 256, 1024), F32, kind="ExternalOutput").ap()
    build(nc, A, out)
    r = _run(nc, [arrays], core_ids=[0])
    return r.results[0]["out_0"]
```
